# Optimizing a Trainium2 kernel written in Bass

```python
import math
import jax
import jax.numpy as jnp
from jax import lax
import numpy as np

D_MODEL = 1024
BATCH = 1
SEQ = 512
DEPTH = 2

CHUNK = 64
EPS = 1e-6

RWKV_HEAD_DIM = 64
RWKV_HEADS = D_MODEL // 128
RWKV_WIDTH = RWKV_HEADS * RWKV_HEAD_DIM
DECAY_LORA = 64
ICLR_LORA = 64
GATE_LORA = 128
RWKV_GN_EPS = 64e-5
RWKV_SPLITS = (RWKV_WIDTH, RWKV_WIDTH, RWKV_WIDTH, DECAY_LORA, ICLR_LORA, GATE_LORA)
RWKV_PROJ = 3 * RWKV_WIDTH + DECAY_LORA + ICLR_LORA + GATE_LORA

SSD_HEAD_DIM = 64
SSD_WIDTH = D_MODEL
SSD_HEADS = SSD_WIDTH // SSD_HEAD_DIM
SSD_GROUPS = 2
SSD_HEADS_PER_GROUP = SSD_HEADS // SSD_GROUPS
SSD_STATE = 128
SSD_CONV = 4
SSD_CONV_DIM = SSD_WIDTH + 2 * SSD_GROUPS * SSD_STATE

S5_GROUP_CH = 16
S5_WIDTH = D_MODEL // 2
S5_GROUPS = S5_WIDTH // S5_GROUP_CH
S5_STATE = 64

RET_HEADS = 4
RET_QK_DIM = 128
RET_V_DIM = 256
RET_QK_WIDTH = RET_HEADS * RET_QK_DIM
RET_V_WIDTH = RET_HEADS * RET_V_DIM

EVEN_SPLITS = (RWKV_PROJ, SSD_WIDTH, SSD_CONV_DIM, SSD_HEADS)
EVEN_PROJ = RWKV_PROJ + SSD_WIDTH + SSD_CONV_DIM + SSD_HEADS
EVEN_OUT = RWKV_WIDTH + SSD_WIDTH
ODD_SPLITS = (S5_WIDTH, RET_QK_WIDTH, RET_QK_WIDTH, RET_V_WIDTH, RET_V_WIDTH)
ODD_PROJ = S5_WIDTH + 2 * RET_QK_WIDTH + 2 * RET_V_WIDTH
ODD_OUT = S5_WIDTH + RET_V_WIDTH

FFN_HIDDEN = ((8 * D_MODEL // 3 + 127) // 128) * 128
FFN_CONV = 3

kernel_name = "chunk_causal_hybrid_rwkv7_ssd_s5_retnet"

def split_cols(h, sizes):
    idx = np.cumsum(sizes)[:-1].tolist()
    return jnp.split(h, idx, axis=-1)

def rms_norm(x, g):
    xf = x.astype(jnp.float32)
    y = xf * lax.rsqrt(jnp.mean(xf * xf, axis=-1, keepdims=True) + EPS)
    return (y * g.astype(jnp.float32)).astype(x.dtype)

def causal_dwconv(x, w, b):
    K, C = w.shape
    y = lax.conv_general_dilated(
        x, w[:, None, :].astype(x.dtype), window_strides=(1,), padding=[(K - 1, 0)],
        dimension_numbers=("NWC", "WIO", "NWC"), feature_group_count=C)
    return y + b.astype(x.dtype)

def token_shift(x):
    return jnp.pad(x, ((0, 0), (1, 0), (0, 0)))[:, :-1]

def exclusive_chunk_scan(states, decay):
    def step(h, inp):
        s, d = inp
        return h * d + s, h
    h0 = jnp.zeros_like(states[:, 0])
    _, prev = lax.scan(step, h0, (jnp.moveaxis(states, 1, 0), jnp.moveaxis(decay, 1, 0)))
    return jnp.moveaxis(prev, 0, 1)

def rwkv7_recurrence(r, decay, k, v, kk, a):
    Bsz, L, H, N = r.shape

    def step(S, inp):
        r_t, w_t, k_t, v_t, kk_t, a_t = inp
        sa = jnp.einsum("bhij,bhj->bhi", S, -kk_t)
        S = (S * w_t[:, :, None, :] + sa[..., None] * (kk_t * a_t)[:, :, None, :]
             + v_t[..., None] * k_t[:, :, None, :])
        return S, jnp.einsum("bhij,bhj->bhi", S, r_t)

    S0 = jnp.zeros((Bsz, H, N, N), jnp.float32)
    xs = tuple(jnp.moveaxis(t, 1, 0) for t in (r, decay, k, v, kk, a))
    _, y = lax.scan(step, S0, xs)
    return jnp.moveaxis(y, 0, 1)

def rwkv7_group(p, mu, w0, w2, a0, a2, g2, k_k, k_a, r_k, ln_g, ln_b):
    mu, w0, w2, a0, a2, g2, k_k, k_a, r_k, ln_g, ln_b = (
        t.astype(jnp.float32) for t in (mu, w0, w2, a0, a2, g2, k_k, k_a, r_k, ln_g, ln_b))
    Bsz, L, _ = p.shape
    H, N = RWKV_HEADS, RWKV_HEAD_DIM
    p = p + (token_shift(p) - p) * mu
    r, k, v, z_w, z_a, z_g = split_cols(p, RWKV_SPLITS)
    w_log = -jax.nn.softplus(-(w0 + jnp.tanh(z_w) @ w2)) - 0.5
    decay = jnp.exp(-jnp.exp(w_log))
    a = jax.nn.sigmoid(a0 + z_a @ a2)
    g = jax.nn.sigmoid(z_g) @ g2
    kk = (k * k_k).reshape(Bsz, L, H, N)
    kk = kk * lax.rsqrt(jnp.maximum(jnp.sum(kk * kk, axis=-1, keepdims=True), 1e-24))
    k = k * (1.0 + (a - 1.0) * k_a)
    heads = lambda t: t.reshape(Bsz, L, H, N)
    rh, kh, vh, ah, dh = heads(r), heads(k), heads(v), heads(a), heads(decay)
    y = rwkv7_recurrence(rh, dh, kh, vh, kk, ah)
    mean = jnp.mean(y, axis=-1, keepdims=True)
    var = jnp.mean(jnp.square(y - mean), axis=-1, keepdims=True)
    y = ((y - mean) * lax.rsqrt(var + RWKV_GN_EPS)).reshape(Bsz, L, RWKV_WIDTH) * ln_g + ln_b
    y = y + (jnp.sum(rh * kh * r_k, axis=-1, keepdims=True) * vh).reshape(Bsz, L, RWKV_WIDTH)
    return y * g

def ssd_chunked(x, a, bm, cm):
    Bsz, L, G, J, P = x.shape
    N = bm.shape[-1]
    nc = L // CHUNK
    x = x.reshape(Bsz, nc, CHUNK, G, J, P)
    a = a.reshape(Bsz, nc, CHUNK, G, J)
    bm = bm.reshape(Bsz, nc, CHUNK, G, N)
    cm = cm.reshape(Bsz, nc, CHUNK, G, N)
    a_cum = jnp.cumsum(a, axis=2)
    causal = jnp.tril(jnp.ones((CHUNK, CHUNK), dtype=bool))[:, :, None, None]
    seg = a_cum[:, :, :, None] - a_cum[:, :, None, :]
    intra = jnp.exp(jnp.where(causal, seg, -jnp.inf))
    cb = jnp.einsum("bclgn,bcsgn->bclsg", cm, bm)
    y_diag = jnp.einsum("bclsg,bclsgj,bcsgjp->bclgjp", cb, intra, x)
    decay_to_end = jnp.exp(a_cum[:, :, -1:] - a_cum)
    states = jnp.einsum("bclgn,bclgj,bclgjp->bcgjpn", bm, decay_to_end, x)
    chunk_decay = jnp.exp(a_cum[:, :, -1])[..., None, None]
    prev = exclusive_chunk_scan(states, chunk_decay)
    y_off = jnp.einsum("bclgn,bcgjpn,bclgj->bclgjp", cm, prev, jnp.exp(a_cum))
    return (y_diag + y_off).reshape(Bsz, L, G, J, P)

def ssd_group(z, xbc, dt_raw, conv_w, conv_b, dt_bias, a_log, d_skip, norm_g):
    conv_w, conv_b, dt_bias, a_log, d_skip, norm_g = (
        t.astype(jnp.float32) for t in (conv_w, conv_b, dt_bias, a_log, d_skip, norm_g))
    Bsz, L, _ = z.shape
    G, J, P, N = SSD_GROUPS, SSD_HEADS_PER_GROUP, SSD_HEAD_DIM, SSD_STATE
    xbc = jax.nn.silu(causal_dwconv(xbc, conv_w, conv_b))
    xs, bm, cm = split_cols(xbc, (SSD_WIDTH, G * N, G * N))
    xs = xs.reshape(Bsz, L, G, J, P)
    bm = bm.reshape(Bsz, L, G, N)
    cm = cm.reshape(Bsz, L, G, N)
    dt = jax.nn.softplus(dt_raw + dt_bias).reshape(Bsz, L, G, J)
    A = -jnp.exp(a_log).reshape(G, J)
    y = ssd_chunked(xs * dt[..., None], dt * A, bm, cm) + d_skip.reshape(G, J)[..., None] * xs
    y = y.reshape(Bsz, L, G, J * P) * jax.nn.silu(z.reshape(Bsz, L, G, J * P))
    y = y * lax.rsqrt(jnp.mean(y * y, axis=-1, keepdims=True) + EPS)
    return y.reshape(Bsz, L, SSD_WIDTH) * norm_g

def rwkv_ssd_mixer(h, w_in, rwkv_mu, rwkv_w0, rwkv_w2, rwkv_a0, rwkv_a2, rwkv_g2, rwkv_k_k,
                   rwkv_k_a, rwkv_r_k, rwkv_ln_g, rwkv_ln_b, ssd_conv_w, ssd_conv_b,
                   ssd_dt_bias, ssd_a_log, ssd_d, ssd_norm_g, w_out):
    proj = (h @ w_in).astype(jnp.float32)
    p_rwkv, p_z, p_xbc, p_dt = split_cols(proj, EVEN_SPLITS)
    y_a = rwkv7_group(p_rwkv, rwkv_mu, rwkv_w0, rwkv_w2, rwkv_a0, rwkv_a2, rwkv_g2,
                      rwkv_k_k, rwkv_k_a, rwkv_r_k, rwkv_ln_g, rwkv_ln_b)
    y_b = ssd_group(p_z, p_xbc, p_dt, ssd_conv_w, ssd_conv_b, ssd_dt_bias, ssd_a_log,
                    ssd_d, ssd_norm_g)
    y = jnp.concatenate([y_a, y_b], axis=-1).astype(h.dtype)
    return y @ w_out

def s5_group(u, lam_re, lam_im, log_dt, b_re, b_im, c_re, c_im, d_skip, w_glu, b_glu):
    lam_re, lam_im, log_dt, b_re, b_im, c_re, c_im, d_skip, w_glu, b_glu = (
        t.astype(jnp.float32) for t in
        (lam_re, lam_im, log_dt, b_re, b_im, c_re, c_im, d_skip, w_glu, b_glu))
    Bsz, L, _ = u.shape
    G, H = S5_GROUPS, S5_GROUP_CH
    uf = u.reshape(Bsz, L, G, H)
    lam = lax.complex(lam_re, lam_im)
    lam_bar = jnp.exp(lam * jnp.exp(log_dt)[:, None])
    b_bar = ((lam_bar - 1.0) / lam)[..., None] * lax.complex(b_re, b_im)
    bu = jnp.einsum("gph,blgh->blgp", b_bar, uf)
    a_el = jnp.broadcast_to(lam_bar, bu.shape)

    def combine(e1, e2):
        a1, b1 = e1
        a2, b2 = e2
        return a2 * a1, a2 * b1 + b2

    _, states = lax.associative_scan(combine, (a_el, bu), axis=1)
    c = lax.complex(c_re, c_im)
    y = jnp.einsum("ghp,blgp->blgh", c, states).real + d_skip.reshape(G, H) * uf
    y = jax.nn.gelu(y.reshape(Bsz, L, S5_WIDTH))
    return y * jax.nn.sigmoid(y @ w_glu + b_glu)

def rotary(x, pos):
    half = x.shape[-1] // 2
    theta = 1.0 / (10000.0 ** jnp.linspace(0.0, 1.0, half, dtype=jnp.float32))
    ang = pos.astype(jnp.float32)[:, None] * theta[None, :]
    cos = jnp.cos(ang)[None, :, None, :]
    sin = jnp.sin(ang)[None, :, None, :]
    x1, x2 = x[..., :half], x[..., half:]
    return jnp.concatenate([x1 * cos - x2 * sin, x1 * sin + x2 * cos], axis=-1)

def retention_group(q, k, v, g):
    Bsz, L, _ = q.shape
    H, DK, DV = RET_HEADS, RET_QK_DIM, RET_V_DIM
    nc = L // CHUNK
    pos = jnp.arange(L)
    q = rotary(q.reshape(Bsz, L, H, DK), pos)
    k = rotary(k.reshape(Bsz, L, H, DK), pos) * (DK ** -0.5)
    log_gamma = jnp.log(1.0 - 2.0 ** (-5.0 - jnp.arange(H, dtype=jnp.float32)))
    qc = q.reshape(Bsz, nc, CHUNK, H, DK)
    kc = k.reshape(Bsz, nc, CHUNK, H, DK)
    vc = v.reshape(Bsz, nc, CHUNK, H, DV)
    t = jnp.arange(CHUNK, dtype=jnp.float32)
    diff = t[:, None] - t[None, :]
    intra = jnp.where((diff >= 0)[..., None],
                      jnp.exp(jnp.maximum(diff, 0.0)[..., None] * log_gamma), 0.0)
    scores = jnp.einsum("bclhd,bcshd->bclsh", qc, kc) * intra
    y = jnp.einsum("bclsh,bcshe->bclhe", scores, vc)
    k_dec = jnp.exp((CHUNK - 1.0 - t)[:, None] * log_gamma)
    states = jnp.einsum("bcshd,sh,bcshe->bchde", kc, k_dec, vc)
    chunk_decay = jnp.broadcast_to(jnp.exp(CHUNK * log_gamma)[:, None, None], (Bsz, nc, H, 1, 1))
    prev = exclusive_chunk_scan(states, chunk_decay)
    q_dec = jnp.exp((t + 1.0)[:, None] * log_gamma)
    y = y + jnp.einsum("bclhd,lh,bchde->bclhe", qc, q_dec, prev)
    y = y.reshape(Bsz, L, H, DV)
    y = y * lax.rsqrt(jnp.mean(y * y, axis=-1, keepdims=True) + EPS)
    return jax.nn.silu(g) * y.reshape(Bsz, L, RET_V_WIDTH)

def s5_retention_mixer(h, w_in, lam_re, lam_im, log_dt, b_re, b_im, c_re, c_im, d_skip,
                       w_glu, b_glu, w_out):
    proj = (h @ w_in).astype(jnp.float32)
    u, q, k, v, g = split_cols(proj, ODD_SPLITS)
    y_c = s5_group(u, lam_re, lam_im, log_dt, b_re, b_im, c_re, c_im, d_skip, w_glu, b_glu)
    y_d = retention_group(q, k, v, g)
    y = jnp.concatenate([y_c, y_d], axis=-1).astype(h.dtype)
    return y @ w_out

def conv_ffn(h, w_up, conv_w, conv_b, w_down):
    u = causal_dwconv(h @ w_up, conv_w, conv_b)
    gate, val = jnp.split(u, 2, axis=-1)
    return (jax.nn.silu(gate) * val) @ w_down

def setup_inputs(seed: int = 0) -> dict:
    key = jax.random.key(seed)
    ks = iter(jax.random.split(key, 96))
    f32 = jnp.float32

    def nrm(shape, scale):
        return scale * jax.random.normal(next(ks), shape, f32)

    def gain(n):
        return 1.0 + nrm((n,), 0.02)

    def unif(shape, lo, hi):
        return jax.random.uniform(next(ks), shape, f32, lo, hi)

    D = D_MODEL
    F2 = 2 * FFN_HIDDEN
    inp = {}
    inp["x"] = nrm((BATCH, SEQ, D), 1.0)
    inp["l0_norm_mix"] = gain(D)
    inp["l0_w_in"] = nrm((D, EVEN_PROJ), D ** -0.5)
    inp["l0_rwkv_mu"] = unif((RWKV_PROJ,), 0.0, 1.0)
    ramp = jnp.arange(RWKV_WIDTH, dtype=f32) / (RWKV_WIDTH - 1)
    inp["l0_rwkv_w0"] = -6.0 + 5.0 * ramp ** 0.85 + 0.5 + nrm((RWKV_WIDTH,), 0.01)
    inp["l0_rwkv_w2"] = nrm((DECAY_LORA, RWKV_WIDTH), 0.1 * DECAY_LORA ** -0.5)
    inp["l0_rwkv_a0"] = nrm((RWKV_WIDTH,), 0.1)
    inp["l0_rwkv_a2"] = nrm((ICLR_LORA, RWKV_WIDTH), 0.1 * ICLR_LORA ** -0.5)
    inp["l0_rwkv_g2"] = nrm((GATE_LORA, RWKV_WIDTH), GATE_LORA ** -0.5)
    inp["l0_rwkv_k_k"] = 0.85 + nrm((RWKV_WIDTH,), 0.02)
    inp["l0_rwkv_k_a"] = 1.0 + nrm((RWKV_WIDTH,), 0.02)
    inp["l0_rwkv_r_k"] = nrm((RWKV_HEADS, RWKV_HEAD_DIM), 0.1)
    inp["l0_rwkv_ln_g"] = gain(RWKV_WIDTH)
    inp["l0_rwkv_ln_b"] = nrm((RWKV_WIDTH,), 0.02)
    inp["l0_ssd_conv_w"] = nrm((SSD_CONV, SSD_CONV_DIM), SSD_CONV ** -0.5)
    inp["l0_ssd_conv_b"] = nrm((SSD_CONV_DIM,), 0.02)
    dt0 = jnp.exp(unif((SSD_HEADS,), math.log(1e-3), math.log(1e-1)))
    inp["l0_ssd_dt_bias"] = dt0 + jnp.log(-jnp.expm1(-dt0))
    inp["l0_ssd_a_log"] = jnp.log(unif((SSD_HEADS,), 1.0, 16.0))
    inp["l0_ssd_d"] = gain(SSD_HEADS)
    inp["l0_ssd_norm_g"] = gain(SSD_WIDTH)
    inp["l0_w_out"] = nrm((EVEN_OUT, D), EVEN_OUT ** -0.5)
    inp["l0_norm_ffn"] = gain(D)
    inp["l0_ffn_up"] = nrm((D, F2), D ** -0.5)
    inp["l0_ffn_conv_w"] = nrm((FFN_CONV, F2), FFN_CONV ** -0.5)
    inp["l0_ffn_conv_b"] = nrm((F2,), 0.02)
    inp["l0_ffn_down"] = nrm((FFN_HIDDEN, D), FFN_HIDDEN ** -0.5)
    inp["l1_norm_mix"] = gain(D)
    inp["l1_w_in"] = nrm((D, ODD_PROJ), D ** -0.5)
    inp["l1_s5_lam_re"] = -0.5 + nrm((S5_GROUPS, S5_STATE), 0.01)
    inp["l1_s5_lam_im"] = (math.pi * jnp.arange(S5_STATE, dtype=f32))[None, :] + nrm((S5_GROUPS, S5_STATE), 0.01)
    inp["l1_s5_log_dt"] = unif((S5_GROUPS,), math.log(1e-3), math.log(1e-1))
    inp["l1_s5_b_re"] = nrm((S5_GROUPS, S5_STATE, S5_GROUP_CH), (2 * S5_GROUP_CH) ** -0.5)
    inp["l1_s5_b_im"] = nrm((S5_GROUPS, S5_STATE, S5_GROUP_CH), (2 * S5_GROUP_CH) ** -0.5)
    inp["l1_s5_c_re"] = nrm((S5_GROUPS, S5_GROUP_CH, S5_STATE), S5_STATE ** -0.5)
    inp["l1_s5_c_im"] = nrm((S5_GROUPS, S5_GROUP_CH, S5_STATE), S5_STATE ** -0.5)
    inp["l1_s5_d"] = nrm((S5_WIDTH,), 1.0)
    inp["l1_s5_w_glu"] = nrm((S5_WIDTH, S5_WIDTH), S5_WIDTH ** -0.5)
    inp["l1_s5_b_glu"] = nrm((S5_WIDTH,), 0.02)
    inp["l1_w_out"] = nrm((ODD_OUT, D), ODD_OUT ** -0.5)
    inp["l1_norm_ffn"] = gain(D)
    inp["l1_ffn_up"] = nrm((D, F2), D ** -0.5)
    inp["l1_ffn_conv_w"] = nrm((FFN_CONV, F2), FFN_CONV ** -0.5)
    inp["l1_ffn_conv_b"] = nrm((F2,), 0.02)
    inp["l1_ffn_down"] = nrm((FFN_HIDDEN, D), FFN_HIDDEN ** -0.5)
    inp["final_norm"] = gain(D)
    return inp

def reference(x,
              l0_norm_mix, l0_w_in, l0_rwkv_mu, l0_rwkv_w0, l0_rwkv_w2, l0_rwkv_a0, l0_rwkv_a2,
              l0_rwkv_g2, l0_rwkv_k_k, l0_rwkv_k_a, l0_rwkv_r_k, l0_rwkv_ln_g, l0_rwkv_ln_b,
              l0_ssd_conv_w, l0_ssd_conv_b, l0_ssd_dt_bias, l0_ssd_a_log, l0_ssd_d, l0_ssd_norm_g,
              l0_w_out, l0_norm_ffn, l0_ffn_up, l0_ffn_conv_w, l0_ffn_conv_b, l0_ffn_down,
              l1_norm_mix, l1_w_in, l1_s5_lam_re, l1_s5_lam_im, l1_s5_log_dt, l1_s5_b_re,
              l1_s5_b_im, l1_s5_c_re, l1_s5_c_im, l1_s5_d, l1_s5_w_glu, l1_s5_b_glu, l1_w_out,
              l1_norm_ffn, l1_ffn_up, l1_ffn_conv_w, l1_ffn_conv_b, l1_ffn_down,
              final_norm):
    mixers = (
        (rwkv_ssd_mixer, (l0_w_in, l0_rwkv_mu, l0_rwkv_w0, l0_rwkv_w2, l0_rwkv_a0, l0_rwkv_a2,
                          l0_rwkv_g2, l0_rwkv_k_k, l0_rwkv_k_a, l0_rwkv_r_k, l0_rwkv_ln_g,
                          l0_rwkv_ln_b, l0_ssd_conv_w, l0_ssd_conv_b, l0_ssd_dt_bias,
                          l0_ssd_a_log, l0_ssd_d, l0_ssd_norm_g, l0_w_out)),
        (s5_retention_mixer, (l1_w_in, l1_s5_lam_re, l1_s5_lam_im, l1_s5_log_dt, l1_s5_b_re,
                              l1_s5_b_im, l1_s5_c_re, l1_s5_c_im, l1_s5_d, l1_s5_w_glu,
                              l1_s5_b_glu, l1_w_out)),
    )
    mix_norms = (l0_norm_mix, l1_norm_mix)
    ffn_norms = (l0_norm_ffn, l1_norm_ffn)
    ffns = ((l0_ffn_up, l0_ffn_conv_w, l0_ffn_conv_b, l0_ffn_down),
            (l1_ffn_up, l1_ffn_conv_w, l1_ffn_conv_b, l1_ffn_down))
    for i in range(DEPTH):
        mixer, params = mixers[i]
        x = x + mixer(rms_norm(x, mix_norms[i]), *params)
        x = x + conv_ffn(rms_norm(x, ffn_norms[i]), *ffns[i])
    return rms_norm(x, final_norm)


_drawn_inputs = setup_inputs


def setup_inputs(seed=0):
    import zlib

    import numpy as np

    out = dict(_drawn_inputs(seed))
    spreads = {}
    factors = {'l0_rwkv_w2': 8.0,
     'l0_rwkv_a0': 3.553,
     'l0_rwkv_a2': 4.266,
     'l0_rwkv_k_k': 28.298,
     'l0_rwkv_k_a': 7.774,
     'l0_rwkv_ln_g': 8.0,
     'l0_rwkv_ln_b': 8.0,
     'l0_ssd_d': 5.214,
     'l0_ssd_norm_g': 3.315,
     'l0_norm_ffn': 3.701,
     'l0_ffn_conv_b': 3.867,
     'l1_norm_mix': 3.923,
     'l1_s5_lam_re': 64.0,
     'l1_s5_lam_im': 37.0,
     'l1_s5_log_dt': 39.2,
     'l1_s5_b_re': 52.984,
     'l1_s5_b_im': 54.128,
     'l1_s5_c_re': 52.672,
     'l1_s5_c_im': 53.952,
     'l1_s5_b_glu': 64.0,
     'l1_norm_ffn': 5.121,
     'l1_ffn_conv_b': 5.47,
     'final_norm': 9.084}
    for name, (base, spread) in spreads.items():
        noise = np.random.default_rng([zlib.crc32(name.encode()), seed]).standard_normal(out[name].shape)
        drawn = base * np.exp(spread * noise) if base else spread * noise
        out[name] = jnp.asarray(drawn.astype(out[name].dtype))
    for name, factor in factors.items():
        out[name] = (out[name] * factor).astype(out[name].dtype)
    return out
```

```python
from contextlib import ExitStack, contextmanager

import numpy as np

import concourse.bass as bass
from concourse import mybir

F32 = mybir.dt.float32
ACT = mybir.ActivationFunctionType
ALU = mybir.AluOpType

P = 128
T = 512
D = 1024
KD = D // P
TT = T // P
EPS = 1e-6
SOFT = float(np.exp(-0.5))

H_RWKV, N_RWKV, CH = 8, 64, 64
NC = T // CH
GN_EPS = 64e-5
SSD_G, SSD_J, SSD_P = 2, 8, 64
S5_G, S5_CH, S5_N, S5_T = 32, 16, 64, 8
S5_C = T // S5_T
S5_PAIR = S5_G // 2
RET_H, DK, DV = 4, 128, 256
FH = 2816
KF = FH // P
KO = 12
SLOT = KF * P

MAGIC = 12582912.0
INV_2PI = float(1.0 / (2.0 * np.pi))
PI_A = 6.28125
PI_B = float(np.float32(2.0 * np.pi - 6.28125))
PI_C = float(2.0 * np.pi - 6.28125 - float(np.float32(2.0 * np.pi - 6.28125)))
PI_MAX = 3.1415925

COLS0 = [("mix_g0", KD), ("mu", 14), ("w0", 4), ("a0", 4), ("k_k", 4), ("k_a", 4), ("r_k", 4), ("ln_g", 4),
         ("ln_b", 4), ("cw", 4 * 12), ("cb", 12), ("dt_bias", 64), ("a_log", 64), ("w_dt", 128), ("ssd_d", 8), ("ssd_g", 8),
         ("ffn_g0", KD), ("fcw0", 3 * 2 * KF), ("fcb0", 2 * KF), ("mix_g1", KD), ("s5_d", 4), ("b_glu", 4),
         ("ffn_g1", KD), ("fcw1", 3 * 2 * KF), ("fcb1", 2 * KF), ("final_g", KD)]
COLS1 = [("lam_re", 16), ("lam_im", 16), ("log_dt", 16), ("b_re", 256), ("b_im", 256), ("c_re", 256),
         ("c_im", 256)]
CONST0 = [("ident", P), ("ones", P), ("bones", P), ("triu", P), ("strict", P), ("incl", P), ("level", 6 * P),
          ("ident2", 64), ("reset", T)]
CONST1 = [("cosq", T), ("sinq", T), ("cosk", T), ("sink", T), ("decay", RET_H * P), ("qdec", RET_H * P),
          ("kdec", RET_H), ("gchunk", RET_H)]


def offsets(parts):
    at, out = 0, {}
    for name, n in parts:
        out[name] = (at, n)
        at += n
    return out, at


O_COL0, N_COL0 = offsets(COLS0)
O_COL1, N_COL1 = offsets(COLS1)
O_CON0, N_CON0 = offsets(CONST0)
O_CON1, N_CON1 = offsets(CONST1)


def constants():
    r = np.arange(P)
    s, t = r[:, None], r[None, :]
    same = (s // CH) == (t // CH)
    c = {
        "ident": np.eye(P), "ones": np.ones((P, P)), "bones": np.where(same, 1.0 / CH, 0.0),
        "triu": (s <= t), "strict": same & (s < t), "incl": same & (s <= t),
        "ident2": np.tile(np.eye(CH), (2, 1)),
        "reset": np.tile((np.arange(T) % CH != 0)[None, :], (P, 1)),
    }
    c["level"] = np.concatenate(
        [(s // (2 << l) == t // (2 << l)) & (s % (2 << l) < (1 << l)) & (t % (2 << l) >= (1 << l))
         for l in range(6)], axis=1)
    half = DK // 2
    theta = (1.0 / (10000.0 ** np.linspace(0.0, 1.0, half))).astype(np.float32)
    ang = (np.arange(T, dtype=np.float32)[None, :] * theta[:, None]).astype(np.float64)
    cos, sin = np.cos(ang), np.sin(ang)
    c["cosq"] = np.concatenate([cos, cos])
    c["sinq"] = np.concatenate([-sin, sin])
    c["cosk"], c["sink"] = c["cosq"] * DK ** -0.5, c["sinq"] * DK ** -0.5
    lg = np.log(1.0 - 2.0 ** (-5.0 - np.arange(RET_H)))
    c["decay"] = np.concatenate([np.where(s <= t, np.exp(np.maximum(t - s, 0) * g), 0.0) for g in lg], axis=1)
    c["qdec"] = np.concatenate([np.tile(np.exp((r + 1.0) * g)[None, :], (P, 1)) for g in lg], axis=1)
    c["kdec"] = np.stack([np.exp((P - 1.0 - r) * g) for g in lg], axis=1)
    c["gchunk"] = np.tile(np.exp(P * lg)[None, :], (P, 1))
    pack = lambda parts: np.concatenate([np.asarray(c[n], np.float32) for n, _ in parts], axis=1)
    return pack(CONST0), pack(CONST1)


class Own:

    def __init__(self, eng, sem):
        self.eng, self.sem, self.base, self.k, self.i, self.per = eng, sem, 0, 0, None, 0

    def count(self):
        return self.base + self.k if self.i is None else self.base + self.per * self.i + self.k

    def go(self, ins):
        ins.then_inc(self.sem, 1)
        self.k += 1

    def wait(self):
        self.eng.wait_ge(self.sem, self.count())

    def do(self, ins):
        self.go(ins)
        self.wait()

    @contextmanager
    def loop(self, trips, per):
        self.base, self.k, self.per = self.base + self.k, 0, per
        with self.eng.Fori(0, trips) as i:
            self.i = i
            yield i
        assert self.k == per, f"the loop signals {self.k} results a turn, not {per}"
        self.base, self.k, self.i = self.base + per * trips, 0, None


RWKV_DVE, SSD_DVE, RET_DVE = 1, 1, 1

STEPS = [("lora", 1), ("rwkv", 8), ("ssd", 12), ("out0", 8), ("up0", KF), ("down0", 8), ("u", 2), ("ret", 16),
         ("glu", 2), ("out1", 8), ("up1", KF), ("down1", 8)]
O_STEP, N_STEP = offsets(STEPS)
S0 = {k: v[0] for k, v in O_STEP.items()}


def slot_of(base, u, i=0, stride=2):
    return (base + u) % 2, (base + u) // 2 + stride // 2 * i


def trunk(nc, a):
    ctx = ExitStack()
    with ctx:
        def sb(name, shape):
            return ctx.enter_context(nc.sbuf_tensor(name, shape, F32))

        def sem(name):
            return ctx.enter_context(nc.semaphore(name))

        x_t = sb("x_t", [P, KD, T])
        h_t = sb("h_t", [P, KD, T])
        y_t = sb("y_t", [P, KO, T])
        wslot = sb("wslot", [P, 2, SLOT])
        col0 = sb("col0", [P, N_COL0])
        con0 = sb("con0", [P, N_CON0])
        rn = sb("rn", [P, T])
        dts = sb("dts", [P, 8, 64])
        acc_t = sb("acc_t", [64, P])
        REG = 112 * 256
        region = sb("region", [P, REG])
        ps = ctx.enter_context(nc.psum_tensor("ps", [P, 8, 512], F32))

        def C(name, j=0, n=1):
            return col0[:, O_COL0[name][0] + j:O_COL0[name][0] + j + n]

        def Cd(name, j):
            return col0[:, bass.ds(O_COL0[name][0] + j, 1)]

        def K(name):
            o, n = O_CON0[name]
            return con0[:, o:o + n]

        def carver():
            at = [0]

            def take(*dims):
                n = int(np.prod(dims))
                v = region[:, at[0]:at[0] + n]
                at[0] += n
                assert at[0] <= REG, at[0]
                if len(dims) == 2:
                    v = v.rearrange("p (a b) -> p a b", a=dims[0])
                if len(dims) == 3:
                    v = v.rearrange("p (a b c) -> p a b c", a=dims[0], b=dims[1])
                return v
            return take

        take = carver()
        sw, ai, gate = take(4, T), take(4, T), take(4, T)
        pad = take(3, T + 1)
        rr, kq, vv, kk, pp, ip, bh, kh, zz, rd, bt, kt, bonus, tmp = (take(T) for _ in range(14))
        v_tok, b_tok, k_tok = (take(TT, P) for _ in range(3))
        at_, bt_, qb_, qk_, al_, tl, tu, xx = (take(8, P) for _ in range(8))
        rh, wn = take(8, P), take(8, P)
        gt, hh_, st = take(NC, 64), take(NC, 64), take(NC, 64)

        take = carver()
        zs, xs = take(4, T), take(4, T)
        bc_f = take(2, T)
        acb, seg = take(32, P), take(32, P)
        xdt, xdd = take(TT, 512), take(TT, 512)
        b_tk, cbm = take(TT, P), take(TT, P)
        s_ssd = take(3, 512)
        yg = take(4, T)
        dte, cdk = take(32), take(32)

        take = carver()
        hid = take(KF, T)
        cg = take(2, 2, T)

        take = carver()
        con1 = take(N_CON1)
        col1 = take(N_COL1)
        u_p = take(4, T)
        uc = take(S5_G, S5_C)
        lam = take(24, 16)
        pw = take(2, S5_PAIR, 9)
        pwr = take(2, S5_PAIR, 8)
        bb = take(2, S5_PAIR, 16)
        ck = take(2, S5_PAIR, 144)
        wms = take(2 * S5_PAIR, P)
        wm, wm2, kker = wms[:, 0:S5_PAIR, :], wms[:, S5_PAIR:, :], wms
        tmp5 = take(S5_PAIR, 144)
        toep = take(S5_G, P)
        vin = take(S5_C, 2, 16)
        xst = tmp5.rearrange("p a b -> p (a b)")[:, 0:S5_C * 32].rearrange("p (c r q) -> p c r q", c=S5_C, r=2)
        y_ext = y_t[:, :, :].rearrange("p a b -> p (a b)")
        wt_r = y_ext[:, 0:S5_PAIR * P].rearrange("p (a b) -> p a b", a=S5_PAIR)
        wt_i = y_ext[:, S5_PAIR * P:2 * S5_PAIR * P].rearrange("p (a b) -> p a b", a=S5_PAIR)
        xc = y_ext[:, 2 * S5_PAIR * P:3 * S5_PAIR * P].rearrange("p (r a b) -> p r a b", r=2, a=S5_PAIR)
        s5_end_keep = N_CON1 + N_COL1 + 4 * T
        yc = wm.rearrange("p a b -> p (a b)").rearrange("p (g c) -> p g c", g=S5_G)

        rest = [s5_end_keep]

        def keep(*dims):
            n = int(np.prod(dims))
            v = region[:, rest[0]:rest[0] + n]
            rest[0] += n
            assert rest[0] <= REG
            return v.rearrange("p (a b) -> p a b", a=dims[0]) if len(dims) == 2 else v
        y_gl, y_in = keep(4, T), keep(4, T)
        qr, kr, qd, rm = keep(T), keep(T), keep(T), keep(T)
        sm, k_tk = keep(TT, P), keep(TT, P)
        v_tk = keep(TT, DV)
        gs, sq2 = keep(2, T), keep(2, T)
        s_ret = keep(3, DV)

        def K1(name, j=0, n=None):
            o, m = O_CON1[name]
            return con1[:, o + j:o + j + (m if n is None else n)]

        def K1d(name, j, n):
            return con1[:, bass.ds(O_CON1[name][0] + j, n)]

        def C1(name):
            o, n = O_COL1[name]
            return col1[:, o:o + n]

        x_in = h_t[:, :, :].rearrange("p a b -> p (a b)").rearrange("p (t d) -> p t d", t=TT)
        d_acc = nc.dram_tensor("d_acc", [64, P], F32, kind="Internal").ap()
        d_u = nc.dram_tensor("d_u", [512, 8, 64], F32, kind="Internal").ap()
        d_y = nc.dram_tensor("d_y", [512, 8, 64], F32, kind="Internal").ap()

        semaphores = {}

        def on(name):
            if name not in semaphores:
                semaphores[name] = ctx.enter_context(nc.semaphore(name))
            return semaphores[name]

        w_landed = [on("w_landed_0"), on("w_landed_1")]
        psum_free = [on("psum_free_0"), on("psum_free_1")]

        def bank(n, m=1):
            return ps[:, n, :] if m == 1 else ps[:, n:n + m, :]

        def split(v, n):
            return v.rearrange("p (a b) -> p a b", a=n)

        def over(v, n):
            return v.unsqueeze(2).broadcast_to([v.shape[0], v.shape[1], n])

        def each(v, n):
            return v.unsqueeze(1).broadcast_to([v.shape[0], n, v.shape[1]])

        block = ctx.enter_context(nc.Block())

        @block.sync
        def _(sp):
            sp.dma_start(x_in, a["x"].rearrange("b (t p) d -> p (b t) d", p=P)).then_inc(on("x_loaded"), 16)
            sp.dma_start(con0[:], a["con0"]).then_inc(on("consts_in"), 16)
            sp.dma_start(col0[:], a["col0"]).then_inc(on("cols_in"), 16)

            def load(src, n, step, slot, free):
                if free:
                    sp.wait_ge(on("gemm_done"), step - 1)
                sp.dma_start(wslot[:, slot, 0:n], src).then_inc(w_landed[slot], 16)

            def stream(name, phase, n):
                w, base, count = a[name], S0[phase], O_STEP[phase][1]
                u = 0
                while u < count and (base + u < 2 or (count - u) % 2):
                    load(w[u], n, base + u, (base + u) % 2, base + u >= 2)
                    u += 1
                if count == u:
                    return
                with sp.Fori(0, (count - u) // 2) as i:
                    for v in (u, u + 1):
                        load(w[bass.ds(2 * i + v, 1)].rearrange("a p n -> p (a n)"), n, base + v + 2 * i,
                             (base + v) % 2, True)

            for name, phase, n in (("w_lora", "lora", 2048), ("w_rwkv", "rwkv", 2048), ("w_ssd", "ssd", 2048),
                                   ("w_out0", "out0", KO * P), ("w_up0", "up0", 2048), ("w_down0", "down0", SLOT),
                                   ("w_u", "u", 2048), ("w_ret", "ret", 2048), ("w_glu", "glu", 1024),
                                   ("w_out1", "out1", KO * P), ("w_up1", "up1", 2048),
                                   ("w_down1", "down1", SLOT)):
                stream(name, phase, n)
            for t in range(TT):
                sp.wait_ge(on("rows_ready"), t + 1)
                sp.dma_start(a["out"].rearrange("b (t p) d -> (b t) p d", p=P)[t],
                             y_t[:, 2 * t:2 * t + 2, :].rearrange("p a b -> p (a b)")).then_inc(on("stored"), 16)
            sp.wait_ge(on("stored"), 16 * TT)

        @block.gpsimd
        def _(pool):
            pool.dma_start(at_[0:64, 0:4, :], a["w2"]).then_inc(on("lora_in"), 16)
            pool.dma_start(at_[64:128, 0:4, :], a["a2"]).then_inc(on("lora_in"), 16)
            pool.dma_start(bt_[:, 0:4, :], a["g2"]).then_inc(on("lora_in"), 16)
            pool.wait_ge(on("acc_turned"), 1)
            pool.dma_start(d_acc, acc_t[:, :]).then_inc(on("acc_stored"), 16)
            pool.wait_ge(on("acc_stored"), 16)
            for g in range(SSD_G):
                if g == 0:
                    pool.wait_ge(on("rwkv_head"), 4)
                else:
                    pool.wait_ge(on("ssd_group"), g)
                pool.dma_start(acb, d_acc[g * 32:(g + 1) * 32].unsqueeze(0).broadcast_to([P, 32, P]))\
                    .then_inc(on("acc_spread"), 16)
            pool.wait_ge(on("x_ready"), 3 * KD)
            pool.dma_start(con1, a["con1"]).then_inc(on("consts1_in"), 16)
            pool.dma_start(col1, a["col1"]).then_inc(on("consts1_in"), 16)
            pool.wait_ge(on("u_ready"), 4)
            for i in range(4):
                pool.dma_start(d_u[i * P:(i + 1) * P].rearrange("p s c -> p (s c)"), u_p[:, i, :])\
                    .then_inc(on("u_stored"), 16)
            pool.wait_ge(on("u_stored"), 64)
            for s in range(S5_T):
                pool.dma_start(uc[s * 16:(s + 1) * 16, :, :],
                               d_u[:, s, :].rearrange("(g c) k -> c g k", c=16)).then_inc(on("u_spread"), 16)
            pool.wait_ge(on("kernels_out"), 2)
            pool.wait_ge(on("toep_cleared"), 1)
            for s in range(S5_T):
                pool.dma_start(toep[s * 16:(s + 1) * 16, :, s * 16:P], kker[0:16, :, 0:P - s * 16])\
                    .then_inc(on("kernels_spread"), 16)
            pool.wait_ge(on("s5_out"), 4)
            for t in range(S5_T):
                pool.dma_start(d_y[:, t, :].rearrange("(g c) k -> c g k", c=16), yc[t * 16:(t + 1) * 16, :, :])\
                    .then_inc(on("s5_stored"), 16)
            pool.wait_ge(on("s5_stored"), 16 * S5_T)
            for i in range(4):
                pool.dma_start(y_in[:, i, :], d_y[i * P:(i + 1) * P].rearrange("p s c -> p (s c)"))\
                    .then_inc(on("s5_back"), 16)
            pool.wait_ge(on("s5_back"), 64)

        @block.scalar
        def _(act):
            own = Own(act, on("act_own"))

            def norm(n):
                for k in range(KD):
                    act.wait_ge(on("x_ready"), KD * n + k + 1)
                    own.go(act.activation(h_t[:, k, :], x_t[:, k, :], ACT.Square))
                    own.wait()
                    act.sem_inc(on("squares"), 1)
                act.wait_ge(on("norm_var"), n + 1)
                own.do(act.activation(rn[:], rn[:], ACT.Sqrt))
                act.sem_inc(on("norm_std"), 1)

            def root(var, std, n):
                act.wait_ge(on(var), n)
                own.do(act.activation(rn[:], rn[:], ACT.Sqrt))
                act.sem_inc(on(std), 1)

            def mlp(layer):
                base = S0[f"up{layer}"]
                with own.loop(KF // 2, 6) as i:
                    for u in (0, 1):
                        par = (base + u) % 2
                        act.wait_ge(on("gemm_done"), base + u + 2 * i + 1)
                        act.wait_ge(on("cg_read"), layer * KF + u + 2 * i + 1)
                        for half in (0, 1):
                            j = u + 2 * i + KF * half
                            own.go(act.activation(cg[:, par, half, :], bank(2 * par + half), ACT.Identity,
                                                  scale=Cd(f"fcw{layer}", j + 2 * 2 * KF), bias=Cd(f"fcb{layer}", j)))
                        own.wait()
                        act.sem_inc(on("mlp_affine"), 1)
                        act.wait_ge(on("mlp_conv"), layer * KF + u + 2 * i + 1)
                        own.do(act.activation(cg[:, par, 0, :], cg[:, par, 0, :], ACT.Silu))
                        act.sem_inc(on("mlp_gate"), 1)

            act.wait_ge(on("x_turned"), 1)
            for k in range(KD):
                own.do(act.activation(x_t[:, k, :], bank(k), ACT.Copy))
                act.sem_inc(on("x_ready"), 1)
            norm(0)
            act.wait_ge(on("cols_in"), 16)

            for j in range(3):
                own.do(act.activation(pad[:, j, 0:1], col0[:, 0:1], ACT.Copy, scale=0.0))
            act.wait_ge(on("gemm_done"), 1)
            for j in (0, 1):
                own.do(act.activation(pad[:, j, 1:T + 1], bank(j), ACT.Copy))
            act.sem_inc(psum_free[0], 1)
            act.sem_inc(on("lora_pad"), 1)
            act.wait_ge(on("lora_mixed"), 1)
            own.do(act.activation(rr[0:64], kq[0:64], ACT.Tanh))
            own.do(act.activation(rr[64:128], kq[64:128], ACT.Copy))
            own.do(act.activation(vv[:], kk[:], ACT.Sigmoid))
            act.sem_inc(on("lora_acts"), 1)
            act.wait_ge(on("dt_abs"), 1)
            own.do(act.activation(dts[:, 1, :], dts[:, 1, :], ACT.Exp, scale=-1.0))
            own.do(act.activation(dts[:, 2, :], dts[:, 1, :], ACT.Ln, bias=1.0))
            own.do(act.activation(dts[:, 3, :], C("a_log", 0, 64), ACT.Exp))
            act.sem_inc(on("dt_exp"), 1)

            for j in range(4):
                act.wait_ge(on("lora_w"), j + 1)
                own.do(act.activation(sw[:, j, :], bank(2 * (j % 2) + 4), ACT.Sigmoid, bias=C("w0", j)))
                own.do(act.activation(ai[:, j, :], bank(2 * (j % 2) + 5), ACT.Sigmoid, bias=C("a0", j)))
                act.sem_inc(on("lora_w_out"), 1)

            base = S0["rwkv"]
            with own.loop(4, 26) as r:
                act.wait_ge(on("gemm_done"), base + 2 * r + 1)
                act.wait_ge(on("pads_read"), r + 1)
                for j in (0, 1):
                    own.do(act.activation(pad[:, j, 1:T + 1], bank(2 + j), ACT.Copy))
                act.sem_inc(psum_free[1], 1)
                act.sem_inc(on("rk_pad"), 1)
                act.wait_ge(on("gemm_done"), base + 2 * r + 2)
                own.do(act.activation(pad[:, 2, 1:T + 1], bank(0), ACT.Copy))
                act.sem_inc(psum_free[0], 1)
                act.sem_inc(on("v_pad"), 1)
                act.wait_ge(on("log_decay"), r + 1)
                own.do(act.activation(pp[:], zz[:], ACT.Exp, scale=-SOFT))
                own.do(act.activation(ip[:], zz[:], ACT.Exp, scale=SOFT))
                act.sem_inc(on("decays"), 1)
                act.wait_ge(on("kk_var"), r + 1)
                own.do(act.activation(rn[:], rn[:], ACT.Sqrt))
                act.sem_inc(on("kk_std"), 1)
                act.wait_ge(on("tok_turned"), r + 1)
                for hd in (0, 1):
                    own.do(act.activation(rh[:, 4 * hd:4 * hd + 4, 0:64],
                                          split(bank(0), 4)[:, :, 64 * hd:64 * hd + 64], ACT.Copy))
                own.do(act.activation(v_tok, split(bank(1), 4), ACT.Copy))
                own.do(act.activation(b_tok, split(bank(2), 4), ACT.Copy))
                own.do(act.activation(k_tok, split(bank(3), 4), ACT.Copy))
                act.sem_inc(on("toks"), 1)
                act.wait_ge(on("bv_done"), r + 1)
                own.do(act.activation(rh[:, :, 64:128], split(bank(0), 8), ACT.Copy))
                act.sem_inc(on("rhs_ready"), 1)
                for level in range(1, 6):
                    act.wait_ge(on("x_done"), 6 * r + level + 1)
                    for half in (0, 1):
                        own.do(act.activation(xx[:, 4 * half:4 * half + 4, :], split(bank(4 + half), 4), ACT.Copy))
                    act.sem_inc(on("x_out"), 1)
                act.wait_ge(on("wu_done"), r + 1)
                for half in (0, 1):
                    own.do(act.activation(wn[:, 4 * half:4 * half + 4, :], split(bank(6 + half), 4), ACT.Copy,
                                          scale=-1.0))
                act.sem_inc(on("wn_ready"), 1)
                act.wait_ge(on("gn_dev"), r + 1)
                own.do(act.activation(tmp[:], kk[:], ACT.Square))
                act.sem_inc(on("gn_sq"), 1)
                act.wait_ge(on("gn_var"), r + 1)
                own.do(act.activation(rn[:], rn[:], ACT.Sqrt))
                act.sem_inc(on("gn_std"), 1)

            base = S0["ssd"]
            with own.loop(SSD_G, 24) as g:
                def affine(u, tiles):
                    act.wait_ge(on("gemm_done"), base + u + 6 * g + 1)
                    slot, _ = slot_of(base, u)
                    for m, (dst, j) in enumerate(tiles):
                        own.go(act.activation(dst, bank(2 * slot + m), ACT.Identity,
                                              scale=Cd("cw", 3 * 12 + 6 * g + j), bias=Cd("cb", 6 * g + j)))
                    own.wait()
                    act.sem_inc(on("ssd_affine"), 1)

                def silu(u, tiles):
                    act.wait_ge(on("ssd_conv"), 4 * g + u + 1)
                    for dst in tiles:
                        own.go(act.activation(dst, dst, ACT.Silu))
                    own.wait()
                    act.sem_inc(on("xbc_ready"), 1)

                affine(0, [(bc_f[:, 0, :], 0)])
                affine(1, [(bc_f[:, 1, :], 1)])
                silu(0, [bc_f[:, 0, :]])
                affine(2, [(xs[:, 0, :], 2), (xs[:, 1, :], 3)])
                silu(1, [bc_f[:, 1, :]])
                affine(3, [(xs[:, 2, :], 4), (xs[:, 3, :], 5)])
                silu(2, [xs[:, 0, :], xs[:, 1, :]])
                silu(3, [xs[:, 2, :], xs[:, 3, :]])
                for u in (4, 5):
                    act.wait_ge(on("gemm_done"), base + u + 6 * g + 1)
                    slot, _ = slot_of(base, u)
                    for m in (0, 1):
                        own.go(act.activation(zs[:, 2 * (u - 4) + m, :], bank(2 * slot + m), ACT.Silu))
                    own.wait()
                    act.sem_inc(psum_free[slot], 1)
                    act.sem_inc(on("zs_ready"), 1)
                act.wait_ge(on("ssd_logs"), g + 1)
                own.do(act.activation(dte, dte, ACT.Exp))
                own.do(act.activation(seg.rearrange("p a b -> p (a b)"), seg.rearrange("p a b -> p (a b)"), ACT.Exp))
                own.do(act.activation(acb.rearrange("p a b -> p (a b)"), acb.rearrange("p a b -> p (a b)"), ACT.Exp))
                act.sem_inc(on("ssd_exps"), 1)
                for i in range(4):
                    act.wait_ge(on("yg_ready"), 4 * g + i + 1)
                    own.do(act.activation(xs[:, i, :], yg[:, i, :], ACT.Square))
                    act.sem_inc(on("yg_sq"), 1)
                root("ssd_var", "ssd_std", g + 1)

            norm(1)
            mlp(0)
            norm(2)

            act.wait_ge(on("consts1_in"), 32)
            own.do(act.activation(lam[:, 0, :], C1("log_dt"), ACT.Exp))
            act.sem_inc(on("s5_dt"), 1)
            act.wait_ge(on("s5_angle"), 1)
            own.do(act.activation(lam[:, 1, :], lam[:, 1, :], ACT.Exp))
            own.do(act.activation(lam[:, 3, :], lam[:, 2, :], ACT.Sin))
            own.do(act.activation(lam[:, 4, :], lam[:, 2, :], ACT.Sin, scale=0.5))
            act.sem_inc(on("s5_trig"), 1)
            for half, dst in ((0, wt_r), (1, wt_i)):
                act.wait_ge(on("wm_turned"), half + 1)
                for b in range(4):
                    own.do(act.activation(dst[:, 4 * b:4 * b + 4, :], split(bank(4 + b), 4), ACT.Copy))
                act.sem_inc(on("wm_out"), 1)
            for half in (0, 1):
                act.wait_ge(on("kernels_done"), half + 1)
                for b in range(4):
                    eight = kker[0:16, 16 * half + 8 * (b % 2):16 * half + 8 * (b % 2) + 8, :]
                    own.do(act.activation(eight.rearrange("p (g o) c -> p g o c", o=2)[:, :, b // 2, :],
                                          split(bank(4 + b), 4)[0:16], ACT.Copy))
                act.sem_inc(on("kernels_out"), 1)
            act.wait_ge(on("vin_done"), 1)
            for ri in (0, 1):
                for b in (0, 1):
                    own.do(act.activation(vin[:, :, ri, 8 * b:8 * b + 8],
                                          split(bank(4 + 2 * ri + b), 8).rearrange("p q c -> p c q"), ACT.Copy))
            act.sem_inc(on("vin_out"), 1)
            act.wait_ge(on("s5_y"), 1)
            act.wait_ge(on("kernels_spread"), 16 * S5_T)
            for b in range(4):
                every_other = yc[:, 16 * (b % 2):16 * (b % 2) + 16, :].rearrange("p (g o) c -> p g o c", o=2)
                own.do(act.activation(every_other[:, :, b // 2, :], split(bank(4 + b), 8), ACT.Copy))
                act.sem_inc(on("s5_out"), 1)
            for i in range(4):
                act.wait_ge(on("s5_skip"), i + 1)
                own.do(act.activation(y_gl[:, i, :].rearrange("p (c s) -> p s c", s=S5_T), split(y_in[:, i, :], S5_T),
                                      ACT.Gelu_apprx_tanh))
                act.sem_inc(on("gelu_ready"), 1)

            base = S0["ret"]
            with own.loop(RET_H, 9) as h:
                act.wait_ge(on("ret_read"), h + 1)
                for v in (0, 1):
                    act.wait_ge(on("gemm_done"), base + 1 + v + 4 * h + 1)
                    slot, _ = slot_of(base, 1 + v)
                    own.do(act.activation(v_tk[:, :, v * P:(v + 1) * P], split(bank(2 * slot), 4), ACT.Copy))
                    act.sem_inc(psum_free[slot], 1)
                act.sem_inc(on("v_tok_ready"), 1)
                act.wait_ge(on("gemm_done"), base + 3 + 4 * h + 1)
                slot, _ = slot_of(base, 3)
                for m in (0, 1):
                    own.do(act.activation(gs[:, m, :], bank(2 * slot + m), ACT.Silu))
                act.sem_inc(psum_free[slot], 1)
                act.sem_inc(on("gs_ready"), 1)
                act.wait_ge(on("scores_done"), h + 1)
                own.do(act.activation(k_tk, split(bank(5), 4), ACT.Copy, scale=K1d("kdec", h, 1)))
                act.sem_inc(on("k_tok_ready"), 1)
                act.wait_ge(on("ret_y"), h + 1)
                for m in (0, 1):
                    own.do(act.activation(sq2[:, m, :], bank(4 + m), ACT.Square))
                act.sem_inc(on("ret_sq"), 1)
                act.wait_ge(on("ret_var"), h + 1)
                own.do(act.activation(rn[:], rn[:], ACT.Sqrt))
                act.sem_inc(on("ret_std"), 1)
                own.do(act.activation(dts[:, 7, 0:1], dts[:, 0, 0:1], ACT.Copy))

            base = S0["glu"]
            for u in (0, 1):
                slot, _ = slot_of(base, u)
                act.wait_ge(on("gemm_done"), base + u + 1)
                for m in (0, 1):
                    own.do(act.activation([qr, kr, qd, rm][2 * u + m], bank(2 * slot + m), ACT.Sigmoid,
                                          bias=C("b_glu", 2 * u + m)))
                act.sem_inc(psum_free[slot], 1)
                act.sem_inc(on("glu_gate"), 1)

            norm(3)
            mlp(1)
            norm(4)

        @block.tensor
        def _(pe):
            ones, ident, bones = K("ones"), K("ident"), K("bones")

            def begin(base, u, i=0, stride=2):
                slot, before = slot_of(base, u, i, stride)
                pe.wait_ge(w_landed[slot], 16 * (before + 1))
                if base + u >= 2:
                    pe.wait_ge(psum_free[slot], before)
                return slot

            def product(base, u, i, stride, kt_, rhs, tiles=2):
                slot = begin(base, u, i, stride)
                w = wslot[:, slot, 0:tiles * kt_ * P].rearrange("p (m k c) -> p m k c", m=tiles, k=kt_)
                for m in range(tiles):
                    for k in range(kt_):
                        mm = pe.matmul(bank(2 * slot + m), w[:, m, k, :], rhs(k), start=k == 0, stop=k == kt_ - 1)
                mm.then_inc(on("gemm_done"), 1)

            h_of, y_of, hid_of = (lambda k: h_t[:, k, :]), (lambda k: y_t[:, k, :]), (lambda k: hid[:, k, :])

            def norm(n, free):
                if free:
                    free()
                for k in range(KD):
                    pe.wait_ge(on("squares"), KD * n + k + 1)
                    mm = pe.matmul(bank(7), ones, h_t[:, k, :], start=k == 0, stop=k == KD - 1)
                mm.then_inc(on("norm_sum"), 1)
                pe.wait_ge(on("h_ready"), KD * (n + 1))

            def mlp(layer):
                with pe.Fori(0, KF // 2) as i:
                    for u in (0, 1):
                        product(S0[f"up{layer}"], u, i, 2, KD, h_of)
                pe.wait_ge(on("hid_ready"), KF * (layer + 1))
                with pe.Fori(0, KD // 2) as i:
                    for u in (0, 1):
                        product(S0[f"down{layer}"], u, i, 2, KF, hid_of, 1)

            def project_out(layer):
                with pe.Fori(0, KD // 2) as i:
                    for u in (0, 1):
                        product(S0[f"out{layer}"], u, i, 2, KO, y_of, 1)

            pe.wait_ge(on("x_loaded"), 16)
            pe.wait_ge(on("consts_in"), 16)
            for k in range(KD):
                for t in range(TT):
                    mm = pe.transpose(ps[:, k, t * P:(t + 1) * P], x_in[:, t, k * P:(k + 1) * P], ident)
            mm.then_inc(on("x_turned"), 1)
            norm(0, None)

            product(S0["lora"], 0, 0, 2, KD, h_of)
            pe.wait_ge(on("cols_in"), 16)
            wdt = C("w_dt", 0, 128).rearrange("p (k h) -> p k h", k=KD)
            for t in range(TT):
                for k in range(KD):
                    mm = pe.matmul(ps[:, 6, t * 16:(t + 1) * 16], h_t[:, k, t * P:(t + 1) * P], wdt[:, k, :],
                                   start=k == 0, stop=k == KD - 1)
            mm.then_inc(on("dt_sum"), 1)
            pe.wait_ge(on("dt_rates"), 1)
            pe.matmul(ps[:, 6, 0:64], K("triu"), dts[:, 5, :], start=True, stop=True).then_inc(on("acc_sum"), 1)
            pe.wait_ge(on("acc_ready"), 1)
            pe.transpose(ps[0:64, 6, 0:P], dts[:, 6, :], ident).then_inc(on("acc_turn"), 1)
            pe.wait_ge(on("acc_turned"), 1)
            pe.wait_ge(on("lora_acts"), 1)
            pe.wait_ge(on("lora_in"), 48)
            for j in range(4):
                if j >= 2:
                    pe.wait_ge(on("lora_w_out"), j - 1)
                b = 2 * (j % 2) + 4
                pe.matmul(bank(b), at_[0:64, j, :], rr[0:64], start=True, stop=True)
                pe.matmul(bank(b + 1), at_[64:128, j, :], rr[64:128], start=True, stop=True)\
                    .then_inc(on("lora_w"), 1)
            for j in range(4):
                if j >= 2:
                    pe.wait_ge(on("lora_g_out"), j - 1)
                pe.matmul(bank(2 + j % 2), bt_[:, j, :], vv[:], start=True, stop=True).then_inc(on("lora_g"), 1)
            pe.wait_ge(on("lora_g_out"), 4)

            base = S0["rwkv"]
            pairs = [(hd, t) for hd in (0, 1) for t in range(TT)]

            def mat(b0, m):
                return ps[:, b0 + m // 4, (m % 4) * P:(m % 4 + 1) * P]

            with pe.Fori(0, 4) as r:
                product(base, 0, r, 2, KD, h_of)
                pe.wait_ge(on("gn_read"), r + 1)
                product(base, 1, r, 2, KD, h_of, 1)
                pe.wait_ge(on("kk_sq"), r + 1)
                pe.matmul(bank(4), bones, tmp[:], start=True, stop=True).then_inc(on("kk_sum"), 1)
                pe.wait_ge(on("bonus_in"), r + 1)
                pe.matmul(bank(5), bones, bt[:], start=True, stop=True).then_inc(on("bonus_sum"), 1)
                pe.wait_ge(on("keys"), r + 1)
                for hd in (0, 1):
                    lo, hi = 64 * hd, 64 * hd + 64
                    for b, (lh, rhs_) in enumerate(((bh, zz), (kh, zz), (bh, rd), (kh, rd))):
                        for t in range(TT):
                            mm = pe.matmul(ps[:, 4 * hd + b, t * P:(t + 1) * P], lh[lo:hi, t * P:(t + 1) * P],
                                           rhs_[lo:hi, t * P:(t + 1) * P], start=True, stop=True)
                    mm.then_inc(on("grams"), 1)
                pe.wait_ge(on("tails"), r + 1)
                pe.wait_ge(on("grams_out"), 2 * r + 1)
                for b, src in enumerate((zz, vv, bt, kt)):
                    for t in range(TT):
                        mm = pe.transpose(ps[:, b, t * P:(t + 1) * P], src[:, t * P:(t + 1) * P], ident)
                mm.then_inc(on("tok_turned"), 1)
                pe.wait_ge(on("al_ready"), 6 * r + 1)
                for m in range(8):
                    mm = pe.matmul(mat(4, m), al_[:, m, :], ident, start=True, stop=True)
                mm.then_inc(on("x_done"), 1)
                pe.wait_ge(on("toks"), r + 1)
                for m, (hd, t) in enumerate(pairs):
                    mm = pe.matmul(ps[:, 0, m * 64:(m + 1) * 64], bt_[:, m, :], v_tok[:, t, 64 * hd:64 * hd + 64],
                                   start=True, stop=True)
                mm.then_inc(on("bv_done"), 1)
                for level in range(1, 6):
                    pe.wait_ge(on("al_ready"), 6 * r + level + 1)
                    for m in range(8):
                        mm = pe.matmul(mat(4, m), al_[:, m, :], tl[:, m, :], start=True, stop=True)
                    mm.then_inc(on("x_done"), 1)
                    pe.wait_ge(on("x_out"), 5 * r + level)
                    if level < 5:
                        for m in range(8):
                            pe.matmul(mat(6, m), tu[:, m, :], xx[:, m, :], start=True, stop=True)
                    for m in range(8):
                        mm = pe.matmul(mat(4, m), xx[:, m, :], tu[:, m, :], start=True, stop=True)
                    mm.then_inc(on("tx_done"), 1)
                pe.wait_ge(on("tu_ready"), r + 1)
                pe.wait_ge(on("rhs_ready"), r + 1)
                for m in range(8):
                    mm = pe.matmul(mat(6, m), tu[:, m, :], rh[:, m, :], start=True, stop=True)
                mm.then_inc(on("wu_done"), 1)
                pe.wait_ge(on("wn_ready"), r + 1)
                for m, (hd, t) in enumerate(pairs):
                    lo, hi = 64 * hd, 64 * hd + 64
                    pe.matmul(ps[lo:hi, 4, t * P:(t + 1) * P], wn[:, m, 0:64], qb_[:, m, :], start=True, stop=True)
                    for q in (0, 1):
                        c, ql, qh = 2 * t + q, 64 * q, 64 * q + 64
                        pe.matmul(ps[lo:hi, 5 + q, c * 64:(c + 1) * 64], wn[ql:qh, m, 0:64], b_tok[ql:qh, t, lo:hi],
                                  start=True, stop=True)
                        pe.matmul(ps[lo:hi, 7 * q, c * 64:(c + 1) * 64], b_tok[ql:qh, t, lo:hi], wn[ql:qh, m, 64:128],
                                  start=True, stop=False)
                        mm = pe.matmul(ps[lo:hi, 7 * q, c * 64:(c + 1) * 64], k_tok[ql:qh, t, lo:hi],
                                       v_tok[ql:qh, t, lo:hi], start=False, stop=True)
                mm.then_inc(on("chunk_maps"), 1)
                for c in range(1, NC - 1):
                    pe.wait_ge(on("state_ready"), (NC - 1) * r + c)
                    pe.sem_inc(on("state_seen"), 1)
                    for lo in (0, 64):
                        mm = pe.matmul(ps[lo:lo + 64, 1, c * 64:(c + 1) * 64], gt[lo:lo + 64, c, :],
                                       st[lo:lo + 64, c, :], start=True, stop=True)
                    mm.then_inc(on("state_moved"), 1)
                pe.wait_ge(on("state_ready"), (NC - 1) * (r + 1))
                for m, (hd, t) in enumerate(pairs):
                    lo, hi = 64 * hd, 64 * hd + 64
                    out = ps[lo:hi, 2, t * P:(t + 1) * P]
                    pe.matmul(out, v_tok[:, t, lo:hi], qk_[:, m, :], start=True, stop=False)
                    mm = pe.matmul(out, wn[:, m, 64:128], qb_[:, m, :], start=False, stop=True)
                    for q in (0, 1):
                        c = 2 * t + q
                        if c:
                            mm = pe.matmul(ps[lo:hi, 2, c * 64:(c + 1) * 64], st[lo:hi, c, :],
                                           rd[lo:hi, c * 64:(c + 1) * 64], start=False, stop=True,
                                           skip_group_check=True)
                mm.then_inc(on("rwkv_y"), 1)
                pe.wait_ge(on("gn_in"), r + 1)
                pe.matmul(bank(3), bones, kk[:], start=True, stop=True).then_inc(on("gn_mean"), 1)
                pe.wait_ge(on("gn_sq"), r + 1)
                pe.matmul(bank(0), bones, tmp[:], start=True, stop=True).then_inc(on("gn_sum"), 1)
            pe.wait_ge(on("rwkv_head"), 4)

            base = S0["ssd"]
            with pe.Fori(0, SSD_G) as g:
                for u, tiles in enumerate((1, 1, 2, 2, 2, 2)):
                    product(base, u, g, 6, KD, h_of, tiles)
                pe.wait_ge(on("xbc_ready"), 4 * g + 2)
                for t in range(TT):
                    tok = slice(t * P, (t + 1) * P)
                    pe.matmul(ps[:, 4, tok], bc_f[:, 0, tok], bc_f[:, 1, tok], start=True, stop=True)
                    mm = pe.transpose(ps[:, 5, tok], bc_f[:, 0, tok], ident)
                mm.then_inc(on("cb_done"), 1)
                pe.wait_ge(on("cb_out"), g + 1)
                pe.wait_ge(on("xbc_ready"), 4 * g + 4)
                for t in range(TT):
                    for i in range(4):
                        mm = pe.transpose(ps[:, 4 + t, i * P:(i + 1) * P], xs[:, i, t * P:(t + 1) * P], ident)
                mm.then_inc(on("xs_turned"), 1)
                pe.wait_ge(on("xd_ready"), g + 1)
                for t in range(TT - 1):
                    mm = pe.matmul(bank(4 + t), b_tk[:, t, :], xdd[:, t, :], start=True, stop=True)
                mm.then_inc(on("ssd_new"), 1)
                pe.wait_ge(on("ssd_state"), g + 1)
                pe.wait_ge(on("ssd_masks"), g + 1)
                for i in range(4):
                    for t in range(TT):
                        for hd in (0, 1):
                            j = 2 * i + hd
                            out = ps[64 * hd:64 * hd + 64, 4 + i, t * P:(t + 1) * P]
                            mm = pe.matmul(out, xdt[:, t, j * 64:(j + 1) * 64], seg[:, t * 8 + j, :],
                                           start=True, stop=t == 0)
                            if t:
                                mm = pe.matmul(out, s_ssd[:, t - 1, j * 64:(j + 1) * 64], acb[:, t * 8 + j, :],
                                               start=False, stop=True)
                mm.then_inc(on("ssd_y"), 1)
                for i in range(4):
                    pe.wait_ge(on("yg_sq"), 4 * g + i + 1)
                    if i == 0:
                        pe.wait_ge(on("yg_ready"), 4 * g + 4)
                    mm = pe.matmul(bank(4), ones, xs[:, i, :], start=i == 0, stop=i == 3)
                mm.then_inc(on("ssd_sum"), 1)
                pe.wait_ge(on("ssd_group"), g + 1)

            project_out(0)
            norm(1, None)
            mlp(0)
            norm(2, None)

            base = S0["u"]
            for u in (0, 1):
                product(base, u, 0, 2, KD, h_of)
            for half, src in ((0, wm), (1, wm2)):
                pe.wait_ge(on("wm_ready"), 1)
                if half:
                    pe.wait_ge(on("wm_out"), 1)
                for q in range(S5_PAIR):
                    mm = pe.transpose(mat(4, q), src[:, q, :], ident)
                mm.then_inc(on("wm_turned"), 1)
            pe.wait_ge(on("wm_out"), 2)
            pe.wait_ge(on("ck_ready"), 1)
            for half in (0, 1):
                if half:
                    pe.wait_ge(on("kernels_out"), 1)
                for n in range(16):
                    g = 16 * half + n
                    q, lo = g // 2, 64 * (g % 2)
                    out = ps[0:16, 4 + 2 * (n % 2) + n // 8, (n // 2 % 4) * P:(n // 2 % 4 + 1) * P]
                    pe.matmul(out, bb[lo:lo + 64, 0, q, :], ck[lo:lo + 64, 0, q, 0:P], start=True, stop=False)
                    mm = pe.matmul(out, bb[lo:lo + 64, 1, q, :], ck[lo:lo + 64, 1, q, 0:P], start=False, stop=True)
                mm.then_inc(on("kernels_done"), 1)
            pe.wait_ge(on("kernels_out"), 2)
            pe.wait_ge(on("u_spread"), 16 * S5_T)
            for ri, src in ((0, wt_r), (1, wt_i)):
                for g in range(S5_G):
                    q, lo = g // 2, 64 * (g % 2)
                    mm = pe.matmul(ps[lo:lo + 64, 4 + 2 * ri + q // 8, (q % 8) * 64:(q % 8 + 1) * 64],
                                   src[:, q, lo:lo + 64], uc[:, g, :], start=True, stop=True)
            mm.then_inc(on("vin_done"), 1)
            pe.wait_ge(on("s5_states"), 1)
            pe.wait_ge(on("kernels_spread"), 16 * S5_T)
            for g in range(S5_G):
                q, lo = g // 2, 64 * (g % 2)
                out = ps[:, 4 + 2 * (g % 2) + q // 8, (q % 8) * 64:(q % 8 + 1) * 64]
                pe.matmul(out, toep[:, g, :], uc[:, g, :], start=True, stop=False)
                pe.matmul(out, ck[lo:lo + 64, 0, q, 16:144], xc[lo:lo + 64, 0, q, :], start=False, stop=False)
                mm = pe.matmul(out, ck[lo:lo + 64, 1, q, 16:144], xc[lo:lo + 64, 1, q, :], start=False, stop=True)
            mm.then_inc(on("s5_y"), 1)
            pe.wait_ge(on("s5_out"), 4)

            base = S0["ret"]
            with pe.Fori(0, RET_H) as h:
                product(base, 0, h, 4, KD, h_of)
                for v in (0, 1):
                    slot = begin(base, 1 + v, h, 4)
                    w = wslot[:, slot, 0:KD * P].rearrange("p (k c) -> p k c", k=KD)
                    for t in range(TT):
                        for k in range(KD):
                            mm = pe.matmul(ps[:, 2 * slot, t * P:(t + 1) * P], h_t[:, k, t * P:(t + 1) * P],
                                           w[:, k, :], start=k == 0, stop=k == KD - 1)
                    mm.then_inc(on("gemm_done"), 1)
                product(base, 3, h, 4, KD, h_of)
                pe.wait_ge(on("ret_read"), h + 1)
                pe.wait_ge(on("qk_ready"), h + 1)
                for t in range(TT):
                    tok = slice(t * P, (t + 1) * P)
                    pe.matmul(ps[:, 4, tok], kr[:, tok], qr[:, tok], start=True, stop=True)
                    mm = pe.transpose(ps[:, 5, tok], kr[:, tok], ident)
                mm.then_inc(on("scores_done"), 1)
                pe.wait_ge(on("k_tok_ready"), h + 1)
                pe.wait_ge(on("v_tok_ready"), h + 1)
                for t in range(TT - 1):
                    mm = pe.matmul(ps[:, 6 + t // 2, (t % 2) * DV:(t % 2 + 1) * DV], k_tk[:, t, :], v_tk[:, t, :],
                                   start=True, stop=True)
                mm.then_inc(on("ret_new"), 1)
                pe.wait_ge(on("scores_ready"), h + 1)
                pe.wait_ge(on("ret_state"), h + 1)
                for m in (0, 1):
                    for t in range(TT):
                        out = ps[:, 4 + m, t * P:(t + 1) * P]
                        mm = pe.matmul(out, v_tk[:, t, m * P:(m + 1) * P], sm[:, t, :], start=True, stop=t == 0)
                        if t:
                            mm = pe.matmul(out, s_ret[:, t - 1, m * P:(m + 1) * P], qd[:, t * P:(t + 1) * P],
                                           start=False, stop=True)
                mm.then_inc(on("ret_y"), 1)
                pe.wait_ge(on("ret_sq"), h + 1)
                for m in (0, 1):
                    mm = pe.matmul(bank(6), ones, sq2[:, m, :], start=m == 0, stop=m == 1)
                mm.then_inc(on("ret_sum"), 1)
            pe.wait_ge(on("ret_head"), RET_H)
            pe.wait_ge(on("gelu_ready"), 4)
            for u in (0, 1):
                product(S0["glu"], u, 0, 2, 4, lambda k: y_gl[:, k, :])
            pe.wait_ge(on("glu_out"), 4)
            project_out(1)
            norm(3, None)
            mlp(1)
            norm(4, None)
            for t in range(TT):
                if t >= 2:
                    pe.wait_ge(on("rows_ready"), t - 1)
                for k in range(KD):
                    mm = pe.transpose(ps[:, 4 + 2 * (t % 2) + k // 4, (k % 4) * P:(k % 4 + 1) * P],
                                      h_t[:, k, t * P:(t + 1) * P], ident)
                mm.then_inc(on("rows_turned"), 1)

        @block.vector
        def _(dve):
            own = Own(dve, on("dve_own"))
            do, go = own.do, own.go
            TTo, TS, STT = dve.tensor_tensor, dve.tensor_scalar, dve.scalar_tensor_tensor

            def norm(n, gain):
                dve.wait_ge(on("norm_sum"), n + 1)
                do(TS(rn[:], bank(7), 1.0 / D, EPS, ALU.mult, ALU.add))
                dve.sem_inc(on("norm_var"), 1)
                dve.wait_ge(on("norm_std"), n + 1)
                do(dve.reciprocal(rn[:], rn[:]))
                for k in range(KD):
                    do(STT(h_t[:, k, :], x_t[:, k, :], C(gain, k), rn[:], ALU.mult, ALU.mult))
                    dve.sem_inc(on("h_ready"), 1)

            def residual(phase):
                base = S0[phase]
                with own.loop(KD // 2, 2) as i:
                    for u in (0, 1):
                        slot, _ = slot_of(base, u)
                        dve.wait_ge(on("gemm_done"), base + u + 2 * i + 1)
                        xj = x_t[:, bass.ds(2 * i + u, 1), :].rearrange("p a b -> p (a b)")
                        do(TTo(xj, xj, bank(2 * slot), ALU.add))
                        dve.sem_inc(psum_free[slot], 1)
                        dve.sem_inc(on("x_ready"), 1)

            def mlp(layer):
                base = S0[f"up{layer}"]
                with own.loop(KF // 2, 10) as i:
                    for u in (0, 1):
                        slot, _ = slot_of(base, u)
                        dve.wait_ge(on("mlp_affine"), layer * KF + u + 2 * i + 1)
                        for tap in (1, 0):
                            sh = 2 - tap
                            for half in (0, 1):
                                dst = cg[:, slot, half, sh:T]
                                j = u + 2 * i + KF * half + tap * 2 * KF
                                go(STT(dst, bank(2 * slot + half)[:, 0:T - sh], Cd(f"fcw{layer}", j), dst,
                                       ALU.mult, ALU.add))
                            own.wait()
                        dve.sem_inc(psum_free[slot], 1)
                        dve.sem_inc(on("mlp_conv"), 1)
                        dve.wait_ge(on("mlp_gate"), layer * KF + u + 2 * i + 1)
                        hj = hid[:, bass.ds(2 * i + u, 1), :].rearrange("p a b -> p (a b)")
                        do(TTo(hj, cg[:, slot, 0, :], cg[:, slot, 1, :], ALU.mult))
                        dve.sem_inc(on("cg_read"), 1)
                        dve.sem_inc(on("hid_ready"), 1)
                residual(f"down{layer}")

            for name, free in (("pads_read", 1), ("gn_read", 1), ("cg_read", 2), ("ret_read", 1)):
                dve.sem_inc(on(name), free)
            dve.wait_ge(on("cols_in"), 16)
            dve.wait_ge(on("consts_in"), 16)
            norm(0, "mix_g0")

            def mix(dst, j, mu):
                do(TTo(dst, pad[:, j, 0:T], pad[:, j, 1:T + 1], ALU.subtract))
                do(STT(dst, dst, mu, pad[:, j, 1:T + 1], ALU.mult, ALU.add))

            dve.wait_ge(on("lora_pad"), 1)
            mix(kq, 0, C("mu", 12))
            mix(kk, 1, C("mu", 13))
            dve.sem_inc(on("lora_mixed"), 1)
            grp = lambda n, g: split(dts[:, n, g * 32:(g + 1) * 32], TT)
            dve.wait_ge(on("dt_sum"), 1)
            for g in range(SSD_G):
                do(TTo(grp(0, g), split(ps[:, 6, 0:64], TT)[:, :, 8 * g:8 * g + 8],
                       split(C("dt_bias", g * 32, 32), TT), ALU.add))
            do(STT(dts[:, 1, :], dts[:, 0, :], -1.0, dts[:, 0, :], ALU.mult, ALU.max))
            dve.sem_inc(on("dt_abs"), 1)
            dve.wait_ge(on("dt_exp"), 1)
            do(TS(dts[:, 4, :], dts[:, 1, :], 1.0, None, ALU.add))
            do(STT(dts[:, 1, :], dts[:, 4, :], -1.0, dts[:, 1, :], ALU.add, ALU.subtract))
            do(dve.reciprocal(dts[:, 4, :], dts[:, 4, :]))
            do(TTo(dts[:, 1, :], dts[:, 1, :], dts[:, 4, :], ALU.mult))
            do(TTo(dts[:, 2, :], dts[:, 2, :], dts[:, 1, :], ALU.subtract))
            do(STT(dts[:, 0, :], dts[:, 0, :], 0.0, dts[:, 2, :], ALU.max, ALU.add))
            do(STT(dts[:, 5, :], dts[:, 0, :], -1.0, dts[:, 3, :], ALU.mult, ALU.mult))
            dve.sem_inc(on("dt_rates"), 1)
            dve.wait_ge(on("acc_sum"), 1)
            do(dve.tensor_copy(dts[:, 6, :], ps[:, 6, 0:64]))
            dve.sem_inc(on("acc_ready"), 1)
            dve.wait_ge(on("acc_turn"), 1)
            do(dve.tensor_copy(acc_t[:, :], ps[0:64, 6, 0:P]))
            dve.sem_inc(on("acc_turned"), 1)
            for j in range(4):
                dve.wait_ge(on("lora_g"), j + 1)
                do(dve.tensor_copy(gate[:, j, :], bank(2 + j % 2)))
                dve.sem_inc(on("lora_g_out"), 1)
            dve.wait_ge(on("lora_w_out"), 4)

            def row(v, r):
                return v[:, bass.ds(r, 1), :].rearrange("p a b -> p (a b)")

            chunks = lambda v: split(v, NC)
            with own.loop(4, 80) as r:
                dve.wait_ge(on("rk_pad"), r + 1)
                mix(rr, 0, Cd("mu", r))
                mix(kq, 1, Cd("mu", r + 4))
                do(dve.tensor_tensor_scan(zz, K("reset"), row(sw, r), 0.0, ALU.mult, ALU.add))
                dve.sem_inc(on("log_decay"), 1)
                do(TS(kk, kq, Cd("k_k", r), None, ALU.mult))
                do(TTo(tmp, kk, kk, ALU.mult))
                dve.sem_inc(on("kk_sq"), 1)
                do(TS(bh, row(ai, r), -1.0, Cd("k_a", r), ALU.add, ALU.mult))
                do(STT(kh, bh, 1.0, kq, ALU.add, ALU.mult))
                do(STT(bt, rr, Cd("r_k", r), kh, ALU.mult, ALU.mult))
                dve.sem_inc(on("bonus_in"), 1)
                dve.wait_ge(on("v_pad"), r + 1)
                mix(vv, 2, Cd("mu", r + 8))
                dve.sem_inc(on("pads_read"), 1)
                dve.wait_ge(on("kk_sum"), r + 1)
                do(TS(rn[:], bank(4), float(N_RWKV), 1e-24, ALU.mult, ALU.max))
                dve.sem_inc(on("kk_var"), 1)
                dve.wait_ge(on("bonus_sum"), r + 1)
                do(STT(bonus, bank(5), float(N_RWKV), vv, ALU.mult, ALU.mult))
                dve.wait_ge(on("decays"), r + 1)
                do(TTo(rd, rr, pp, ALU.mult))
                do(TTo(kh, kh, ip, ALU.mult))
                dve.wait_ge(on("kk_std"), r + 1)
                do(dve.reciprocal(rn[:], rn[:]))
                do(TTo(kk, kk, rn[:], ALU.mult))
                do(TTo(bh, kk, row(ai, r), ALU.mult))
                do(TTo(bh, bh, ip, ALU.mult))
                go(TTo(chunks(zz)[:, :, 1:CH], chunks(kk)[:, :, 1:CH], chunks(pp)[:, :, 0:CH - 1], ALU.mult))
                go(dve.tensor_copy(chunks(zz)[:, :, 0:1], chunks(kk)[:, :, 0:1]))
                own.wait()
                dve.sem_inc(on("keys"), 1)
                end = chunks(pp)[:, :, CH - 1:CH].broadcast_to([P, NC, CH])
                go(TTo(chunks(bt), chunks(bh), end, ALU.mult))
                go(TTo(chunks(kt), chunks(kh), end, ALU.mult))
                go(TTo(gt, each(K("ident2"), NC), end, ALU.mult))
                own.wait()
                dve.sem_inc(on("tails"), 1)
                for hd in (0, 1):
                    dve.wait_ge(on("grams"), 2 * r + hd + 1)
                    for b, (dst, mask) in enumerate(((at_, "strict"), (bt_, "strict"), (qb_, "incl"), (qk_, "incl"))):
                        go(TTo(dst[:, 4 * hd:4 * hd + 4, :], split(bank(4 * hd + b), 4), each(K(mask), 4), ALU.mult))
                    own.wait()
                    dve.sem_inc(on("grams_out"), 1)

                def level_part(level):
                    mask = K("level")[:, level * P:(level + 1) * P]
                    go(TTo(al_, at_, each(mask, 8), ALU.mult))
                level_part(0)
                own.wait()
                do(TTo(tu, each(K("ident"), 8), al_, ALU.subtract))
                dve.sem_inc(on("al_ready"), 1)
                dve.wait_ge(on("x_done"), 6 * r + 1)
                for half in (0, 1):
                    go(TTo(tl[:, 4 * half:4 * half + 4, :], each(K("ident"), 4), split(bank(4 + half), 4),
                           ALU.subtract))
                level_part(1)
                own.wait()
                dve.sem_inc(on("al_ready"), 1)
                for level in range(1, 6):
                    dve.wait_ge(on("x_done"), 6 * r + level + 1)
                    if level < 5:
                        level_part(level + 1)
                    dve.wait_ge(on("tx_done"), 5 * r + level)
                    for half in (0, 1):
                        m = slice(4 * half, 4 * half + 4)
                        if level < 5:
                            go(TTo(tl[:, m, :], tl[:, m, :], split(bank(6 + half), 4), ALU.subtract))
                        go(TTo(tu[:, m, :], tu[:, m, :], split(bank(4 + half), 4), ALU.subtract))
                    own.wait()
                    dve.sem_inc(on("al_ready" if level < 5 else "tu_ready"), 1)
                dve.wait_ge(on("chunk_maps"), r + 1)
                go(TTo(rd, rd, bank(4), ALU.add))
                half = lambda v, q: v.rearrange("p (t q) c -> p t q c", q=2)[:, :, q, :]
                for q in (0, 1):
                    go(TTo(half(gt, q), half(gt, q), half(chunks(bank(5 + q)), q), ALU.add))
                    go(dve.tensor_copy(half(hh_, q), half(chunks(bank(7 * q)), q)))
                own.wait()
                do(dve.tensor_copy(st[:, 1, :], hh_[:, 0, :]))
                dve.sem_inc(on("state_ready"), 1)
                for c in range(1, NC - 1):
                    dve.wait_ge(on("state_moved"), (NC - 2) * r + c)
                    do(TTo(st[:, c + 1, :], hh_[:, c, :], ps[:, 1, c * 64:(c + 1) * 64], ALU.add))
                    dve.sem_inc(on("state_ready"), 1)
                dve.wait_ge(on("rwkv_y"), r + 1)
                do(dve.tensor_copy(kk, bank(2)))
                dve.sem_inc(on("gn_in"), 1)
                dve.wait_ge(on("gn_mean"), r + 1)
                do(TTo(kk, kk, bank(3), ALU.subtract))
                dve.sem_inc(on("gn_dev"), 1)
                dve.wait_ge(on("gn_sum"), r + 1)
                do(TS(rn[:], bank(0), GN_EPS, None, ALU.add))
                dve.sem_inc(on("gn_var"), 1)
                dve.sem_inc(on("gn_read"), 1)
                dve.wait_ge(on("gn_std"), r + 1)
                do(dve.reciprocal(rn[:], rn[:]))
                do(TTo(kk, kk, rn[:], ALU.mult))
                do(TS(kk, kk, Cd("ln_g", r), Cd("ln_b", r), ALU.mult, ALU.add))
                do(TTo(kk, kk, bonus, ALU.add))
                do(TTo(row(y_t, r), kk, row(gate, r), ALU.mult))
                dve.sem_inc(on("rwkv_head"), 1)

            base = S0["ssd"]
            with own.loop(SSD_G, 58) as g:
                def dt_of(n, t=None):
                    return dts[:, n, bass.ds(32 * g + (0 if t is None else 8 * t), 32 if t is None else 8)]

                def conv(u, tiles):
                    dve.wait_ge(on("ssd_affine"), 4 * g + u + 1)
                    slot, _ = slot_of(base, u)
                    for tap in (2, 1, 0):
                        sh = 3 - tap
                        for m, (dst, j) in enumerate(tiles):
                            go(STT(dst[:, sh:T], bank(2 * slot + m)[:, 0:T - sh], Cd("cw", 12 * tap + 6 * g + j),
                                   dst[:, sh:T], ALU.mult, ALU.add))
                        own.wait()
                    dve.sem_inc(psum_free[slot], 1)
                    dve.sem_inc(on("ssd_conv"), 1)

                conv(0, [(bc_f[:, 0, :], 0)])
                dve.wait_ge(on("acc_spread"), 16 * (g + 1))
                go(TTo(dte, acb[:, :, P - 1:P].rearrange("p a b -> p (a b)"), dt_of(6), ALU.subtract))
                go(TTo(seg, acb, over(dt_of(6), P), ALU.subtract))
                own.wait()
                do(TS(seg, seg, 0.0, None, ALU.min))
                dve.sem_inc(on("ssd_logs"), 1)
                conv(1, [(bc_f[:, 1, :], 1)])
                conv(2, [(xs[:, 0, :], 2), (xs[:, 1, :], 3)])
                conv(3, [(xs[:, 2, :], 4), (xs[:, 3, :], 5)])
                dve.wait_ge(on("cb_done"), g + 1)
                go(TTo(cbm, split(bank(4), TT), each(K("triu"), TT), ALU.mult))
                go(dve.tensor_copy(b_tk, split(bank(5), TT)))
                own.wait()
                dve.sem_inc(on("cb_out"), 1)
                dve.wait_ge(on("ssd_exps"), g + 1)
                do(dve.tensor_copy(cdk, acb[:, :, P - 1:P].rearrange("p a b -> p (a b)")))
                dve.wait_ge(on("xs_turned"), g + 1)
                heads = lambda v: split(v, SSD_J)
                for t in range(TT):
                    go(TTo(heads(xdt[:, t, :]), heads(bank(4 + t)), over(dt_of(0, t), 64), ALU.mult))
                own.wait()
                for t in range(TT - 1):
                    go(TTo(heads(xdd[:, t, :]), heads(xdt[:, t, :]), over(dte[:, 8 * t:8 * t + 8], 64), ALU.mult))
                own.wait()
                dve.sem_inc(on("xd_ready"), 1)
                dve.wait_ge(on("xbc_ready"), 4 * g + 2)
                for t in range(TT):
                    go(TTo(seg[:, 8 * t:8 * t + 8, :], seg[:, 8 * t:8 * t + 8, :], each(cbm[:, t, :], 8), ALU.mult))
                    go(TTo(acb[:, 8 * t:8 * t + 8, :], acb[:, 8 * t:8 * t + 8, :],
                           each(bc_f[:, 1, t * P:(t + 1) * P], 8), ALU.mult))
                own.wait()
                dve.sem_inc(on("ssd_masks"), 1)
                dve.wait_ge(on("ssd_new"), g + 1)
                do(dve.tensor_copy(s_ssd[:, 0, :], bank(4)))
                for t in (1, 2):
                    do(TTo(heads(s_ssd[:, t, :]), heads(s_ssd[:, t - 1, :]), over(cdk[:, 8 * t:8 * t + 8], 64),
                           ALU.mult))
                    do(TTo(s_ssd[:, t, :], s_ssd[:, t, :], bank(4 + t), ALU.add))
                dve.sem_inc(on("ssd_state"), 1)
                dve.wait_ge(on("ssd_y"), g + 1)
                dve.wait_ge(on("zs_ready"), 2 * g + 2)
                for i in range(4):
                    do(STT(yg[:, i, :], xs[:, i, :], Cd("ssd_d", 4 * g + i), bank(4 + i), ALU.mult, ALU.add))
                    do(TTo(yg[:, i, :], yg[:, i, :], zs[:, i, :], ALU.mult))
                    dve.sem_inc(on("yg_ready"), 1)
                dve.wait_ge(on("ssd_sum"), g + 1)
                do(TS(rn[:], bank(4), 1.0 / 512, EPS, ALU.mult, ALU.add))
                dve.sem_inc(on("ssd_var"), 1)
                dve.wait_ge(on("ssd_std"), g + 1)
                do(dve.reciprocal(rn[:], rn[:]))
                for i in range(4):
                    go(STT(y_t[:, bass.ds(4 + 4 * g + i, 1), :].rearrange("p a b -> p (a b)"), yg[:, i, :],
                           Cd("ssd_g", 4 * g + i), rn[:], ALU.mult, ALU.mult))
                own.wait()
                dve.sem_inc(on("ssd_group"), 1)

            residual("out0")
            norm(1, "ffn_g0")
            mlp(0)
            norm(2, "mix_g1")

            dve.wait_ge(on("s5_dt"), 1)
            L = lambda n: lam[:, n, :]
            mul = lambda o, p, q: do(TTo(o, p, q, ALU.mult))
            mul(L(1), C1("lam_re"), L(0))
            mul(L(2), C1("lam_im"), L(0))
            do(TS(L(5), L(2), INV_2PI, MAGIC, ALU.mult, ALU.add))
            do(TS(L(5), L(5), -MAGIC, None, ALU.add))
            for part in (PI_A, PI_B, PI_C):
                do(STT(L(2), L(5), -part, L(2), ALU.mult, ALU.add))
            do(TS(L(2), L(2), PI_MAX, -PI_MAX, ALU.min, ALU.max))
            dve.sem_inc(on("s5_angle"), 1)
            base = S0["u"]
            for u in (0, 1):
                slot, _ = slot_of(base, u)
                dve.wait_ge(on("gemm_done"), base + u + 1)
                for m in (0, 1):
                    do(dve.tensor_copy(split(u_p[:, 2 * u + m, :], S5_T),
                                       bank(2 * slot + m).rearrange("p (c s) -> p s c", s=S5_T)))
                    dve.sem_inc(on("u_ready"), 1)
                dve.sem_inc(psum_free[slot], 1)
            do(dve.memset(toep, 0.0))
            dve.sem_inc(on("toep_cleared"), 1)
            dve.wait_ge(on("s5_trig"), 1)
            mul(L(4), L(4), L(4))
            do(TS(L(4), L(4), -2.0, 1.0, ALU.mult, ALU.add))
            mul(L(6), L(1), L(4))
            mul(L(7), L(1), L(3))
            do(TS(L(8), L(6), -1.0, None, ALU.add))
            mul(L(9), C1("lam_re"), C1("lam_re"))
            mul(L(10), C1("lam_im"), C1("lam_im"))
            do(TTo(L(9), L(9), L(10), ALU.add))
            do(dve.reciprocal(L(9), L(9)))
            mul(L(10), L(8), C1("lam_re"))
            mul(L(11), L(7), C1("lam_im"))
            do(TTo(L(10), L(10), L(11), ALU.add))
            mul(L(10), L(10), L(9))
            mul(L(11), L(7), C1("lam_re"))
            mul(L(12), L(8), C1("lam_im"))
            do(TTo(L(11), L(11), L(12), ALU.subtract))
            mul(L(11), L(11), L(9))

            t_a = tmp5

            def cmul(o_re, o_im, p_re, p_im, q_re, q_im, t, neg_im=False):
                mul(o_re, p_re, q_re)
                mul(t, p_im, q_im)
                do(TTo(o_re, o_re, t, ALU.subtract))
                mul(o_im, p_re, q_im)
                mul(t, p_im, q_re)
                if neg_im:
                    do(STT(o_im, o_im, -1.0, t, ALU.mult, ALU.subtract))
                else:
                    do(TTo(o_im, o_im, t, ALU.add))

            ch16 = lambda v: split(v, S5_PAIR)
            cmul(bb[:, 0], bb[:, 1], over(L(10), 16), over(L(11), 16), ch16(C1("b_re")), ch16(C1("b_im")),
                 ch16(t_a.rearrange("p a b -> p (a b)")[:, 0:256]))
            do(dve.memset(pw[:, 0, :, 0:1], 1.0))
            do(dve.memset(pw[:, 1, :, 0:1], 0.0))
            col = lambda ri, n: pw[:, ri, :, n:n + 1].rearrange("p a b -> p (a b)")
            for n in range(1, 9):
                cmul(col(0, n), col(1, n), col(0, n - 1), col(1, n - 1), L(6), L(7), L(13))
            for s in range(S5_T):
                go(dve.tensor_copy(pwr[:, :, :, s:s + 1], pw[:, :, :, 7 - s:8 - s]))
            own.wait()
            for ri in (0, 1):
                do(dve.tensor_copy(lam[:, 14 + ri, :], col(0, 8)))
            do(TS(L(16), col(1, 8), -1.0, None, ALU.mult))
            do(dve.tensor_copy(L(17), col(1, 8)))
            for q in range(S5_PAIR):
                o_re, o_im = split(wm[:, q, :], 8), split(wm2[:, q, :], 8)
                t = split(t_a[:, q, 0:P], 8)
                b_re, b_im = each(bb[:, 0, q, :], 8), each(bb[:, 1, q, :], 8)
                p_re, p_im = over(pwr[:, 0, q, :], 16), over(pwr[:, 1, q, :], 16)
                cmul(o_re, o_im, p_re, p_im, b_re, b_im, t)
            dve.sem_inc(on("wm_ready"), 1)
            for q in range(S5_PAIR):
                o_re, o_im = split(ck[:, 0, q, :], 9), split(ck[:, 1, q, :], 9)
                t = split(t_a[:, q, :], 9)
                c_re, c_im = each(ch16(C1("c_re"))[:, q, :], 9), each(ch16(C1("c_im"))[:, q, :], 9)
                p_re, p_im = over(pw[:, 0, q, :], 16), over(pw[:, 1, q, :], 16)
                cmul(o_re, o_im, p_re, p_im, c_re, c_im, t, neg_im=True)
            dve.sem_inc(on("ck_ready"), 1)
            dve.wait_ge(on("vin_out"), 1)
            do(dve.memset(xst[:, 0, :, :], 0.0))
            do(dve.tensor_copy(xst[:, 1, :, :], vin[:, 0, :, :]))
            turn = lambda v, c: v[:, bass.ds(c, 1), :, :].rearrange("p a r q -> p (a r q)")
            keep_, cross = lam[:, 14:16, :].rearrange("p a b -> p (a b)"), lam[:, 18:20, :]
            with own.loop(S5_C - 2, 5) as c:
                x_c = xst[:, bass.ds(c + 1, 1), :, :].rearrange("p a r q -> p (a r) q")
                go(TTo(lam[:, 20:22, :].rearrange("p a b -> p (a b)"), turn(xst, c + 1), keep_, ALU.mult))
                go(TTo(cross[:, 0, :], x_c[:, 1, :], L(16), ALU.mult))
                go(TTo(cross[:, 1, :], x_c[:, 0, :], L(17), ALU.mult))
                own.wait()
                do(TTo(cross, cross, lam[:, 20:22, :], ALU.add))
                do(TTo(turn(xst, c + 2), cross.rearrange("p a b -> p (a b)"), turn(vin, c + 1), ALU.add))
            for ri in (0, 1):
                go(dve.tensor_copy(xc[:, ri, :, :], xst[:, :, ri, :].rearrange("p c q -> p q c")))
            own.wait()
            dve.sem_inc(on("s5_states"), 1)
            dve.wait_ge(on("s5_back"), 64)
            for i in range(4):
                do(STT(y_in[:, i, :], u_p[:, i, :], C("s5_d", i), y_in[:, i, :], ALU.mult, ALU.add))
                dve.sem_inc(on("s5_skip"), 1)

            base = S0["ret"]
            with own.loop(RET_H, 19) as h:
                dve.wait_ge(on("gemm_done"), base + 4 * h + 1)
                slot, _ = slot_of(base, 0)
                for m, (dst, cos, sin) in enumerate(((qr, "cosq", "sinq"), (kr, "cosk", "sink"))):
                    src = bank(2 * slot + m)
                    go(TTo(rm[0:64], src[64:128], K1(sin)[0:64], ALU.mult))
                    go(TTo(rm[64:128], src[0:64], K1(sin)[64:128], ALU.mult))
                    go(TTo(dst, src, K1(cos), ALU.mult))
                    own.wait()
                    do(TTo(dst, dst, rm, ALU.add))
                dve.sem_inc(psum_free[slot], 1)
                dve.sem_inc(on("qk_ready"), 1)
                do(TTo(split(qd, TT), split(qr, TT), each(K1d("qdec", P * h, P), TT), ALU.mult))
                dve.wait_ge(on("scores_done"), h + 1)
                do(TTo(sm, split(bank(4), TT), each(K1d("decay", P * h, P), TT), ALU.mult))
                dve.sem_inc(on("scores_ready"), 1)
                dve.wait_ge(on("ret_new"), h + 1)
                do(dve.tensor_copy(s_ret[:, 0:2, :], split(bank(6), 2)))
                do(STT(s_ret[:, 1, :], s_ret[:, 0, :], K1d("gchunk", h, 1), s_ret[:, 1, :], ALU.mult, ALU.add))
                do(STT(s_ret[:, 2, :], s_ret[:, 1, :], K1d("gchunk", h, 1), ps[:, 7, 0:DV], ALU.mult, ALU.add))
                dve.sem_inc(on("ret_state"), 1)
                dve.wait_ge(on("ret_sum"), h + 1)
                do(TS(rn[:], bank(6), 1.0 / DV, EPS, ALU.mult, ALU.add))
                dve.sem_inc(on("ret_var"), 1)
                dve.wait_ge(on("ret_std"), h + 1)
                do(dve.reciprocal(rn[:], rn[:]))
                dve.wait_ge(on("gs_ready"), h + 1)
                for m in (0, 1):
                    do(TTo(gs[:, m, :], gs[:, m, :], rn[:], ALU.mult))
                    do(TTo(y_t[:, bass.ds(4 + 2 * h + m, 1), :].rearrange("p a b -> p (a b)"), gs[:, m, :],
                           bank(4 + m), ALU.mult))
                dve.sem_inc(on("ret_read"), 1)
                dve.sem_inc(on("ret_head"), 1)
            for u in (0, 1):
                dve.wait_ge(on("glu_gate"), u + 1)
                for m in (0, 1):
                    do(TTo(y_t[:, 2 * u + m, :], y_gl[:, 2 * u + m, :], [qr, kr, qd, rm][2 * u + m], ALU.mult))
                    dve.sem_inc(on("glu_out"), 1)

            residual("out1")
            norm(3, "ffn_g1")
            mlp(1)
            norm(4, "final_g")
            for t in range(TT):
                dve.wait_ge(on("rows_turned"), t + 1)
                do(dve.tensor_copy(y_t[:, 2 * t:2 * t + 2, :], bank(4 + 2 * (t % 2), 2)))
                dve.sem_inc(on("rows_ready"), 1)


def tiles_of(w, order):
    k, n = w.shape
    t = w.reshape(k // P, P, n // P, P).transpose(2, 1, 0, 3)
    width = max(len(o) for o in order) * (k // P) * P
    out = np.zeros((len(order), P, width), w.dtype)
    for s, o in enumerate(order):
        part = t[list(o)].transpose(1, 0, 2, 3).reshape(P, -1)
        out[s, :, :part.shape[1]] = part
    return out


def feature_cols(v):
    return v.reshape(-1, P).T


def per_pair(v):
    v = v.reshape(S5_PAIR, 2, S5_N, -1).transpose(1, 2, 0, 3)
    return v.reshape(P, -1)


def kernel(**inputs):
    import concourse.bacc as bacc
    from concourse.bass_utils import run_bass_kernel_spmd

    v = {k: np.asarray(x) for k, x in inputs.items()}
    w_in = v["l0_w_in"]
    con0, con1_ = constants()
    order12 = [8, 10, 0, 1, 2, 3, 9, 11, 4, 5, 6, 7]
    per_head = lambda x: np.tile(x.reshape(SSD_G, 1, SSD_J), (P, 1, TT, 1)).reshape(P, 64)
    c0 = {
        "mix_g0": feature_cols(v["l0_norm_mix"]), "mu": feature_cols(v["l0_rwkv_mu"]),
        "w0": feature_cols(v["l0_rwkv_w0"]), "a0": feature_cols(v["l0_rwkv_a0"]),
        "k_k": feature_cols(v["l0_rwkv_k_k"]), "k_a": feature_cols(v["l0_rwkv_k_a"]),
        "r_k": feature_cols(v["l0_rwkv_r_k"].reshape(-1)), "ln_g": feature_cols(v["l0_rwkv_ln_g"]),
        "ln_b": feature_cols(v["l0_rwkv_ln_b"]),
        "cw": np.concatenate([feature_cols(w)[:, order12] for w in v["l0_ssd_conv_w"]], axis=1),
        "cb": feature_cols(v["l0_ssd_conv_b"])[:, order12],
        "dt_bias": per_head(v["l0_ssd_dt_bias"]), "a_log": per_head(v["l0_ssd_a_log"]),
        "w_dt": w_in[:, 4352:4368].reshape(KD, P, 16).transpose(1, 0, 2).reshape(P, -1),
        "ssd_d": feature_cols(np.repeat(v["l0_ssd_d"], SSD_P)), "ssd_g": feature_cols(v["l0_ssd_norm_g"]),
        "ffn_g0": feature_cols(v["l0_norm_ffn"]),
        "fcw0": np.concatenate([feature_cols(w) for w in v["l0_ffn_conv_w"]], axis=1),
        "fcb0": feature_cols(v["l0_ffn_conv_b"]), "mix_g1": feature_cols(v["l1_norm_mix"]),
        "s5_d": feature_cols(v["l1_s5_d"]), "b_glu": feature_cols(v["l1_s5_b_glu"]),
        "ffn_g1": feature_cols(v["l1_norm_ffn"]),
        "fcw1": np.concatenate([feature_cols(w) for w in v["l1_ffn_conv_w"]], axis=1),
        "fcb1": feature_cols(v["l1_ffn_conv_b"]), "final_g": feature_cols(v["final_norm"]),
    }
    c1 = {
        "lam_re": per_pair(v["l1_s5_lam_re"]), "lam_im": per_pair(v["l1_s5_lam_im"]),
        "log_dt": per_pair(np.repeat(v["l1_s5_log_dt"][:, None], S5_N, axis=1)),
        "b_re": per_pair(v["l1_s5_b_re"]), "b_im": per_pair(v["l1_s5_b_im"]),
        "c_re": per_pair(v["l1_s5_c_re"].transpose(0, 2, 1)), "c_im": per_pair(v["l1_s5_c_im"].transpose(0, 2, 1)),
    }
    ssd = []
    for g in range(SSD_G):
        o = order12[6 * g:6 * g + 6]
        ssd += [[22 + o[0]], [22 + o[1]], [22 + o[2], 22 + o[3]], [22 + o[4], 22 + o[5]]]
        ssd += [[14 + 4 * g, 15 + 4 * g], [16 + 4 * g, 17 + 4 * g]]
    ret = []
    for h in range(RET_H):
        ret += [[4 + h, 8 + h], [12 + 2 * h], [13 + 2 * h], [20 + 2 * h, 21 + 2 * h]]
    main = w_in[:, :4352]
    alone = [[j] for j in range(KD)]
    gates = [[j, KF + j] for j in range(KF)]
    arrays = {
        "x": v["x"], "con0": con0, "con1": con1_,
        "col0": np.concatenate([c0[n] for n, _ in COLS0], axis=1),
        "col1": np.concatenate([c1[n] for n, _ in COLS1], axis=1),
        "w2": v["l0_rwkv_w2"].reshape(64, 4, P), "a2": v["l0_rwkv_a2"].reshape(64, 4, P),
        "g2": v["l0_rwkv_g2"].reshape(P, 4, P),
        "w_lora": tiles_of(main, [[12, 13]]),
        "w_rwkv": tiles_of(main, [o for r in range(4) for o in ([r, 4 + r], [8 + r])]),
        "w_ssd": tiles_of(main, ssd),
        "w_out0": tiles_of(v["l0_w_out"], alone), "w_up0": tiles_of(v["l0_ffn_up"], gates),
        "w_down0": tiles_of(v["l0_ffn_down"], alone),
        "w_u": tiles_of(v["l1_w_in"], [[0, 1], [2, 3]]), "w_ret": tiles_of(v["l1_w_in"], ret),
        "w_glu": tiles_of(v["l1_s5_w_glu"], [[0, 1], [2, 3]]),
        "w_out1": tiles_of(v["l1_w_out"], alone), "w_up1": tiles_of(v["l1_ffn_up"], gates),
        "w_down1": tiles_of(v["l1_ffn_down"], alone),
    }
    arrays = {f"in_{k}": np.ascontiguousarray(x) for k, x in arrays.items()}
    nc = bacc.Bacc("TRN2", target_bir_lowering=False, num_devices=1)
    a = {k[3:]: nc.dram_tensor(k, x.shape, F32, kind="ExternalInput").ap() for k, x in arrays.items()}
    a["out"] = nc.dram_tensor("out_0", (1, T, D), F32, kind="ExternalOutput").ap()
    trunk(nc, a)
    r = run_bass_kernel_spmd(nc, [arrays], core_ids=[0])
    return r.results[0]["out_0"]
```

```python
from contextlib import ExitStack, contextmanager

import numpy as np

import concourse.bass as bass
from concourse import mybir

F32 = mybir.dt.float32
F32R = mybir.dt.float32r
ACT = mybir.ActivationFunctionType
ALU = mybir.AluOpType

P = 128
T = 512
D = 1024
KD = D // P
TT = T // P
EPS = 1e-6
SOFT = float(np.exp(-0.5))

H_RWKV, N_RWKV, CH = 8, 64, 64
NC = T // CH
GN_EPS = 64e-5
SSD_G, SSD_J, SSD_P = 2, 8, 64
S5_G, S5_CH, S5_N, S5_T = 32, 16, 64, 8
S5_C = T // S5_T
S5_PAIR = S5_G // 2
RET_H, DK, DV = 4, 128, 256
FH = 2816
KF = FH // P
KO = 12
SLOT = 16 * P
KH = (12, 10)

MAGIC = 12582912.0
INV_2PI = float(1.0 / (2.0 * np.pi))
PI_A = 6.28125
PI_B = float(np.float32(2.0 * np.pi - 6.28125))
PI_C = float(2.0 * np.pi - 6.28125 - float(np.float32(2.0 * np.pi - 6.28125)))
PI_MAX = 3.1415925

COLS0 = [("mix_g0", KD), ("mu", 14), ("w0", 4), ("a0", 4), ("k_k", 4), ("k_a", 4), ("r_k", 4), ("ln_g", 4),
         ("ln_b", 4), ("cw", 4 * 12), ("cb", 12), ("dt_bias", 64), ("a_log", 64), ("w_dt", 128), ("ssd_d", 8), ("ssd_g", 8),
         ("ffn_g0", KD), ("fcw0", 3 * 2 * KF), ("fcb0", 2 * KF), ("mix_g1", KD), ("s5_d", 4), ("b_glu", 4),
         ("ffn_g1", KD), ("fcw1", 3 * 2 * KF), ("fcb1", 2 * KF), ("final_g", KD)]
COLS1 = [("lam_re", 16), ("lam_im", 16), ("log_dt", 16), ("b_re", 256), ("b_im", 256), ("c_re", 256),
         ("c_im", 256)]
CONST = [("ident", P), ("ones", P), ("eps", 1), ("gn_eps", 1)]
CONST0 = [("bones", P), ("triu", P), ("strict", P), ("incl", P), ("level", 6 * P), ("ident2", 64), ("reset", T)]
CONST1 = [("cosq", T), ("sinq", T), ("cosk", T), ("sink", T), ("decay", RET_H * P), ("qdec", RET_H * P),
          ("kdec", RET_H), ("gchunk", RET_H)]


def offsets(parts):
    at, out = 0, {}
    for name, n in parts:
        out[name] = (at, n)
        at += n
    return out, at


O_COL0, N_COL0 = offsets(COLS0)
O_COL1, N_COL1 = offsets(COLS1)
O_CON, N_CON = offsets(CONST)
O_CON0, N_CON0 = offsets(CONST0)
O_CON1, N_CON1 = offsets(CONST1)


def constants():
    r = np.arange(P)
    s, t = r[:, None], r[None, :]
    same = (s // CH) == (t // CH)
    c = {
        "ident": np.eye(P), "ones": np.ones((P, P)), "eps": np.full((P, 1), EPS), "gn_eps": np.full((P, 1), GN_EPS), "bones": np.where(same, 1.0 / CH, 0.0),
        "triu": (s <= t), "strict": same & (s < t), "incl": same & (s <= t),
        "ident2": np.tile(np.eye(CH), (2, 1)),
        "reset": np.tile((np.arange(T) % CH != 0)[None, :], (P, 1)),
    }
    c["level"] = np.concatenate(
        [(s // (2 << l) == t // (2 << l)) & (s % (2 << l) < (1 << l)) & (t % (2 << l) >= (1 << l))
         for l in range(6)], axis=1)
    half = DK // 2
    theta = (1.0 / (10000.0 ** np.linspace(0.0, 1.0, half))).astype(np.float32)
    ang = (np.arange(T, dtype=np.float32)[None, :] * theta[:, None]).astype(np.float64)
    cos, sin = np.cos(ang), np.sin(ang)
    c["cosq"] = np.concatenate([cos, cos])
    c["sinq"] = np.concatenate([-sin, sin])
    c["cosk"], c["sink"] = c["cosq"] * DK ** -0.5, c["sinq"] * DK ** -0.5
    lg = np.log(1.0 - 2.0 ** (-5.0 - np.arange(RET_H)))
    c["decay"] = np.concatenate([np.where(s <= t, np.exp(np.maximum(t - s, 0) * g), 0.0) for g in lg], axis=1)
    c["qdec"] = np.concatenate([np.tile(np.exp((r + 1.0) * g)[None, :], (P, 1)) for g in lg], axis=1)
    c["kdec"] = np.stack([np.exp((P - 1.0 - r) * g) for g in lg], axis=1)
    c["gchunk"] = np.tile(np.exp(P * lg)[None, :], (P, 1))
    pack = lambda parts: np.concatenate([np.asarray(c[n], np.float32) for n, _ in parts], axis=1)
    return pack(CONST), pack(CONST0), pack(CONST1)


class Own:

    def __init__(self, eng, sem):
        self.eng, self.sem, self.base, self.k, self.i, self.per = eng, sem, 0, 0, None, 0

    def count(self):
        return self.base + self.k if self.i is None else self.base + self.per * self.i + self.k

    def go(self, ins):
        ins.then_inc(self.sem, 1)
        self.k += 1

    def wait(self):
        self.eng.wait_ge(self.sem, self.count())

    def do(self, ins):
        self.go(ins)
        self.wait()

    @contextmanager
    def loop(self, trips, per, start=0):
        self.base, self.k, self.per = self.base + self.k, 0, per
        with self.eng.Fori(start, start + trips) as i:
            self.i = i - start if start else i
            yield i
        assert self.k == per, f"the loop signals {self.k} results a turn, not {per}"
        self.base, self.k, self.i = self.base + per * trips, 0, None


STEPS = [("lora", 1), ("rwkv", 16), ("ssd", 8), ("out0", 8),
         ("up0a", 2 * KH[0]), ("down0a", 8), ("up0b", 2 * KH[1]), ("down0b", 8), ("u", 2), ("ret", 16), ("glu", 2),
         ("out1", 8), ("up1a", 2 * KH[0]), ("down1a", 8), ("up1b", 2 * KH[1]), ("down1b", 8)]
O_STEP, N_STEP = offsets(STEPS)
S0 = {k: v[0] for k, v in O_STEP.items()}
SPLIT_STEPS = KD + 2 * KF + 2 * KD


def slot_of(base, u, i=0, stride=2):
    return (base + u) % 2, (base + u) // 2 + stride // 2 * i


def mlp_bank(base, u):
    return 2 * ((base + u) % 2) + u // 2 % 2


def pieces_before(step):
    return sum(max(0, min(SPLIT_STEPS, step - S0[f"out{layer}"])) for layer in (0, 1))


def trunk(nc, a):
    ctx = ExitStack()
    with ctx:
        def sb(name, shape):
            return ctx.enter_context(nc.sbuf_tensor(name, shape, F32))

        def sem(name):
            return ctx.enter_context(nc.semaphore(name))

        x_t = sb("x_t", [P, KD, T])
        h_t = sb("h_t", [P, KD, T])
        wslot = sb("wslot", [P, 2, SLOT])
        col0 = sb("col0", [P, N_COL0])
        con = sb("con", [P, N_CON])
        rn = sb("rn", [P, T])
        spare = sb("spare", [P, 1])
        N_UP = 12368
        upper = sb("upper", [P, N_UP])
        ps = ctx.enter_context(nc.psum_tensor("ps", [P, 8, 512], F32))
        mixers, mlps = ExitStack(), ExitStack()
        with mixers:
            y_t = mixers.enter_context(nc.sbuf_tensor("y_t", [P, KO, T], F32))
            con0 = mixers.enter_context(nc.sbuf_tensor("con0", [P, N_CON0], F32))
            dts = mixers.enter_context(nc.sbuf_tensor("dts", [P, 8, 64], F32))
            acc_t = mixers.enter_context(nc.sbuf_tensor("acc_t", [64, P], F32))
            N_LOW = 16600
            lower = mixers.enter_context(nc.sbuf_tensor("lower", [P, N_LOW], F32))
        with mlps:
            h_s = mlps.enter_context(nc.sbuf_tensor("h_s", [P, 2, KD, T], F32R))
            hid_s = mlps.enter_context(nc.sbuf_tensor("hid_s", [P, 2, KH[0], T], F32R))
            w_s = mlps.enter_context(nc.sbuf_tensor("w_s", [P, 2, 2, KH[0] * P], F32R))
        cg = h_t[:, 0:4, :].rearrange("p (a b) c -> p a b c", a=2)

        def C(name, j=0, n=1):
            return col0[:, O_COL0[name][0] + j:O_COL0[name][0] + j + n]

        def Cd(name, j):
            return col0[:, bass.ds(O_COL0[name][0] + j, 1)]

        def K(name):
            o, n = O_CON[name] if name in O_CON else O_CON0[name]
            return (con if name in O_CON else con0)[:, o:o + n]

        def split_of(v):
            return v.rearrange("p (a b) -> p a b", a=4)

        def carver(*rooms):
            at = [0] * len(rooms)

            def take(*dims):
                n = int(np.prod(dims))
                r = next(r for r, (_, size) in enumerate(rooms) if at[r] + n <= size)
                v = rooms[r][0][:, at[r]:at[r] + n]
                at[r] += n
                if len(dims) == 2:
                    v = v.rearrange("p (a b) -> p a b", a=dims[0])
                if len(dims) == 3:
                    v = v.rearrange("p (a b c) -> p a b c", a=dims[0], b=dims[1])
                return v
            return take

        take = carver((lower, N_LOW), (upper, N_UP))
        sw, ai, gate = take(4, T), take(4, T), take(4, T)
        pad = take(3, T + 1)
        rr, kq, vv, kk, pp, ip, bh, kh, zz, rd, bt, kt, bonus, tmp = (take(T) for _ in range(14))
        v_tok, b_tok, k_tok = (take(TT, P) for _ in range(3))
        at_, bt_, qb_, qk_, al_, tl, tu, xx = (take(8, P) for _ in range(8))
        rh, wn = take(8, P), take(8, P)
        gt, hh_, st = take(NC, 64), take(NC, 64), take(NC, 64)

        take = carver((lower, N_LOW), (upper, N_UP))
        xs = take(4, T)
        bc_f = take(2, T)
        acb, seg = take(32, P), take(32, P)
        xdt, xdd = take(TT, 512), take(TT, 512)
        b_tk, cbm = take(TT, P), take(TT, P)
        s_ssd = take(3, 512)
        yg = take(4, T)
        dte, cdk = take(32), take(32)

        take = carver((lower, N_LOW))
        con1 = take(N_CON1)
        toep = take(S5_G, P)
        uc = take(S5_G, S5_C)
        u_p = take(4, T)
        gs, sq2 = take(2, T), take(2, T)
        qr, kr, qd, rm = (take(T) for _ in range(4))
        sm, k_tk = take(TT, P), take(TT, P)
        flat = toep.rearrange("p a b -> p (a b)")
        y_gl, y_in = split_of(flat[:, 0:4 * T]), split_of(uc.rearrange("p a b -> p (a b)"))
        take = carver((upper, N_UP))
        col1 = take(N_COL1)
        v_tk = split_of(col1[:, 0:TT * DV])
        lam = take(24, 16)
        pw = take(2, S5_PAIR, 9)
        pwr = take(2, S5_PAIR, 8)
        bb = take(2, S5_PAIR, 16)
        ck = take(2, S5_PAIR, 144)
        wms = take(2 * S5_PAIR, P)
        wm, wm2, kker = wms[:, 0:S5_PAIR, :], wms[:, S5_PAIR:, :], wms
        s5_tmp = take(1152)
        s_ret = s5_tmp[:, 0:3 * DV].rearrange("p (a b) -> p a b", a=3)
        k_flat = wms.rearrange("p a b -> p (a b)")
        vin, xst = (k_flat[:, o:o + 2048].rearrange("p (c r q) -> p c r q", c=S5_C, r=2) for o in (0, 2048))
        xc = k_flat[:, 0:2048].rearrange("p (r a b) -> p r a b", r=2, a=S5_PAIR)
        yc = k_flat[:, 2048:4096].rearrange("p (g c) -> p g c", g=S5_G)
        y_ext = y_t[:, :, :].rearrange("p a b -> p (a b)")
        wt_r = y_ext[:, 0:S5_PAIR * P].rearrange("p (a b) -> p a b", a=S5_PAIR)
        wt_i = y_ext[:, 8 * T:8 * T + S5_PAIR * P].rearrange("p (a b) -> p a b", a=S5_PAIR)

        def K1(name, j=0, n=None):
            o, m = O_CON1[name]
            return con1[:, o + j:o + j + (m if n is None else n)]

        def K1d(name, j, n):
            return con1[:, bass.ds(O_CON1[name][0] + j, n)]

        def C1(name):
            o, n = O_COL1[name]
            return col1[:, o:o + n]

        x_in = h_t[:, :, :].rearrange("p a b -> p (a b)").rearrange("p (t d) -> p t d", t=TT)
        d_acc = nc.dram_tensor("d_acc", [64, P], F32, kind="Internal").ap()
        d_u = nc.dram_tensor("d_u", [512, 8, 64], F32, kind="Internal").ap()
        d_y = nc.dram_tensor("d_y", [512, 8, 64], F32, kind="Internal").ap()

        semaphores = {}

        def on(name):
            if name not in semaphores:
                semaphores[name] = ctx.enter_context(nc.semaphore(name))
            return semaphores[name]

        w_landed = [on("w_landed_0"), on("w_landed_1")]
        psum_free = [on("psum_free_0"), on("psum_free_1")]

        def bank(n, m=1):
            return ps[:, n, :] if m == 1 else ps[:, n:n + m, :]

        def split(v, n):
            return v.rearrange("p (a b) -> p a b", a=n)

        def over(v, n):
            return v.unsqueeze(2).broadcast_to([v.shape[0], v.shape[1], n])

        def each(v, n):
            return v.unsqueeze(1).broadcast_to([v.shape[0], n, v.shape[1]])

        block = ctx.enter_context(nc.Block())

        @block.sync
        def _(sp):
            sp.dma_start(x_in, a["x"].rearrange("b (t p) d -> p (b t) d", p=P)).then_inc(on("x_loaded"), 16)
            sp.dma_start(con[:], a["con"]).then_inc(on("consts_in"), 16)
            sp.dma_start(con0[:], a["con0"]).then_inc(on("consts0_in"), 16)
            sp.dma_start(col0[:], a["col0"]).then_inc(on("cols_in"), 16)

            def load(src, n, step, slot, first):
                if first in range(S0["out0"] + 2, S0["u"] + 2) or first >= S0["out1"] + 2:
                    sp.wait_ge(on("w_split"), step - first + pieces_before(first - 2) + 1)
                elif first >= 2:
                    sp.wait_ge(on("gemm_done"), step - 1)
                sp.dma_start(wslot[:, slot, 0:n], src).then_inc(w_landed[slot], 16)

            def stream(name, phase, n, skip=0):
                w, base, count = a[name], S0[phase], O_STEP[phase][1]
                u = 0
                while u < count and (u < 2 or (count - u) % 2):
                    load(w[skip + u], n, base + u, (base + u) % 2, base + u)
                    u += 1
                if count == u:
                    return
                with sp.Fori(0, (count - u) // 2) as i:
                    for v in (u, u + 1):
                        load(w[bass.ds(2 * i + v + skip, 1)].rearrange("a p n -> p (a n)"), n, base + v + 2 * i,
                             (base + v) % 2, base + v)

            def mlp(layer):
                for part, kh in enumerate(KH):
                    stream(f"w_up{layer}", f"up{layer}{'ab'[part]}", KD * P, 2 * KH[0] * part)
                    stream(f"w_down{layer}{'ab'[part]}", f"down{layer}{'ab'[part]}", kh * P)

            for name, phase, n in (("w_lora", "lora", 2048), ("w_rwkv", "rwkv", 2048), ("w_ssd", "ssd", 2048),
                                   ("w_out0", "out0", KO * P)):
                stream(name, phase, n)
            mlp(0)
            for name, phase, n in (("w_u", "u", 2048), ("w_ret", "ret", 2048), ("w_glu", "glu", 1024),
                                   ("w_out1", "out1", KO * P)):
                stream(name, phase, n)
            mlp(1)
            for t in range(TT):
                sp.wait_ge(on("rows_ready"), t + 1)
                sp.dma_start(a["out"].rearrange("b (t p) d -> (b t) p d", p=P)[t],
                             y_t[:, 2 * t:2 * t + 2, :].rearrange("p a b -> p (a b)")).then_inc(on("stored"), 16)
            sp.wait_ge(on("stored"), 16 * TT)

        @block.gpsimd
        def _(pool):
            own = Own(pool, on("pool_own"))
            pool.dma_start(at_[0:64, 0:4, :], a["w2"]).then_inc(on("lora_in"), 16)
            pool.dma_start(at_[64:128, 0:4, :], a["a2"]).then_inc(on("lora_in"), 16)
            pool.dma_start(bt_[:, 0:4, :], a["g2"]).then_inc(on("lora_in"), 16)
            pool.wait_ge(on("acc_turned"), 1)
            pool.dma_start(d_acc, acc_t[:, :]).then_inc(on("acc_stored"), 16)
            pool.wait_ge(on("acc_stored"), 16)
            for g in range(SSD_G):
                if g == 0:
                    pool.wait_ge(on("rwkv_head"), 4)
                else:
                    pool.wait_ge(on("ssd_group"), g)
                pool.dma_start(acb, d_acc[g * 32:(g + 1) * 32].unsqueeze(0).broadcast_to([P, 32, P]))\
                    .then_inc(on("acc_spread"), 16)
            pool.wait_ge(on("ssd_group"), SSD_G)
            pool.dma_start(col1, a["col1"]).then_inc(on("cols1_in"), 16)

            def split_weights(phase, kt):
                base, n = S0[phase], kt * P
                with own.loop(O_STEP[phase][1] // 2, 2) as i:
                    for u in (0, 1):
                        slot, _ = slot_of(base, u, i)
                        pool.wait_ge(on("w_high"), pieces_before(base) + u + 2 * i + 1)
                        own.do(pool.tensor_tensor(w_s[:, slot, 1, 0:n], wslot[:, slot, 0:n],
                                                  w_s[:, slot, 0, 0:n].bitcast(F32), ALU.subtract))
                        pool.sem_inc(on("w_split"), 1)

            def split_layer(layer):
                split_weights(f"out{layer}", KO)
                for part, kh in enumerate(KH):
                    split_weights(f"up{layer}{'ab'[part]}", KD)
                    split_weights(f"down{layer}{'ab'[part]}", kh)

            split_layer(0)
            TTo = pool.tensor_tensor
            pool.wait_ge(on("gemm_done"), S0["u"])
            pool.dma_start(con1, a["con1"]).then_inc(on("consts1_in"), 16)
            own.do(pool.memset(toep, 0.0))
            pool.wait_ge(on("u_ready"), 4)
            for i in range(4):
                pool.dma_start(d_u[i * P:(i + 1) * P].rearrange("p s c -> p (s c)"), u_p[:, i, :])\
                    .then_inc(on("u_stored"), 16)
            pool.wait_ge(on("u_stored"), 64)
            for s in range(S5_T):
                pool.dma_start(uc[s * 16:(s + 1) * 16, :, :],
                               d_u[:, s, :].rearrange("(g c) k -> c g k", c=16)).then_inc(on("u_spread"), 16)
            pool.wait_ge(on("kernels_out"), 2)
            for s in range(S5_T):
                pool.dma_start(toep[s * 16:(s + 1) * 16, :, s * 16:P], kker[0:16, :, 0:P - s * 16])\
                    .then_inc(on("kernels_spread"), 16)

            pool.wait_ge(on("vin_out"), 1)
            own.do(pool.memset(xst[:, 0, :, :], 0.0))
            own.do(pool.tensor_copy(xst[:, 1, :, :], vin[:, 0, :, :]))
            turn = lambda v, c: v[:, bass.ds(c, 1), :, :].rearrange("p a r q -> p (a r q)")
            keep_, cross = lam[:, 14:16, :].rearrange("p a b -> p (a b)"), lam[:, 18:20, :]
            with own.loop(S5_C - 2, 5) as c:
                x_c = xst[:, bass.ds(c + 1, 1), :, :].rearrange("p a r q -> p (a r) q")
                own.go(TTo(lam[:, 20:22, :].rearrange("p a b -> p (a b)"), turn(xst, c + 1), keep_, ALU.mult))
                own.go(TTo(cross[:, 0, :], x_c[:, 1, :], lam[:, 16, :], ALU.mult))
                own.go(TTo(cross[:, 1, :], x_c[:, 0, :], lam[:, 17, :], ALU.mult))
                own.wait()
                own.do(TTo(cross, cross, lam[:, 20:22, :], ALU.add))
                own.do(TTo(turn(xst, c + 2), cross.rearrange("p a b -> p (a b)"), turn(vin, c + 1), ALU.add))
            for ri in (0, 1):
                own.go(pool.tensor_copy(xc[:, ri, :, :], xst[:, :, ri, :].rearrange("p c q -> p q c")))
            own.wait()
            pool.sem_inc(on("s5_states"), 1)
            pool.wait_ge(on("s5_out"), 4)
            for t in range(S5_T):
                pool.dma_start(d_y[:, t, :].rearrange("(g c) k -> c g k", c=16), yc[t * 16:(t + 1) * 16, :, :])\
                    .then_inc(on("s5_stored"), 16)
            pool.wait_ge(on("s5_stored"), 16 * S5_T)
            for i in range(4):
                pool.dma_start(y_in[:, i, :], d_y[i * P:(i + 1) * P].rearrange("p s c -> p (s c)"))\
                    .then_inc(on("s5_back"), 16)
            pool.wait_ge(on("s5_back"), 64)
            pool.wait_ge(on("ret_head"), RET_H)
            pool.wait_ge(on("glu_out"), 4)
            split_layer(1)

        @block.scalar
        def _(act):
            own = Own(act, on("act_own"))

            def tables_of(function):
                own.do(act.activation(spare[:], K("eps"), function))

            def root(summed, n, src, scale, eps, read, done):
                tables_of(ACT.Ln)
                act.wait_ge(on(summed), n)
                own.do(act.activation(rn[:], src, ACT.Ln, scale=scale, bias=K(eps)))
                if read:
                    act.sem_inc(on(read), 1)
                own.do(act.activation(rn[:], rn[:], ACT.Exp, scale=-0.5))
                act.sem_inc(on(done), 1)

            def norm(n, between=None):
                for k in range(KD):
                    act.wait_ge(on("x_ready"), KD * n + k + 1)
                    own.go(act.activation(h_t[:, k, :], x_t[:, k, :], ACT.Square))
                    own.wait()
                    act.sem_inc(on("squares"), 1)
                if between:
                    between()
                root("norm_sum", n + 1, bank(7), 1.0 / D, "eps", "norm_read", "norm_root")

            def high(phase, u, i=0, stride=2):
                base, n = S0[phase], (KD if "up" in phase else KH["b" in phase]) * P
                slot, before = slot_of(base, u, i, stride)
                act.wait_ge(w_landed[slot], 16 * (before + 1))
                act.wait_ge(on("gemm_done"), base + u + stride * i - 1)
                own.do(act.activation(w_s[:, slot, 0, 0:n], wslot[:, slot, 0:n], ACT.Copy))
                act.sem_inc(on("w_high"), 1)

            def norm_split(n, phase):
                norm(n, lambda: [high(phase, u) for u in (0, 1)])
                for k in range(KD):
                    act.wait_ge(on("h_whole"), KD * (n // 2) + k + 1)
                    own.do(act.activation(h_s[:, 0, k, :], h_t[:, k, :], ACT.Copy))
                    act.sem_inc(on("h_high"), 1)

            def up(layer, part):
                phase, down = (f"{name}{layer}{'ab'[part]}" for name in ("up", "down"))
                base, first = S0[phase], KH[0] * part

                def turn(i, last):
                    for v in (0, 1):
                        pair = layer * KF + first + v + 2 * i
                        for u in (0, 1):
                            if last and v:
                                high(down, u)
                            else:
                                high(phase, 2 * v + 2 + u, i, 4)
                        act.wait_ge(on("cg_read"), pair + 1)
                        for half in (0, 1):
                            j = first + v + 2 * i + KF * half
                            own.go(act.activation(cg[:, v, half, :], bank(mlp_bank(base, 2 * v + half)), ACT.Identity,
                                                  scale=Cd(f"fcw{layer}", j + 2 * 2 * KF), bias=Cd(f"fcb{layer}", j)))
                        own.wait()
                        act.sem_inc(on("mlp_affine"), 1)
                        act.wait_ge(on("mlp_conv"), pair + 1)
                        own.do(act.activation(cg[:, v, 0, :], cg[:, v, 0, :], ACT.Silu))
                        act.sem_inc(on("mlp_gate"), 1)

                tables_of(ACT.Silu)
                with own.loop(KH[part] // 2 - 1, 10) as i:
                    turn(i, False)
                turn(KH[part] // 2 - 1, True)

            def highs(phase):
                with own.loop(KD // 2 - 1, 2) as i:
                    for u in (2, 3):
                        high(phase, u, i)

            def down(layer, part):
                highs(f"down{layer}{'ab'[part]}")
                if part == 0:
                    for u in (0, 1):
                        high(f"up{layer}b", u)

            def project_out(layer):
                for u in (0, 1):
                    high(f"out{layer}", u)
                for k in range(KO):
                    own.do(act.activation(hid_s[:, 0, k, :], y_t[:, k, :], ACT.Copy))
                    act.sem_inc(on("y_high"), 1)
                highs(f"out{layer}")

            act.wait_ge(on("consts_in"), 16)
            act.wait_ge(on("x_turned"), 1)
            for k in range(KD):
                own.do(act.activation(x_t[:, k, :], bank(k), ACT.Copy))
                act.sem_inc(on("x_ready"), 1)
            norm(0)
            act.wait_ge(on("cols_in"), 16)

            for j in range(3):
                own.do(act.activation(pad[:, j, 0:1], col0[:, 0:1], ACT.Copy, scale=0.0))
            act.wait_ge(on("gemm_done"), 1)
            for j in (0, 1):
                own.do(act.activation(pad[:, j, 1:T + 1], bank(j), ACT.Copy))
            act.sem_inc(psum_free[0], 1)
            act.sem_inc(on("lora_pad"), 1)
            act.wait_ge(on("lora_mixed"), 1)
            own.do(act.activation(rr[0:64], kq[0:64], ACT.Tanh))
            own.do(act.activation(rr[64:128], kq[64:128], ACT.Copy))
            own.do(act.activation(vv[:], kk[:], ACT.Sigmoid))
            act.sem_inc(on("lora_acts"), 1)
            act.wait_ge(on("dt_abs"), 1)
            own.do(act.activation(dts[:, 1, :], dts[:, 1, :], ACT.Exp, scale=-1.0))
            own.do(act.activation(dts[:, 2, :], dts[:, 1, :], ACT.Ln, bias=1.0))
            own.do(act.activation(dts[:, 3, :], C("a_log", 0, 64), ACT.Exp))
            act.sem_inc(on("dt_exp"), 1)

            for j in range(4):
                act.wait_ge(on("lora_w"), j + 1)
                own.do(act.activation(sw[:, j, :], bank(2 * (j % 2) + 4), ACT.Sigmoid, bias=C("w0", j)))
                own.do(act.activation(ai[:, j, :], bank(2 * (j % 2) + 5), ACT.Sigmoid, bias=C("a0", j)))
                act.sem_inc(on("lora_w_out"), 1)

            base = S0["rwkv"]
            with own.loop(4, 32) as r:
                act.wait_ge(on("gemm_done"), base + 4 * r + 1)
                act.wait_ge(on("pads_read"), r + 1)
                for j in (0, 1):
                    own.do(act.activation(pad[:, j, 1:T + 1], bank(2 + j), ACT.Copy))
                act.sem_inc(psum_free[1], 1)
                act.sem_inc(on("rk_pad"), 1)
                act.wait_ge(on("gemm_done"), base + 4 * r + 2)
                own.do(act.activation(pad[:, 2, 1:T + 1], bank(0), ACT.Copy))
                act.sem_inc(psum_free[0], 1)
                act.sem_inc(on("v_pad"), 1)
                act.wait_ge(on("log_decay"), r + 1)
                own.do(act.activation(pp[:], zz[:], ACT.Exp, scale=-SOFT))
                own.do(act.activation(ip[:], zz[:], ACT.Exp, scale=SOFT))
                act.sem_inc(on("decays"), 1)
                tables_of(ACT.Ln)
                act.wait_ge(on("kk_var"), r + 1)
                own.do(act.activation(rn[:], rn[:], ACT.Ln))
                own.do(act.activation(rn[:], rn[:], ACT.Exp, scale=-0.5))
                act.sem_inc(on("kk_root"), 1)
                for v, par in ((0, 1), (1, 0)):
                    act.wait_ge(on("gemm_done"), base + 4 * r + 3 + v)
                    own.do(act.activation(y_t[:, bass.ds(4 + 2 * r + v, 1), :].rearrange("p a b -> p (a b)"),
                                          bank(2 * par), ACT.Silu))
                    act.sem_inc(psum_free[par], 1)
                    act.sem_inc(on("z_out"), 1)
                act.wait_ge(on("tok_turned"), r + 1)
                for hd in (0, 1):
                    own.do(act.activation(rh[:, 4 * hd:4 * hd + 4, 0:64],
                                          split(bank(0), 4)[:, :, 64 * hd:64 * hd + 64], ACT.Copy))
                own.do(act.activation(v_tok, split(bank(1), 4), ACT.Copy))
                own.do(act.activation(b_tok, split(bank(2), 4), ACT.Copy))
                own.do(act.activation(k_tok, split(bank(3), 4), ACT.Copy))
                act.sem_inc(on("toks"), 1)
                act.wait_ge(on("bv_done"), r + 1)
                own.do(act.activation(rh[:, :, 64:128], split(bank(0), 8), ACT.Copy))
                act.sem_inc(on("rhs_ready"), 1)
                for level in range(1, 6):
                    for hd in (0, 1):
                        act.wait_ge(on("x_done"), 12 * r + 2 * level + hd + 1)
                        own.do(act.activation(xx[:, 4 * hd:4 * hd + 4, :], split(bank(4 + hd), 4), ACT.Copy))
                        act.sem_inc(on("x_out"), 1)
                for half in (0, 1):
                    act.wait_ge(on("wu_done"), 2 * r + half + 1)
                    own.do(act.activation(wn[:, 4 * half:4 * half + 4, :], split(bank(6 + half), 4), ACT.Copy,
                                          scale=-1.0))
                act.sem_inc(on("wn_ready"), 1)
                act.wait_ge(on("gn_dev"), r + 1)
                own.do(act.activation(tmp[:], kk[:], ACT.Square))
                act.sem_inc(on("gn_sq"), 1)
                root("gn_sum", r + 1, bank(0), 1.0, "gn_eps", "gn_read", "gn_root")

            base = S0["ssd"]
            with own.loop(SSD_G, 22) as g:
                def affine(u, tiles):
                    act.wait_ge(on("gemm_done"), base + u + 4 * g + 1)
                    slot, _ = slot_of(base, u)
                    for m, (dst, j) in enumerate(tiles):
                        own.go(act.activation(dst, bank(2 * slot + m), ACT.Identity,
                                              scale=Cd("cw", 3 * 12 + 6 * g + j), bias=Cd("cb", 6 * g + j)))
                    own.wait()
                    act.sem_inc(on("ssd_affine"), 1)

                def silu(u, tiles):
                    act.wait_ge(on("ssd_conv"), 4 * g + u + 1)
                    for dst in tiles:
                        own.go(act.activation(dst, dst, ACT.Silu))
                    own.wait()
                    act.sem_inc(on("xbc_ready"), 1)

                affine(0, [(bc_f[:, 0, :], 0)])
                affine(1, [(bc_f[:, 1, :], 1)])
                silu(0, [bc_f[:, 0, :]])
                affine(2, [(xs[:, 0, :], 2), (xs[:, 1, :], 3)])
                silu(1, [bc_f[:, 1, :]])
                affine(3, [(xs[:, 2, :], 4), (xs[:, 3, :], 5)])
                silu(2, [xs[:, 0, :], xs[:, 1, :]])
                silu(3, [xs[:, 2, :], xs[:, 3, :]])
                act.wait_ge(on("ssd_logs"), g + 1)
                own.do(act.activation(dte, dte, ACT.Exp))
                own.do(act.activation(seg.rearrange("p a b -> p (a b)"), seg.rearrange("p a b -> p (a b)"), ACT.Exp))
                own.do(act.activation(acb.rearrange("p a b -> p (a b)"), acb.rearrange("p a b -> p (a b)"), ACT.Exp))
                act.sem_inc(on("ssd_exps"), 1)
                for i in range(4):
                    act.wait_ge(on("yg_ready"), 4 * g + i + 1)
                    own.do(act.activation(xs[:, i, :], yg[:, i, :], ACT.Square))
                    act.sem_inc(on("yg_sq"), 1)
                root("ssd_sum", g + 1, bank(4), 1.0 / 512, "eps", None, "ssd_root")

            act.wait_ge(on("ssd_group"), SSD_G)
            project_out(0)
            norm_split(1, "up0a")
            up(0, 0)

            act.wait_ge(on("cols1_in"), 16)
            own.do(act.activation(lam[:, 0, :], C1("log_dt"), ACT.Exp))
            act.sem_inc(on("s5_dt"), 1)
            act.wait_ge(on("s5_angle"), 1)
            own.do(act.activation(lam[:, 1, :], lam[:, 1, :], ACT.Exp))
            own.do(act.activation(lam[:, 3, :], lam[:, 2, :], ACT.Sin))
            own.do(act.activation(lam[:, 4, :], lam[:, 2, :], ACT.Sin, scale=0.5))
            act.sem_inc(on("s5_trig"), 1)
            down(0, 0)
            up(0, 1)
            down(0, 1)
            norm(2)

            for half, dst in ((0, wt_r), (1, wt_i)):
                act.wait_ge(on("wm_turned"), half + 1)
                for b in range(4):
                    own.do(act.activation(dst[:, 4 * b:4 * b + 4, :], split(bank(4 + b), 4), ACT.Copy))
                act.sem_inc(on("wm_out"), 1)
            for half in (0, 1):
                act.wait_ge(on("kernels_done"), half + 1)
                for b in range(4):
                    eight = kker[0:16, 16 * half + 8 * (b % 2):16 * half + 8 * (b % 2) + 8, :]
                    own.do(act.activation(eight.rearrange("p (g o) c -> p g o c", o=2)[:, :, b // 2, :],
                                          split(bank(4 + b), 4)[0:16], ACT.Copy))
                act.sem_inc(on("kernels_out"), 1)

            base = S0["ret"]
            act.wait_ge(on("consts1_in"), 16)
            for h in range(RET_H):
                if h == 3:
                    act.wait_ge(on("s5_y"), 1)
                    for b in range(4):
                        every_other = yc[:, 16 * (b % 2):16 * (b % 2) + 16, :].rearrange("p (g o) c -> p g o c", o=2)
                        own.do(act.activation(every_other[:, :, b // 2, :], split(bank(4 + b), 8), ACT.Copy))
                        act.sem_inc(on("s5_out"), 1)
                act.wait_ge(on("ret_read"), h + 1)
                for v in (0, 1):
                    act.wait_ge(on("gemm_done"), base + 1 + v + 4 * h + 1)
                    slot, _ = slot_of(base, 1 + v)
                    own.do(act.activation(v_tk[:, :, v * P:(v + 1) * P], split(bank(2 * slot), 4), ACT.Copy))
                    act.sem_inc(psum_free[slot], 1)
                act.sem_inc(on("v_tok_ready"), 1)
                act.wait_ge(on("gemm_done"), base + 3 + 4 * h + 1)
                slot, _ = slot_of(base, 3)
                for m in (0, 1):
                    own.do(act.activation(gs[:, m, :], bank(2 * slot + m), ACT.Silu))
                act.sem_inc(psum_free[slot], 1)
                act.sem_inc(on("gs_ready"), 1)
                if h == 0:
                    act.wait_ge(on("kernels_spread"), 16 * S5_T)
                    act.wait_ge(on("vin_done"), 1)
                    for ri in (0, 1):
                        for b in (0, 1):
                            own.do(act.activation(vin[:, :, ri, 8 * b:8 * b + 8],
                                                  split(bank(4 + 2 * ri + b), 8).rearrange("p q c -> p c q"), ACT.Copy))
                    act.sem_inc(on("vin_out"), 1)
                act.wait_ge(on("scores_done"), h + 1)
                own.do(act.activation(k_tk, split(bank(5), 4), ACT.Copy, scale=K1("kdec", h, 1)))
                act.sem_inc(on("k_tok_ready"), 1)
                act.wait_ge(on("ret_y"), h + 1)
                for m in (0, 1):
                    own.do(act.activation(sq2[:, m, :], bank(4 + m), ACT.Square))
                act.sem_inc(on("ret_sq"), 1)
                root("ret_sum", h + 1, bank(6), 1.0 / DV, "eps", None, "ret_root")

            for i in range(4):
                act.wait_ge(on("s5_skip"), i + 1)
                own.do(act.activation(y_gl[:, i, :].rearrange("p (c s) -> p s c", s=S5_T), split(y_in[:, i, :], S5_T),
                                      ACT.Gelu_apprx_tanh))
                act.sem_inc(on("gelu_ready"), 1)
            act.wait_ge(on("ret_head"), RET_H)
            base = S0["glu"]
            for u in (0, 1):
                slot, _ = slot_of(base, u)
                act.wait_ge(on("gemm_done"), base + u + 1)
                for m in (0, 1):
                    own.do(act.activation([qr, kr, qd, rm][2 * u + m], bank(2 * slot + m), ACT.Sigmoid,
                                          bias=C("b_glu", 2 * u + m)))
                act.sem_inc(psum_free[slot], 1)
                act.sem_inc(on("glu_gate"), 1)

            act.wait_ge(on("ret_head"), RET_H)
            act.wait_ge(on("glu_out"), 4)
            project_out(1)
            norm_split(3, "up1a")
            for part in (0, 1):
                up(1, part)
                down(1, part)
            norm(4)

        @block.tensor
        def _(pe):
            ones, ident, bones = K("ones"), K("ident"), K("bones")

            def begin(base, u, i=0, stride=2):
                slot, before = slot_of(base, u, i, stride)
                pe.wait_ge(w_landed[slot], 16 * (before + 1))
                if base + u >= 2:
                    pe.wait_ge(psum_free[slot], before)
                return slot

            def product(base, u, i, stride, kt_, rhs, tiles=2):
                slot = begin(base, u, i, stride)
                w = wslot[:, slot, 0:tiles * kt_ * P].rearrange("p (m k c) -> p m k c", m=tiles, k=kt_)
                for m in range(tiles):
                    for k in range(kt_):
                        mm = pe.matmul(bank(2 * slot + m), w[:, m, k, :], rhs(k), start=k == 0, stop=k == kt_ - 1)
                mm.then_inc(on("gemm_done"), 1)

            h_of = lambda k: h_t[:, k, :]

            def product_split(base, u, i, stride, kt_, operand, before_k=None):
                slot, before = slot_of(base, u, i, stride)
                pe.wait_ge(on("w_split"), pieces_before(base) + u + stride * i + 1)
                pe.wait_ge(psum_free[slot], before - 1)
                out = bank(mlp_bank(base, u))
                for k in range(kt_):
                    if before_k:
                        before_k(k)
                    high, low = (w_s[:, slot, part, k * P:(k + 1) * P] for part in (0, 1))
                    pe.matmul(out, high, operand[:, 0, k, :], start=k == 0, stop=False)
                    pe.matmul(out, high, operand[:, 1, k, :], start=False, stop=False)
                    mm = pe.matmul(out, low, operand[:, 0, k, :], start=False, stop=k == kt_ - 1)
                mm.then_inc(on("gemm_done"), 1)

            def norm(n, free):
                for k in range(KD):
                    pe.wait_ge(on("squares"), KD * n + k + 1)
                    mm = pe.matmul(bank(7), ones, h_t[:, k, :], start=k == 0, stop=k == KD - 1)
                mm.then_inc(on("norm_sum"), 1)
                if not free:
                    pe.wait_ge(on("h_ready"), KD * (n + 1))

            def mlp(layer):
                for part, kh in enumerate(KH):
                    up, down = (S0[f"{name}{layer}{'ab'[part]}"] for name in ("up", "down"))
                    with pe.Fori(0, kh // 2) as i:
                        for u in range(4):
                            product_split(up, u, i, 4, KD, h_s)

                    def hidden(k):
                        if k in (0, kh - 2):
                            pe.wait_ge(on("hid_ready"), KF * layer + KH[0] * part + kh - 2 * (k == 0))

                    with pe.Fori(0, KD // 4) as i:
                        for u in range(4):
                            product_split(down, u, i, 4, kh, hid_s, hidden)

            def project_out(layer):
                with pe.Fori(0, KD // 4) as i:
                    for u in range(4):
                        product_split(S0[f"out{layer}"], u, i, 4, KO, hid_s,
                                      lambda k: pe.wait_ge(on("y_split"), KO * layer + k + 1))

            pe.wait_ge(on("x_loaded"), 16)
            pe.wait_ge(on("consts_in"), 16)
            for k in range(KD):
                for t in range(TT):
                    mm = pe.transpose(ps[:, k, t * P:(t + 1) * P], x_in[:, t, k * P:(k + 1) * P], ident)
            mm.then_inc(on("x_turned"), 1)
            norm(0, None)

            product(S0["lora"], 0, 0, 2, KD, h_of)
            pe.wait_ge(on("cols_in"), 16)
            wdt = C("w_dt", 0, 128).rearrange("p (k h) -> p k h", k=KD)
            for t in range(TT):
                for k in range(KD):
                    mm = pe.matmul(ps[:, 6, t * 16:(t + 1) * 16], h_t[:, k, t * P:(t + 1) * P], wdt[:, k, :],
                                   start=k == 0, stop=k == KD - 1)
            mm.then_inc(on("dt_sum"), 1)
            pe.wait_ge(on("dt_rates"), 1)
            pe.matmul(ps[:, 6, 0:64], K("triu"), dts[:, 5, :], start=True, stop=True).then_inc(on("acc_sum"), 1)
            pe.wait_ge(on("acc_ready"), 1)
            pe.transpose(ps[0:64, 6, 0:P], dts[:, 6, :], ident).then_inc(on("acc_turn"), 1)
            pe.wait_ge(on("acc_turned"), 1)
            pe.wait_ge(on("lora_acts"), 1)
            pe.wait_ge(on("lora_in"), 48)
            for j in range(4):
                if j >= 2:
                    pe.wait_ge(on("lora_w_out"), j - 1)
                b = 2 * (j % 2) + 4
                pe.matmul(bank(b), at_[0:64, j, :], rr[0:64], start=True, stop=True)
                pe.matmul(bank(b + 1), at_[64:128, j, :], rr[64:128], start=True, stop=True)\
                    .then_inc(on("lora_w"), 1)
            for j in range(4):
                if j >= 2:
                    pe.wait_ge(on("lora_g_out"), j - 1)
                pe.matmul(bank(2 + j % 2), bt_[:, j, :], vv[:], start=True, stop=True).then_inc(on("lora_g"), 1)
            pe.wait_ge(on("lora_g_out"), 4)

            base = S0["rwkv"]
            pairs = [(hd, t) for hd in (0, 1) for t in range(TT)]

            def mat(b0, m):
                return ps[:, b0 + m // 4, (m % 4) * P:(m % 4 + 1) * P]

            with pe.Fori(0, 4) as r:
                product(base, 0, r, 4, KD, h_of)
                pe.wait_ge(on("gn_read"), r + 1)
                product(base, 1, r, 4, KD, h_of, 1)
                pe.wait_ge(on("kk_sq"), r + 1)
                pe.matmul(bank(4), bones, tmp[:], start=True, stop=True).then_inc(on("kk_sum"), 1)
                product(base, 2, r, 4, KD, h_of, 1)
                product(base, 3, r, 4, KD, h_of, 1)
                pe.wait_ge(on("bonus_in"), r + 1)
                pe.matmul(bank(5), bones, bt[:], start=True, stop=True).then_inc(on("bonus_sum"), 1)
                pe.wait_ge(on("z_out"), 2 * r + 2)
                pe.wait_ge(on("keys"), r + 1)
                for hd in (0, 1):
                    lo, hi = 64 * hd, 64 * hd + 64
                    for b, (lh, rhs_) in enumerate(((bh, zz), (kh, zz), (bh, rd), (kh, rd))):
                        for t in range(TT):
                            mm = pe.matmul(ps[:, 4 * hd + b, t * P:(t + 1) * P], lh[lo:hi, t * P:(t + 1) * P],
                                           rhs_[lo:hi, t * P:(t + 1) * P], start=True, stop=True)
                    mm.then_inc(on("grams"), 1)
                pe.wait_ge(on("tails"), r + 1)
                pe.wait_ge(on("grams_out"), 2 * r + 1)
                for b, src in enumerate((zz, vv, bt, kt)):
                    for t in range(TT):
                        mm = pe.transpose(ps[:, b, t * P:(t + 1) * P], src[:, t * P:(t + 1) * P], ident)
                mm.then_inc(on("tok_turned"), 1)
                for hd in (0, 1):
                    pe.wait_ge(on("al_ready"), 12 * r + hd + 1)
                    for m in range(4 * hd, 4 * hd + 4):
                        mm = pe.matmul(mat(4, m), al_[:, m, :], ident, start=True, stop=True)
                    mm.then_inc(on("x_done"), 1)
                pe.wait_ge(on("toks"), r + 1)
                for m, (hd, t) in enumerate(pairs):
                    mm = pe.matmul(ps[:, 0, m * 64:(m + 1) * 64], bt_[:, m, :], v_tok[:, t, 64 * hd:64 * hd + 64],
                                   start=True, stop=True)
                mm.then_inc(on("bv_done"), 1)
                for level in range(1, 6):
                    for hd in (0, 1):
                        pe.wait_ge(on("al_ready"), 12 * r + 2 * level + hd + 1)
                        for m in range(4 * hd, 4 * hd + 4):
                            mm = pe.matmul(mat(4, m), al_[:, m, :], tl[:, m, :], start=True, stop=True)
                        mm.then_inc(on("x_done"), 1)
                    for hd in (0, 1):
                        pe.wait_ge(on("x_out"), 10 * r + 2 * (level - 1) + hd + 1)
                        if level < 5:
                            for m in range(4 * hd, 4 * hd + 4):
                                pe.matmul(mat(6, m), tu[:, m, :], xx[:, m, :], start=True, stop=True)
                        for m in range(4 * hd, 4 * hd + 4):
                            mm = pe.matmul(mat(4, m), xx[:, m, :], tu[:, m, :], start=True, stop=True)
                        mm.then_inc(on("tx_done"), 1)
                pe.wait_ge(on("rhs_ready"), r + 1)
                for hd in (0, 1):
                    pe.wait_ge(on("tu_ready"), 2 * r + hd + 1)
                    for m in range(4 * hd, 4 * hd + 4):
                        mm = pe.matmul(mat(6, m), tu[:, m, :], rh[:, m, :], start=True, stop=True)
                    mm.then_inc(on("wu_done"), 1)
                pe.wait_ge(on("wn_ready"), r + 1)
                for m, (hd, t) in enumerate(pairs):
                    lo, hi = 64 * hd, 64 * hd + 64
                    pe.matmul(ps[lo:hi, 4, t * P:(t + 1) * P], wn[:, m, 0:64], qb_[:, m, :], start=True, stop=True)
                    for q in (0, 1):
                        c, ql, qh = 2 * t + q, 64 * q, 64 * q + 64
                        pe.matmul(ps[lo:hi, 5 + q, c * 64:(c + 1) * 64], wn[ql:qh, m, 0:64], b_tok[ql:qh, t, lo:hi],
                                  start=True, stop=True)
                        pe.matmul(ps[lo:hi, 7 * q, c * 64:(c + 1) * 64], b_tok[ql:qh, t, lo:hi], wn[ql:qh, m, 64:128],
                                  start=True, stop=False)
                        mm = pe.matmul(ps[lo:hi, 7 * q, c * 64:(c + 1) * 64], k_tok[ql:qh, t, lo:hi],
                                       v_tok[ql:qh, t, lo:hi], start=False, stop=True)
                mm.then_inc(on("chunk_maps"), 1)
                for c in range(1, NC - 1):
                    pe.wait_ge(on("state_ready"), (NC - 1) * r + c)
                    pe.sem_inc(on("state_seen"), 1)
                    for lo in (0, 64):
                        mm = pe.matmul(ps[lo:lo + 64, 1, c * 64:(c + 1) * 64], gt[lo:lo + 64, c, :],
                                       st[lo:lo + 64, c, :], start=True, stop=True)
                    mm.then_inc(on("state_moved"), 1)
                pe.wait_ge(on("state_ready"), (NC - 1) * (r + 1))
                for m, (hd, t) in enumerate(pairs):
                    lo, hi = 64 * hd, 64 * hd + 64
                    out = ps[lo:hi, 2, t * P:(t + 1) * P]
                    pe.matmul(out, v_tok[:, t, lo:hi], qk_[:, m, :], start=True, stop=False)
                    mm = pe.matmul(out, wn[:, m, 64:128], qb_[:, m, :], start=False, stop=True)
                    for q in (0, 1):
                        c = 2 * t + q
                        if c:
                            mm = pe.matmul(ps[lo:hi, 2, c * 64:(c + 1) * 64], st[lo:hi, c, :],
                                           rd[lo:hi, c * 64:(c + 1) * 64], start=False, stop=True,
                                           skip_group_check=True)
                mm.then_inc(on("rwkv_y"), 1)
                pe.wait_ge(on("gn_in"), r + 1)
                pe.matmul(bank(3), bones, kk[:], start=True, stop=True).then_inc(on("gn_mean"), 1)
                pe.wait_ge(on("gn_sq"), r + 1)
                pe.matmul(bank(0), bones, tmp[:], start=True, stop=True).then_inc(on("gn_sum"), 1)
            pe.wait_ge(on("rwkv_head"), 4)

            base = S0["ssd"]
            with pe.Fori(0, SSD_G) as g:
                for u, tiles in enumerate((1, 1, 2, 2)):
                    product(base, u, g, 4, KD, h_of, tiles)
                pe.wait_ge(on("xbc_ready"), 4 * g + 2)
                for t in range(TT):
                    tok = slice(t * P, (t + 1) * P)
                    pe.matmul(ps[:, 4, tok], bc_f[:, 0, tok], bc_f[:, 1, tok], start=True, stop=True)
                    mm = pe.transpose(ps[:, 5, tok], bc_f[:, 0, tok], ident)
                mm.then_inc(on("cb_done"), 1)
                pe.wait_ge(on("cb_out"), g + 1)
                pe.wait_ge(on("xbc_ready"), 4 * g + 4)
                for t in range(TT):
                    for i in range(4):
                        mm = pe.transpose(ps[:, 4 + t, i * P:(i + 1) * P], xs[:, i, t * P:(t + 1) * P], ident)
                mm.then_inc(on("xs_turned"), 1)
                pe.wait_ge(on("xd_ready"), g + 1)
                for t in range(TT - 1):
                    mm = pe.matmul(bank(4 + t), b_tk[:, t, :], xdd[:, t, :], start=True, stop=True)
                mm.then_inc(on("ssd_new"), 1)
                pe.wait_ge(on("ssd_state"), g + 1)
                pe.wait_ge(on("ssd_masks"), g + 1)
                for i in range(4):
                    for t in range(TT):
                        for hd in (0, 1):
                            j = 2 * i + hd
                            out = ps[64 * hd:64 * hd + 64, 4 + i, t * P:(t + 1) * P]
                            mm = pe.matmul(out, xdt[:, t, j * 64:(j + 1) * 64], seg[:, t * 8 + j, :],
                                           start=True, stop=t == 0)
                            if t:
                                mm = pe.matmul(out, s_ssd[:, t - 1, j * 64:(j + 1) * 64], acb[:, t * 8 + j, :],
                                               start=False, stop=True)
                mm.then_inc(on("ssd_y"), 1)
                for i in range(4):
                    pe.wait_ge(on("yg_sq"), 4 * g + i + 1)
                    if i == 0:
                        pe.wait_ge(on("yg_ready"), 4 * g + 4)
                    mm = pe.matmul(bank(4), ones, xs[:, i, :], start=i == 0, stop=i == 3)
                mm.then_inc(on("ssd_sum"), 1)
                pe.wait_ge(on("ssd_group"), g + 1)

            project_out(0)
            norm(1, None)
            mlp(0)
            norm(2, True)

            def turn_wm(half):
                pe.wait_ge(on("wm_ready"), 1)
                pe.wait_ge(on("norm_read"), 3)
                if half:
                    pe.wait_ge(on("wm_out"), 1)
                for q in range(S5_PAIR):
                    mm = pe.transpose(mat(4, q), (wm, wm2)[half][:, q, :], ident)
                mm.then_inc(on("wm_turned"), 1)

            def kernels(half):
                pe.wait_ge(on("wm_out"), 2)
                pe.wait_ge(on("ck_ready"), 1)
                if half:
                    pe.wait_ge(on("kernels_out"), 1)
                for n in range(16):
                    g = 16 * half + n
                    q, lo = g // 2, 64 * (g % 2)
                    out = ps[0:16, 4 + 2 * (n % 2) + n // 8, (n // 2 % 4) * P:(n // 2 % 4 + 1) * P]
                    pe.matmul(out, bb[lo:lo + 64, 0, q, :], ck[lo:lo + 64, 0, q, 0:P], start=True, stop=False)
                    mm = pe.matmul(out, bb[lo:lo + 64, 1, q, :], ck[lo:lo + 64, 1, q, 0:P], start=False, stop=True)
                mm.then_inc(on("kernels_done"), 1)

            turn_wm(0)
            pe.wait_ge(on("h_ready"), KD * 3)
            product(S0["u"], 0, 0, 2, KD, h_of)
            turn_wm(1)
            product(S0["u"], 1, 0, 2, KD, h_of)
            kernels(0)

            def s5_inputs():
                pe.wait_ge(on("u_spread"), 16 * S5_T)
                for ri, src in ((0, wt_r), (1, wt_i)):
                    for g in range(S5_G):
                        q, lo = g // 2, 64 * (g % 2)
                        mm = pe.matmul(ps[lo:lo + 64, 4 + 2 * ri + q // 8, (q % 8) * 64:(q % 8 + 1) * 64],
                                       src[:, q, lo:lo + 64], uc[:, g, :], start=True, stop=True)
                mm.then_inc(on("vin_done"), 1)
                pe.wait_ge(on("vin_out"), 1)

            def s5_outputs():
                pe.wait_ge(on("kernels_spread"), 16 * S5_T)
                pe.wait_ge(on("s5_states"), 1)
                for g in range(S5_G):
                    q, lo = g // 2, 64 * (g % 2)
                    out = ps[:, 4 + 2 * (g % 2) + q // 8, (q % 8) * 64:(q % 8 + 1) * 64]
                    pe.matmul(out, toep[:, g, :], uc[:, g, :], start=True, stop=False)
                    pe.matmul(out, ck[lo:lo + 64, 0, q, 16:144], xc[lo:lo + 64, 0, q, :], start=False, stop=False)
                    mm = pe.matmul(out, ck[lo:lo + 64, 1, q, 16:144], xc[lo:lo + 64, 1, q, :], start=False, stop=True)
                mm.then_inc(on("s5_y"), 1)
                pe.wait_ge(on("s5_out"), 4)

            base = S0["ret"]
            for h in range(RET_H):
                product(base, 0, h, 4, KD, h_of)
                if h == 0:
                    kernels(1)
                if h == 3:
                    pe.wait_ge(on("ret_read"), h + 1)
                    s5_outputs()
                for v in (0, 1):
                    slot = begin(base, 1 + v, h, 4)
                    w = wslot[:, slot, 0:KD * P].rearrange("p (k c) -> p k c", k=KD)
                    for t in range(TT):
                        for k in range(KD):
                            mm = pe.matmul(ps[:, 2 * slot, t * P:(t + 1) * P], h_t[:, k, t * P:(t + 1) * P],
                                           w[:, k, :], start=k == 0, stop=k == KD - 1)
                    mm.then_inc(on("gemm_done"), 1)
                product(base, 3, h, 4, KD, h_of)
                pe.wait_ge(on("ret_read"), h + 1)
                pe.wait_ge(on("kernels_out"), 2)
                if h == 0:
                    s5_inputs()
                pe.wait_ge(on("qk_ready"), h + 1)
                for t in range(TT):
                    tok = slice(t * P, (t + 1) * P)
                    pe.matmul(ps[:, 4, tok], kr[:, tok], qr[:, tok], start=True, stop=True)
                    mm = pe.transpose(ps[:, 5, tok], kr[:, tok], ident)
                mm.then_inc(on("scores_done"), 1)
                pe.wait_ge(on("k_tok_ready"), h + 1)
                pe.wait_ge(on("v_tok_ready"), h + 1)
                for t in range(TT - 1):
                    mm = pe.matmul(ps[:, 6 + t // 2, (t % 2) * DV:(t % 2 + 1) * DV], k_tk[:, t, :], v_tk[:, t, :],
                                   start=True, stop=True)
                mm.then_inc(on("ret_new"), 1)
                pe.wait_ge(on("scores_ready"), h + 1)
                pe.wait_ge(on("ret_state"), h + 1)
                for m in (0, 1):
                    for t in range(TT):
                        out = ps[:, 4 + m, t * P:(t + 1) * P]
                        mm = pe.matmul(out, v_tk[:, t, m * P:(m + 1) * P], sm[:, t, :], start=True, stop=t == 0)
                        if t:
                            mm = pe.matmul(out, s_ret[:, t - 1, m * P:(m + 1) * P], qd[:, t * P:(t + 1) * P],
                                           start=False, stop=True)
                mm.then_inc(on("ret_y"), 1)
                pe.wait_ge(on("ret_sq"), h + 1)
                for m in (0, 1):
                    mm = pe.matmul(bank(6), ones, sq2[:, m, :], start=m == 0, stop=m == 1)
                mm.then_inc(on("ret_sum"), 1)
            pe.wait_ge(on("gelu_ready"), 4)
            for u in (0, 1):
                product(S0["glu"], u, 0, 2, 4, lambda k: y_gl[:, k, :])
            pe.wait_ge(on("glu_out"), 4)
            project_out(1)
            norm(3, None)
            mlp(1)
            norm(4, None)
            for t in range(TT):
                if t >= 2:
                    pe.wait_ge(on("rows_ready"), t - 1)
                for k in range(KD):
                    mm = pe.transpose(ps[:, 4 + 2 * (t % 2) + k // 4, (k % 4) * P:(k % 4 + 1) * P],
                                      h_t[:, k, t * P:(t + 1) * P], ident)
                mm.then_inc(on("rows_turned"), 1)

        @block.vector
        def _(dve):
            own = Own(dve, on("dve_own"))
            do, go = own.do, own.go
            TTo, TS, STT = dve.tensor_tensor, dve.tensor_scalar, dve.scalar_tensor_tensor

            def norm(n, gain):
                dve.wait_ge(on("norm_root"), n + 1)
                for k in range(KD):
                    do(STT(h_t[:, k, :], x_t[:, k, :], C(gain, k), rn[:], ALU.mult, ALU.mult))
                    dve.sem_inc(on("h_ready"), 1)

            def norm_split(n, gain):
                dve.wait_ge(on("norm_root"), n + 1)
                for k in range(KD + 1):
                    if k < KD:
                        do(STT(h_t[:, k, :], x_t[:, k, :], C(gain, k), rn[:], ALU.mult, ALU.mult))
                        dve.sem_inc(on("h_whole"), 1)
                    if k:
                        dve.wait_ge(on("h_high"), KD * (n // 2) + k)
                        do(TTo(h_s[:, 1, k - 1, :], h_t[:, k - 1, :], h_s[:, 0, k - 1, :].bitcast(F32), ALU.subtract))
                        dve.sem_inc(on("h_ready"), 1)

            def add_part(base, u, i=0):
                dve.wait_ge(on("gemm_done"), base + u + 4 * i + 1)
                xj = x_t[:, bass.ds(4 * i + u, 1), :].rearrange("p a b -> p (a b)")
                do(TTo(xj, xj, bank(mlp_bank(base, u)), ALU.add))
                dve.sem_inc(psum_free[(base + u) % 2], 1)

            def add_parts(phase, last):
                with own.loop(KD // 4, 4) as i:
                    for u in range(4):
                        add_part(S0[phase], u, i)
                        if last:
                            dve.sem_inc(on("x_ready"), 1)

            def project_out(layer):
                for k in range(KO):
                    dve.wait_ge(on("y_high"), KO * layer + k + 1)
                    do(TTo(hid_s[:, 1, k, :], y_t[:, k, :], hid_s[:, 0, k, :].bitcast(F32), ALU.subtract))
                    dve.sem_inc(on("y_split"), 1)
                add_parts(f"out{layer}", True)

            def up(layer, part):
                base, first = S0[f"up{layer}{'ab'[part]}"], KH[0] * part
                with own.loop(KH[part] // 2, 14) as i:
                    for v in (0, 1):
                        pair = layer * KF + first + v + 2 * i
                        dve.wait_ge(on("mlp_affine"), pair + 1)
                        for tap in (1, 0):
                            sh = 2 - tap
                            for half in (0, 1):
                                dst = cg[:, v, half, sh:T]
                                j = first + v + 2 * i + KF * half + tap * 2 * KF
                                go(STT(dst, bank(mlp_bank(base, 2 * v + half))[:, 0:T - sh], Cd(f"fcw{layer}", j), dst,
                                       ALU.mult, ALU.add))
                            own.wait()
                        dve.sem_inc(psum_free[0], 1)
                        dve.sem_inc(psum_free[1], 1)
                        dve.sem_inc(on("mlp_conv"), 1)
                        dve.wait_ge(on("mlp_gate"), pair + 1)
                        if part:
                            dve.wait_ge(on("gemm_done"), S0[f"up{layer}b"])
                        tile = lambda n: hid_s[:, n, bass.ds(v + 2 * i, 1), :].rearrange("p a b -> p (a b)")
                        go(TTo(tile(0), cg[:, v, 0, :], cg[:, v, 1, :], ALU.mult))
                        own.wait()
                        do(TTo(cg[:, v, 0, :], cg[:, v, 0, :], cg[:, v, 1, :], ALU.mult))
                        do(TTo(tile(1), cg[:, v, 0, :], tile(0).bitcast(F32), ALU.subtract))
                        dve.sem_inc(on("cg_read"), 1)
                        dve.sem_inc(on("hid_ready"), 1)

            for name, free in (("pads_read", 1), ("gn_read", 1), ("cg_read", 2), ("ret_read", 1)):
                dve.sem_inc(on(name), free)
            dve.wait_ge(on("cols_in"), 16)
            dve.wait_ge(on("consts_in"), 16)
            dve.wait_ge(on("consts0_in"), 16)
            norm(0, "mix_g0")

            def mix(dst, j, mu):
                do(TTo(dst, pad[:, j, 0:T], pad[:, j, 1:T + 1], ALU.subtract))
                do(STT(dst, dst, mu, pad[:, j, 1:T + 1], ALU.mult, ALU.add))

            dve.wait_ge(on("lora_pad"), 1)
            mix(kq, 0, C("mu", 12))
            mix(kk, 1, C("mu", 13))
            dve.sem_inc(on("lora_mixed"), 1)
            grp = lambda n, g: split(dts[:, n, g * 32:(g + 1) * 32], TT)
            dve.wait_ge(on("dt_sum"), 1)
            for g in range(SSD_G):
                do(TTo(grp(0, g), split(ps[:, 6, 0:64], TT)[:, :, 8 * g:8 * g + 8],
                       split(C("dt_bias", g * 32, 32), TT), ALU.add))
            do(STT(dts[:, 1, :], dts[:, 0, :], -1.0, dts[:, 0, :], ALU.mult, ALU.max))
            dve.sem_inc(on("dt_abs"), 1)
            dve.wait_ge(on("dt_exp"), 1)
            do(TS(dts[:, 4, :], dts[:, 1, :], 1.0, None, ALU.add))
            do(STT(dts[:, 1, :], dts[:, 4, :], -1.0, dts[:, 1, :], ALU.add, ALU.subtract))
            do(dve.reciprocal(dts[:, 4, :], dts[:, 4, :]))
            do(TTo(dts[:, 1, :], dts[:, 1, :], dts[:, 4, :], ALU.mult))
            do(TTo(dts[:, 2, :], dts[:, 2, :], dts[:, 1, :], ALU.subtract))
            do(STT(dts[:, 0, :], dts[:, 0, :], 0.0, dts[:, 2, :], ALU.max, ALU.add))
            do(STT(dts[:, 5, :], dts[:, 0, :], -1.0, dts[:, 3, :], ALU.mult, ALU.mult))
            dve.sem_inc(on("dt_rates"), 1)
            dve.wait_ge(on("acc_sum"), 1)
            do(dve.tensor_copy(dts[:, 6, :], ps[:, 6, 0:64]))
            dve.sem_inc(on("acc_ready"), 1)
            dve.wait_ge(on("acc_turn"), 1)
            do(dve.tensor_copy(acc_t[:, :], ps[0:64, 6, 0:P]))
            dve.sem_inc(on("acc_turned"), 1)
            for j in range(4):
                dve.wait_ge(on("lora_g"), j + 1)
                do(dve.tensor_copy(gate[:, j, :], bank(2 + j % 2)))
                dve.sem_inc(on("lora_g_out"), 1)
            dve.wait_ge(on("lora_w_out"), 4)

            def row(v, r):
                return v[:, bass.ds(r, 1), :].rearrange("p a b -> p (a b)")

            chunks = lambda v: split(v, NC)
            with own.loop(4, 84) as r:
                dve.wait_ge(on("rk_pad"), r + 1)
                mix(rr, 0, Cd("mu", r))
                mix(kq, 1, Cd("mu", r + 4))
                do(dve.tensor_tensor_scan(zz, K("reset"), row(sw, r), 0.0, ALU.mult, ALU.add))
                dve.sem_inc(on("log_decay"), 1)
                do(TS(kk, kq, Cd("k_k", r), None, ALU.mult))
                do(TTo(tmp, kk, kk, ALU.mult))
                dve.sem_inc(on("kk_sq"), 1)
                do(TS(bh, row(ai, r), -1.0, Cd("k_a", r), ALU.add, ALU.mult))
                do(STT(kh, bh, 1.0, kq, ALU.add, ALU.mult))
                do(STT(bt, rr, Cd("r_k", r), kh, ALU.mult, ALU.mult))
                dve.sem_inc(on("bonus_in"), 1)
                dve.wait_ge(on("v_pad"), r + 1)
                mix(vv, 2, Cd("mu", r + 8))
                dve.sem_inc(on("pads_read"), 1)
                dve.wait_ge(on("kk_sum"), r + 1)
                do(TS(rn[:], bank(4), float(N_RWKV), 1e-24, ALU.mult, ALU.max))
                dve.sem_inc(on("kk_var"), 1)
                dve.wait_ge(on("bonus_sum"), r + 1)
                do(STT(bonus, bank(5), float(N_RWKV), vv, ALU.mult, ALU.mult))
                dve.wait_ge(on("decays"), r + 1)
                do(TTo(rd, rr, pp, ALU.mult))
                do(TTo(kh, kh, ip, ALU.mult))
                dve.wait_ge(on("kk_root"), r + 1)
                do(TTo(kk, kk, rn[:], ALU.mult))
                do(TTo(bh, kk, row(ai, r), ALU.mult))
                do(TTo(bh, bh, ip, ALU.mult))
                go(TTo(chunks(zz)[:, :, 1:CH], chunks(kk)[:, :, 1:CH], chunks(pp)[:, :, 0:CH - 1], ALU.mult))
                go(dve.tensor_copy(chunks(zz)[:, :, 0:1], chunks(kk)[:, :, 0:1]))
                own.wait()
                dve.sem_inc(on("keys"), 1)
                end = chunks(pp)[:, :, CH - 1:CH].broadcast_to([P, NC, CH])
                go(TTo(chunks(bt), chunks(bh), end, ALU.mult))
                go(TTo(chunks(kt), chunks(kh), end, ALU.mult))
                go(TTo(gt, each(K("ident2"), NC), end, ALU.mult))
                own.wait()
                dve.sem_inc(on("tails"), 1)
                for hd in (0, 1):
                    dve.wait_ge(on("grams"), 2 * r + hd + 1)
                    for b, (dst, mask) in enumerate(((at_, "strict"), (bt_, "strict"), (qb_, "incl"), (qk_, "incl"))):
                        go(TTo(dst[:, 4 * hd:4 * hd + 4, :], split(bank(4 * hd + b), 4), each(K(mask), 4), ALU.mult))
                    own.wait()
                    dve.sem_inc(on("grams_out"), 1)

                def level_part(level, hd):
                    mask, m = K("level")[:, level * P:(level + 1) * P], slice(4 * hd, 4 * hd + 4)
                    go(TTo(al_[:, m, :], at_[:, m, :], each(mask, 4), ALU.mult))

                for hd in (0, 1):
                    m = slice(4 * hd, 4 * hd + 4)
                    level_part(0, hd)
                    own.wait()
                    do(TTo(tu[:, m, :], each(K("ident"), 4), al_[:, m, :], ALU.subtract))
                    dve.sem_inc(on("al_ready"), 1)
                for hd in (0, 1):
                    dve.wait_ge(on("x_done"), 12 * r + hd + 1)
                    go(TTo(tl[:, 4 * hd:4 * hd + 4, :], each(K("ident"), 4), split(bank(4 + hd), 4), ALU.subtract))
                    level_part(1, hd)
                    own.wait()
                    dve.sem_inc(on("al_ready"), 1)
                for level in range(1, 6):
                    for hd in (0, 1):
                        m = slice(4 * hd, 4 * hd + 4)
                        dve.wait_ge(on("tx_done"), 10 * r + 2 * (level - 1) + hd + 1)
                        if level < 5:
                            level_part(level + 1, hd)
                            go(TTo(tl[:, m, :], tl[:, m, :], split(bank(6 + hd), 4), ALU.subtract))
                        go(TTo(tu[:, m, :], tu[:, m, :], split(bank(4 + hd), 4), ALU.subtract))
                        own.wait()
                        dve.sem_inc(on("al_ready" if level < 5 else "tu_ready"), 1)
                dve.wait_ge(on("chunk_maps"), r + 1)
                go(TTo(rd, rd, bank(4), ALU.add))
                half = lambda v, q: v.rearrange("p (t q) c -> p t q c", q=2)[:, :, q, :]
                for q in (0, 1):
                    go(TTo(half(gt, q), half(gt, q), half(chunks(bank(5 + q)), q), ALU.add))
                    go(dve.tensor_copy(half(hh_, q), half(chunks(bank(7 * q)), q)))
                own.wait()
                do(dve.tensor_copy(st[:, 1, :], hh_[:, 0, :]))
                dve.sem_inc(on("state_ready"), 1)
                for c in range(1, NC - 1):
                    dve.wait_ge(on("state_moved"), (NC - 2) * r + c)
                    do(TTo(st[:, c + 1, :], hh_[:, c, :], ps[:, 1, c * 64:(c + 1) * 64], ALU.add))
                    dve.sem_inc(on("state_ready"), 1)
                dve.wait_ge(on("rwkv_y"), r + 1)
                do(dve.tensor_copy(kk, bank(2)))
                dve.sem_inc(on("gn_in"), 1)
                dve.wait_ge(on("gn_mean"), r + 1)
                do(TTo(kk, kk, bank(3), ALU.subtract))
                dve.sem_inc(on("gn_dev"), 1)
                dve.wait_ge(on("gn_root"), r + 1)
                do(TTo(kk, kk, rn[:], ALU.mult))
                do(TS(kk, kk, Cd("ln_g", r), Cd("ln_b", r), ALU.mult, ALU.add))
                do(TTo(kk, kk, bonus, ALU.add))
                do(TTo(row(y_t, r), kk, row(gate, r), ALU.mult))
                dve.sem_inc(on("rwkv_head"), 1)

            base = S0["ssd"]
            with own.loop(SSD_G, 56) as g:
                def dt_of(n, t=None):
                    return dts[:, n, bass.ds(32 * g + (0 if t is None else 8 * t), 32 if t is None else 8)]

                def conv(u, tiles):
                    dve.wait_ge(on("ssd_affine"), 4 * g + u + 1)
                    slot, _ = slot_of(base, u)
                    for tap in (2, 1, 0):
                        sh = 3 - tap
                        for m, (dst, j) in enumerate(tiles):
                            go(STT(dst[:, sh:T], bank(2 * slot + m)[:, 0:T - sh], Cd("cw", 12 * tap + 6 * g + j),
                                   dst[:, sh:T], ALU.mult, ALU.add))
                        own.wait()
                    dve.sem_inc(psum_free[slot], 1)
                    dve.sem_inc(on("ssd_conv"), 1)

                conv(0, [(bc_f[:, 0, :], 0)])
                dve.wait_ge(on("acc_spread"), 16 * (g + 1))
                go(TTo(dte, acb[:, :, P - 1:P].rearrange("p a b -> p (a b)"), dt_of(6), ALU.subtract))
                go(TTo(seg, acb, over(dt_of(6), P), ALU.subtract))
                own.wait()
                do(TS(seg, seg, 0.0, None, ALU.min))
                dve.sem_inc(on("ssd_logs"), 1)
                conv(1, [(bc_f[:, 1, :], 1)])
                conv(2, [(xs[:, 0, :], 2), (xs[:, 1, :], 3)])
                conv(3, [(xs[:, 2, :], 4), (xs[:, 3, :], 5)])
                dve.wait_ge(on("cb_done"), g + 1)
                go(TTo(cbm, split(bank(4), TT), each(K("triu"), TT), ALU.mult))
                go(dve.tensor_copy(b_tk, split(bank(5), TT)))
                own.wait()
                dve.sem_inc(on("cb_out"), 1)
                dve.wait_ge(on("ssd_exps"), g + 1)
                do(dve.tensor_copy(cdk, acb[:, :, P - 1:P].rearrange("p a b -> p (a b)")))
                dve.wait_ge(on("xs_turned"), g + 1)
                heads = lambda v: split(v, SSD_J)
                for t in range(TT):
                    go(TTo(heads(xdt[:, t, :]), heads(bank(4 + t)), over(dt_of(0, t), 64), ALU.mult))
                own.wait()
                for t in range(TT - 1):
                    go(TTo(heads(xdd[:, t, :]), heads(xdt[:, t, :]), over(dte[:, 8 * t:8 * t + 8], 64), ALU.mult))
                own.wait()
                dve.sem_inc(on("xd_ready"), 1)
                dve.wait_ge(on("xbc_ready"), 4 * g + 2)
                for t in range(TT):
                    go(TTo(seg[:, 8 * t:8 * t + 8, :], seg[:, 8 * t:8 * t + 8, :], each(cbm[:, t, :], 8), ALU.mult))
                    go(TTo(acb[:, 8 * t:8 * t + 8, :], acb[:, 8 * t:8 * t + 8, :],
                           each(bc_f[:, 1, t * P:(t + 1) * P], 8), ALU.mult))
                own.wait()
                dve.sem_inc(on("ssd_masks"), 1)
                dve.wait_ge(on("ssd_new"), g + 1)
                do(dve.tensor_copy(s_ssd[:, 0, :], bank(4)))
                for t in (1, 2):
                    do(TTo(heads(s_ssd[:, t, :]), heads(s_ssd[:, t - 1, :]), over(cdk[:, 8 * t:8 * t + 8], 64),
                           ALU.mult))
                    do(TTo(s_ssd[:, t, :], s_ssd[:, t, :], bank(4 + t), ALU.add))
                dve.sem_inc(on("ssd_state"), 1)
                dve.wait_ge(on("ssd_y"), g + 1)
                y_tile = lambda i: y_t[:, bass.ds(4 + 4 * g + i, 1), :].rearrange("p a b -> p (a b)")
                for i in range(4):
                    do(STT(yg[:, i, :], xs[:, i, :], Cd("ssd_d", 4 * g + i), bank(4 + i), ALU.mult, ALU.add))
                    do(TTo(yg[:, i, :], yg[:, i, :], y_tile(i), ALU.mult))
                    dve.sem_inc(on("yg_ready"), 1)
                dve.wait_ge(on("ssd_root"), g + 1)
                for i in range(4):
                    go(STT(y_tile(i), yg[:, i, :],
                           Cd("ssd_g", 4 * g + i), rn[:], ALU.mult, ALU.mult))
                own.wait()
                dve.sem_inc(on("ssd_group"), 1)

            project_out(0)
            norm_split(1, "ffn_g0")
            up(0, 0)
            dve.wait_ge(on("s5_dt"), 1)
            L = lambda n: lam[:, n, :]
            mul = lambda o, p, q: do(TTo(o, p, q, ALU.mult))
            mul(L(1), C1("lam_re"), L(0))
            mul(L(2), C1("lam_im"), L(0))
            do(TS(L(5), L(2), INV_2PI, MAGIC, ALU.mult, ALU.add))
            do(TS(L(5), L(5), -MAGIC, None, ALU.add))
            for part in (PI_A, PI_B, PI_C):
                do(STT(L(2), L(5), -part, L(2), ALU.mult, ALU.add))
            do(TS(L(2), L(2), PI_MAX, -PI_MAX, ALU.min, ALU.max))
            dve.sem_inc(on("s5_angle"), 1)
            dve.wait_ge(on("s5_trig"), 1)
            mul(L(4), L(4), L(4))
            do(TS(L(4), L(4), -2.0, 1.0, ALU.mult, ALU.add))
            mul(L(6), L(1), L(4))
            mul(L(7), L(1), L(3))
            do(TS(L(8), L(6), -1.0, None, ALU.add))
            mul(L(9), C1("lam_re"), C1("lam_re"))
            mul(L(10), C1("lam_im"), C1("lam_im"))
            do(TTo(L(9), L(9), L(10), ALU.add))
            do(dve.reciprocal(L(9), L(9)))
            mul(L(10), L(8), C1("lam_re"))
            mul(L(11), L(7), C1("lam_im"))
            do(TTo(L(10), L(10), L(11), ALU.add))
            mul(L(10), L(10), L(9))
            mul(L(11), L(7), C1("lam_re"))
            mul(L(12), L(8), C1("lam_im"))
            do(TTo(L(11), L(11), L(12), ALU.subtract))
            mul(L(11), L(11), L(9))

            t_a = s5_tmp

            def cmul(o_re, o_im, p_re, p_im, q_re, q_im, t):
                mul(o_re, p_re, q_re)
                mul(t, p_im, q_im)
                do(TTo(o_re, o_re, t, ALU.subtract))
                mul(o_im, p_re, q_im)
                mul(t, p_im, q_re)
                do(TTo(o_im, o_im, t, ALU.add))

            ch16 = lambda v: split(v, S5_PAIR)
            cmul(bb[:, 0], bb[:, 1], over(L(10), 16), over(L(11), 16), ch16(C1("b_re")), ch16(C1("b_im")),
                 ch16(t_a[:, 0:256]))
            do(dve.memset(pw[:, 0, :, 0:1], 1.0))
            do(dve.memset(pw[:, 1, :, 0:1], 0.0))
            col = lambda ri, n: pw[:, ri, :, n:n + 1].rearrange("p a b -> p (a b)")
            for n in range(1, 9):
                cmul(col(0, n), col(1, n), col(0, n - 1), col(1, n - 1), L(6), L(7), L(13))
            for s in range(S5_T):
                go(dve.tensor_copy(pwr[:, :, :, s:s + 1], pw[:, :, :, 7 - s:8 - s]))
            own.wait()
            for ri in (0, 1):
                do(dve.tensor_copy(lam[:, 14 + ri, :], col(0, 8)))
            do(TS(L(16), col(1, 8), -1.0, None, ALU.mult))
            do(dve.tensor_copy(L(17), col(1, 8)))
            do(TS(C1("c_im"), C1("c_im"), -1.0, None, ALU.mult))

            def by(v, n):
                return v.unsqueeze(3).broadcast_to([P, v.shape[1], v.shape[2], n])

            def times(v, n):
                return v.unsqueeze(2).broadcast_to([P, v.shape[1], n, v.shape[2]])

            def matrices(u):
                q, n = slice(4 * (u % 4), 4 * (u % 4) + 4), 8 if u < 4 else 9
                part = lambda v: v[:, q, :].rearrange("p q (a b) -> p q a b", a=n)
                t = s5_tmp[:, 0:4 * n * 16].rearrange("p (q a b) -> p q a b", q=4, a=n)
                if u < 4:
                    o_re, o_im, last = part(wm), part(wm2), ALU.add
                    p_re, p_im = by(pwr[:, 0, q, :], 16), by(pwr[:, 1, q, :], 16)
                    q_re, q_im = times(bb[:, 0, q, :], n), times(bb[:, 1, q, :], n)
                else:
                    o_re, o_im, last = part(ck[:, 0]), part(ck[:, 1]), ALU.subtract
                    p_re, p_im = by(pw[:, 0, q, :], 16), by(pw[:, 1, q, :], 16)
                    q_re, q_im = times(ch16(C1("c_re"))[:, q, :], n), times(ch16(C1("c_im"))[:, q, :], n)
                go(TTo(o_re, p_re, q_re, ALU.mult))
                go(TTo(t, p_im, q_im, ALU.mult))
                own.wait()
                go(TTo(o_re, o_re, t, ALU.subtract if u < 4 else ALU.add))
                go(TTo(o_im, p_re, q_im, ALU.mult))
                own.wait()
                do(TTo(t, p_im, q_re, ALU.mult))
                do(TTo(o_im, o_im, t, last))

            for u in range(KD):
                add_part(S0["down0a"], u)
                matrices(u)
                if u % 4 == 3:
                    dve.sem_inc(on("wm_ready" if u == 3 else "ck_ready"), 1)
            up(0, 1)
            add_parts("down0b", True)
            norm(2, "mix_g1")

            base = S0["u"]
            for u in (0, 1):
                slot, _ = slot_of(base, u)
                dve.wait_ge(on("gemm_done"), base + u + 1)
                for m in (0, 1):
                    do(dve.tensor_copy(split(u_p[:, 2 * u + m, :], S5_T),
                                       bank(2 * slot + m).rearrange("p (c s) -> p s c", s=S5_T)))
                    dve.sem_inc(on("u_ready"), 1)
                dve.sem_inc(psum_free[slot], 1)

            dve.wait_ge(on("consts1_in"), 16)
            base = S0["ret"]
            with own.loop(RET_H, 17) as h:
                dve.wait_ge(on("gemm_done"), base + 4 * h + 1)
                slot, _ = slot_of(base, 0)
                for m, (dst, cos, sin) in enumerate(((qr, "cosq", "sinq"), (kr, "cosk", "sink"))):
                    src = bank(2 * slot + m)
                    go(TTo(rm[0:64], src[64:128], K1(sin)[0:64], ALU.mult))
                    go(TTo(rm[64:128], src[0:64], K1(sin)[64:128], ALU.mult))
                    go(TTo(dst, src, K1(cos), ALU.mult))
                    own.wait()
                    do(TTo(dst, dst, rm, ALU.add))
                dve.sem_inc(psum_free[slot], 1)
                dve.sem_inc(on("qk_ready"), 1)
                do(TTo(split(qd, TT), split(qr, TT), each(K1d("qdec", P * h, P), TT), ALU.mult))
                dve.wait_ge(on("scores_done"), h + 1)
                do(TTo(sm, split(bank(4), TT), each(K1d("decay", P * h, P), TT), ALU.mult))
                dve.sem_inc(on("scores_ready"), 1)
                dve.wait_ge(on("ret_new"), h + 1)
                do(dve.tensor_copy(s_ret[:, 0:2, :], split(bank(6), 2)))
                do(STT(s_ret[:, 1, :], s_ret[:, 0, :], K1d("gchunk", h, 1), s_ret[:, 1, :], ALU.mult, ALU.add))
                do(STT(s_ret[:, 2, :], s_ret[:, 1, :], K1d("gchunk", h, 1), ps[:, 7, 0:DV], ALU.mult, ALU.add))
                dve.sem_inc(on("ret_state"), 1)
                dve.wait_ge(on("ret_root"), h + 1)
                dve.wait_ge(on("gs_ready"), h + 1)
                for m in (0, 1):
                    do(TTo(gs[:, m, :], gs[:, m, :], rn[:], ALU.mult))
                    do(TTo(y_t[:, bass.ds(4 + 2 * h + m, 1), :].rearrange("p a b -> p (a b)"), gs[:, m, :],
                           bank(4 + m), ALU.mult))
                dve.sem_inc(on("ret_read"), 1)
                dve.sem_inc(on("ret_head"), 1)
            dve.wait_ge(on("s5_back"), 64)
            for i in range(4):
                do(STT(y_in[:, i, :], u_p[:, i, :], C("s5_d", i), y_in[:, i, :], ALU.mult, ALU.add))
                dve.sem_inc(on("s5_skip"), 1)
            for u in (0, 1):
                dve.wait_ge(on("glu_gate"), u + 1)
                for m in (0, 1):
                    do(TTo(y_t[:, 2 * u + m, :], y_gl[:, 2 * u + m, :], [qr, kr, qd, rm][2 * u + m], ALU.mult))
                    dve.sem_inc(on("glu_out"), 1)

            project_out(1)
            norm_split(3, "ffn_g1")
            up(1, 0)
            add_parts("down1a", False)
            up(1, 1)
            add_parts("down1b", True)
            norm(4, "final_g")
            for t in range(TT):
                dve.wait_ge(on("rows_turned"), t + 1)
                do(dve.tensor_copy(y_t[:, 2 * t:2 * t + 2, :], bank(4 + 2 * (t % 2), 2)))
                dve.sem_inc(on("rows_ready"), 1)


def tiles_of(w, order):
    k, n = w.shape
    t = w.reshape(k // P, P, n // P, P).transpose(2, 1, 0, 3)
    width = max(len(o) for o in order) * (k // P) * P
    out = np.zeros((len(order), P, width), w.dtype)
    for s, o in enumerate(order):
        part = t[list(o)].transpose(1, 0, 2, 3).reshape(P, -1)
        out[s, :, :part.shape[1]] = part
    return out


def feature_cols(v):
    return v.reshape(-1, P).T


def per_pair(v):
    v = v.reshape(S5_PAIR, 2, S5_N, -1).transpose(1, 2, 0, 3)
    return v.reshape(P, -1)


def kernel(**inputs):
    import concourse.bacc as bacc
    from concourse.bass_utils import run_bass_kernel_spmd

    v = {k: np.asarray(x) for k, x in inputs.items()}
    w_in = v["l0_w_in"]
    con_, con0, con1_ = constants()
    order12 = [8, 10, 0, 1, 2, 3, 9, 11, 4, 5, 6, 7]
    per_head = lambda x: np.tile(x.reshape(SSD_G, 1, SSD_J), (P, 1, TT, 1)).reshape(P, 64)
    c0 = {
        "mix_g0": feature_cols(v["l0_norm_mix"]), "mu": feature_cols(v["l0_rwkv_mu"]),
        "w0": feature_cols(v["l0_rwkv_w0"]), "a0": feature_cols(v["l0_rwkv_a0"]),
        "k_k": feature_cols(v["l0_rwkv_k_k"]), "k_a": feature_cols(v["l0_rwkv_k_a"]),
        "r_k": feature_cols(v["l0_rwkv_r_k"].reshape(-1)), "ln_g": feature_cols(v["l0_rwkv_ln_g"]),
        "ln_b": feature_cols(v["l0_rwkv_ln_b"]),
        "cw": np.concatenate([feature_cols(w)[:, order12] for w in v["l0_ssd_conv_w"]], axis=1),
        "cb": feature_cols(v["l0_ssd_conv_b"])[:, order12],
        "dt_bias": per_head(v["l0_ssd_dt_bias"]), "a_log": per_head(v["l0_ssd_a_log"]),
        "w_dt": w_in[:, 4352:4368].reshape(KD, P, 16).transpose(1, 0, 2).reshape(P, -1),
        "ssd_d": feature_cols(np.repeat(v["l0_ssd_d"], SSD_P)), "ssd_g": feature_cols(v["l0_ssd_norm_g"]),
        "ffn_g0": feature_cols(v["l0_norm_ffn"]),
        "fcw0": np.concatenate([feature_cols(w) for w in v["l0_ffn_conv_w"]], axis=1),
        "fcb0": feature_cols(v["l0_ffn_conv_b"]), "mix_g1": feature_cols(v["l1_norm_mix"]),
        "s5_d": feature_cols(v["l1_s5_d"]), "b_glu": feature_cols(v["l1_s5_b_glu"]),
        "ffn_g1": feature_cols(v["l1_norm_ffn"]),
        "fcw1": np.concatenate([feature_cols(w) for w in v["l1_ffn_conv_w"]], axis=1),
        "fcb1": feature_cols(v["l1_ffn_conv_b"]), "final_g": feature_cols(v["final_norm"]),
    }
    c1 = {
        "lam_re": per_pair(v["l1_s5_lam_re"]), "lam_im": per_pair(v["l1_s5_lam_im"]),
        "log_dt": per_pair(np.repeat(v["l1_s5_log_dt"][:, None], S5_N, axis=1)),
        "b_re": per_pair(v["l1_s5_b_re"]), "b_im": per_pair(v["l1_s5_b_im"]),
        "c_re": per_pair(v["l1_s5_c_re"].transpose(0, 2, 1)), "c_im": per_pair(v["l1_s5_c_im"].transpose(0, 2, 1)),
    }
    ssd = []
    for g in range(SSD_G):
        o = order12[6 * g:6 * g + 6]
        ssd += [[22 + o[0]], [22 + o[1]], [22 + o[2], 22 + o[3]], [22 + o[4], 22 + o[5]]]
    ret = []
    for h in range(RET_H):
        ret += [[4 + h, 8 + h], [12 + 2 * h], [13 + 2 * h], [20 + 2 * h, 21 + 2 * h]]
    main = w_in[:, :4352]
    alone = [[j] for j in range(KD)]
    gates = [[j + KF * half] for j in range(KF) for half in (0, 1)]
    at = KH[0] * P
    arrays = {
        "x": v["x"], "con": con_, "con0": con0, "con1": con1_,
        "col0": np.concatenate([c0[n] for n, _ in COLS0], axis=1),
        "col1": np.concatenate([c1[n] for n, _ in COLS1], axis=1),
        "w2": v["l0_rwkv_w2"].reshape(64, 4, P), "a2": v["l0_rwkv_a2"].reshape(64, 4, P),
        "g2": v["l0_rwkv_g2"].reshape(P, 4, P),
        "w_lora": tiles_of(main, [[12, 13]]),
        "w_rwkv": tiles_of(main, [o for r in range(4) for o in ([r, 4 + r], [8 + r], [14 + 2 * r], [15 + 2 * r])]),
        "w_ssd": tiles_of(main, ssd),
        "w_out0": tiles_of(v["l0_w_out"], alone), "w_up0": tiles_of(v["l0_ffn_up"], gates),
        "w_down0a": tiles_of(v["l0_ffn_down"][:at], alone), "w_down0b": tiles_of(v["l0_ffn_down"][at:], alone),
        "w_u": tiles_of(v["l1_w_in"], [[0, 1], [2, 3]]), "w_ret": tiles_of(v["l1_w_in"], ret),
        "w_glu": tiles_of(v["l1_s5_w_glu"], [[0, 1], [2, 3]]),
        "w_out1": tiles_of(v["l1_w_out"], alone), "w_up1": tiles_of(v["l1_ffn_up"], gates),
        "w_down1a": tiles_of(v["l1_ffn_down"][:at], alone), "w_down1b": tiles_of(v["l1_ffn_down"][at:], alone),
    }
    arrays = {f"in_{k}": np.ascontiguousarray(x) for k, x in arrays.items()}
    nc = bacc.Bacc("TRN2", target_bir_lowering=False, num_devices=1)
    a = {k[3:]: nc.dram_tensor(k, x.shape, F32, kind="ExternalInput").ap() for k, x in arrays.items()}
    a["out"] = nc.dram_tensor("out_0", (1, T, D), F32, kind="ExternalOutput").ap()
    trunk(nc, a)
    r = run_bass_kernel_spmd(nc, [arrays], core_ids=[0])
    return r.results[0]["out_0"]
```

```python
from contextlib import ExitStack, contextmanager

import numpy as np

import concourse.bass as bass
from concourse import mybir

F32 = mybir.dt.float32
F32R = mybir.dt.float32r
ACT = mybir.ActivationFunctionType
ALU = mybir.AluOpType

P = 128
T = 512
D = 1024
KD = D // P
TT = T // P
EPS = 1e-6
SOFT = float(np.exp(-0.5))

H_RWKV, N_RWKV, CH = 8, 64, 64
NC = T // CH
GN_EPS = 64e-5
SSD_G, SSD_J, SSD_P = 2, 8, 64
S5_G, S5_CH, S5_N, S5_T = 32, 16, 64, 8
S5_C = T // S5_T
S5_PAIR = S5_G // 2
RET_H, DK, DV = 4, 128, 256
FH = 2816
KF = FH // P
KO = 12
SLOT = 16 * P
KH = (12, 10)

MAGIC = 12582912.0
INV_2PI = float(1.0 / (2.0 * np.pi))
PI_A = 6.28125
PI_B = float(np.float32(2.0 * np.pi - 6.28125))
PI_C = float(2.0 * np.pi - 6.28125 - float(np.float32(2.0 * np.pi - 6.28125)))
PI_MAX = 3.1415925

COLS0 = [("mix_g0", KD), ("mu", 14), ("w0", 4), ("a0", 4), ("k_k", 4), ("k_a", 4), ("r_k", 4), ("ln_g", 4),
         ("ln_b", 4), ("cw", 4 * 12), ("cb", 12), ("dt_bias", 64), ("a_log", 64), ("w_dt", 128), ("ssd_d", 8), ("ssd_g", 8),
         ("ffn_g0", KD), ("fcw0", 3 * 2 * KF), ("fcb0", 2 * KF), ("mix_g1", KD), ("s5_d", 4), ("b_glu", 4),
         ("ffn_g1", KD), ("fcw1", 3 * 2 * KF), ("fcb1", 2 * KF), ("final_g", KD)]
COLS1 = [("lam_re", 16), ("lam_im", 16), ("log_dt", 16), ("b_re", 256), ("b_im", 256), ("c_re", 256),
         ("c_im", 256)]
CONST = [("ident", P), ("ones", P), ("eps", 1), ("gn_eps", 1)]
CONST0 = [("bones", P), ("triu", P), ("strict", P), ("incl", P), ("level", 6 * P), ("ident2", 64), ("reset", T)]
CONST1 = [("cosq", T), ("sinq", T), ("cosk", T), ("sink", T), ("decay", RET_H * P), ("qdec", RET_H * P),
          ("kdec", RET_H), ("gchunk", RET_H)]


def offsets(parts):
    at, out = 0, {}
    for name, n in parts:
        out[name] = (at, n)
        at += n
    return out, at


O_COL0, N_COL0 = offsets(COLS0)
O_COL1, N_COL1 = offsets(COLS1)
O_CON, N_CON = offsets(CONST)
O_CON0, N_CON0 = offsets(CONST0)
O_CON1, N_CON1 = offsets(CONST1)


def constants():
    r = np.arange(P)
    s, t = r[:, None], r[None, :]
    same = (s // CH) == (t // CH)
    c = {
        "ident": np.eye(P), "ones": np.ones((P, P)), "eps": np.full((P, 1), EPS), "gn_eps": np.full((P, 1), GN_EPS), "bones": np.where(same, 1.0 / CH, 0.0),
        "triu": (s <= t), "strict": same & (s < t), "incl": same & (s <= t),
        "ident2": np.tile(np.eye(CH), (2, 1)),
        "reset": np.tile((np.arange(T) % CH != 0)[None, :], (P, 1)),
    }
    c["level"] = np.concatenate(
        [(s // (2 << l) == t // (2 << l)) & (s % (2 << l) < (1 << l)) & (t % (2 << l) >= (1 << l))
         for l in range(6)], axis=1)
    half = DK // 2
    theta = (1.0 / (10000.0 ** np.linspace(0.0, 1.0, half))).astype(np.float32)
    ang = (np.arange(T, dtype=np.float32)[None, :] * theta[:, None]).astype(np.float64)
    cos, sin = np.cos(ang), np.sin(ang)
    c["cosq"] = np.concatenate([cos, cos])
    c["sinq"] = np.concatenate([-sin, sin])
    c["cosk"], c["sink"] = c["cosq"] * DK ** -0.5, c["sinq"] * DK ** -0.5
    lg = np.log(1.0 - 2.0 ** (-5.0 - np.arange(RET_H)))
    c["decay"] = np.concatenate([np.where(s <= t, np.exp(np.maximum(t - s, 0) * g), 0.0) for g in lg], axis=1)
    c["qdec"] = np.concatenate([np.tile(np.exp((r + 1.0) * g)[None, :], (P, 1)) for g in lg], axis=1)
    c["kdec"] = np.stack([np.exp((P - 1.0 - r) * g) for g in lg], axis=1)
    c["gchunk"] = np.tile(np.exp(P * lg)[None, :], (P, 1))
    pack = lambda parts: np.concatenate([np.asarray(c[n], np.float32) for n, _ in parts], axis=1)
    return pack(CONST), pack(CONST0), pack(CONST1)


class Own:

    def __init__(self, eng, sem):
        self.eng, self.sem, self.base, self.k, self.i, self.per = eng, sem, 0, 0, None, 0

    def count(self):
        return self.base + self.k if self.i is None else self.base + self.per * self.i + self.k

    def go(self, ins):
        ins.then_inc(self.sem, 1)
        self.k += 1

    def wait(self):
        self.eng.wait_ge(self.sem, self.count())

    def do(self, ins):
        self.go(ins)
        self.wait()

    @contextmanager
    def loop(self, trips, per, start=0):
        self.base, self.k, self.per = self.base + self.k, 0, per
        with self.eng.Fori(start, start + trips) as i:
            self.i = i - start if start else i
            yield i
        assert self.k == per, f"the loop signals {self.k} results a turn, not {per}"
        self.base, self.k, self.i = self.base + per * trips, 0, None


STEPS = [("lora", 1), ("rwkv", 16), ("ssd", 8), ("out0", 8),
         ("up0a", 2 * KH[0]), ("down0a", 8), ("up0b", 2 * KH[1]), ("down0b", 8), ("u", 2), ("ret", 16), ("glu", 2),
         ("out1", 8), ("up1a", 2 * KH[0]), ("down1a", 8), ("up1b", 2 * KH[1]), ("down1b", 8)]
O_STEP, N_STEP = offsets(STEPS)
S0 = {k: v[0] for k, v in O_STEP.items()}
SPLIT_STEPS = KD + 2 * KF + 2 * KD


def slot_of(base, u, i=0, stride=2):
    return (base + u) % 2, (base + u) // 2 + stride // 2 * i


def mlp_bank(base, u):
    return 2 * ((base + u) % 2) + u // 2 % 2


def pieces_before(step):
    return sum(max(0, min(SPLIT_STEPS, step - S0[f"out{layer}"])) for layer in (0, 1))


def trunk(nc, a):
    ctx = ExitStack()
    with ctx:
        def sb(name, shape):
            return ctx.enter_context(nc.sbuf_tensor(name, shape, F32))

        def sem(name):
            return ctx.enter_context(nc.semaphore(name))

        x_t = sb("x_t", [P, KD, T])
        h_t = sb("h_t", [P, KD, T])
        wslot = sb("wslot", [P, 2, SLOT])
        col0 = sb("col0", [P, N_COL0])
        con = sb("con", [P, N_CON])
        rn = sb("rn", [P, T])
        spare = sb("spare", [P, 1])
        factors = sb("factors", [P, TT])
        N_UP = 12368
        upper = sb("upper", [P, N_UP])
        ps = ctx.enter_context(nc.psum_tensor("ps", [P, 8, 512], F32))
        mixers, mlps = ExitStack(), ExitStack()
        with mixers:
            y_t = mixers.enter_context(nc.sbuf_tensor("y_t", [P, KO, T], F32))
            con0 = mixers.enter_context(nc.sbuf_tensor("con0", [P, N_CON0], F32))
            dts = mixers.enter_context(nc.sbuf_tensor("dts", [P, 8, 64], F32))
            acc_t = mixers.enter_context(nc.sbuf_tensor("acc_t", [64, P], F32))
            N_LOW = 16600
            lower = mixers.enter_context(nc.sbuf_tensor("lower", [P, N_LOW], F32))
        with mlps:
            h_s = mlps.enter_context(nc.sbuf_tensor("h_s", [P, 2, KD, T], F32R))
            hid_s = mlps.enter_context(nc.sbuf_tensor("hid_s", [P, 2, KH[0], T], F32R))
            w_s = mlps.enter_context(nc.sbuf_tensor("w_s", [P, 2, 2, KH[0] * P], F32R))
        cg = h_t[:, 0:4, :].rearrange("p (a b) c -> p a b c", a=2)

        def C(name, j=0, n=1):
            return col0[:, O_COL0[name][0] + j:O_COL0[name][0] + j + n]

        def Cd(name, j):
            return col0[:, bass.ds(O_COL0[name][0] + j, 1)]

        def K(name):
            o, n = O_CON[name] if name in O_CON else O_CON0[name]
            return (con if name in O_CON else con0)[:, o:o + n]

        def split_of(v):
            return v.rearrange("p (a b) -> p a b", a=4)

        def carver(*rooms):
            at = [0] * len(rooms)

            def take(*dims):
                n = int(np.prod(dims))
                r = next(r for r, (_, size) in enumerate(rooms) if at[r] + n <= size)
                v = rooms[r][0][:, at[r]:at[r] + n]
                at[r] += n
                if len(dims) == 2:
                    v = v.rearrange("p (a b) -> p a b", a=dims[0])
                if len(dims) == 3:
                    v = v.rearrange("p (a b c) -> p a b c", a=dims[0], b=dims[1])
                return v
            return take

        take = carver((lower, N_LOW), (upper, N_UP))
        sw, ai, gate = take(4, T), take(4, T), take(4, T)
        pad = take(3, T + 1)
        rr, kq, vv, kk, pp, ip, bh, kh, zz, rd, bt, kt, bonus, tmp = (take(T) for _ in range(14))
        v_tok, b_tok, k_tok = (take(TT, P) for _ in range(3))
        at_, bt_, qb_, qk_, al_, tl, tu, xx = (take(8, P) for _ in range(8))
        rh, wn = take(8, P), take(8, P)
        gt, hh_, st = take(NC, 64), take(NC, 64), take(NC, 64)

        take = carver((lower, N_LOW))
        xs, xdt = take(4, T), take(TT, 512)
        acb = take(32, P)
        s_ssd = take(3, 512)
        yg = take(4, T)
        xdd, bc_f = take(TT, 512), take(2, T)
        b_tk, cbm = take(TT, P), take(TT, P)
        take = carver((upper, N_UP))
        seg = take(32, P)
        dte, cdk = take(32), take(32)

        take = carver((lower, N_LOW))
        con1 = take(N_CON1)
        gs, sq2 = take(2, T), take(2, T)
        qr, kr, qd, rm = (take(T) for _ in range(4))
        sm, k_tk = take(TT, P), take(TT, P)
        u_p = take(4, T)
        uc = take(S5_G, S5_C)
        toep = take(S5_G, P)
        flat = toep.rearrange("p a b -> p (a b)")
        y_gl, y_gate, y_in = split_of(flat[:, 0:4 * T]), split_of(flat[:, 4 * T:8 * T]), split_of(uc.rearrange("p a b -> p (a b)"))
        take = carver((upper, N_UP))
        col1 = take(N_COL1)
        v_tk = split_of(col1[:, 0:TT * DV])
        lam = take(24, 16)
        pw = take(2, S5_PAIR, 9)
        pwr = take(2, S5_PAIR, 8)
        bb = take(2, S5_PAIR, 16)
        ck = take(2, S5_PAIR, 144)
        wms = take(2 * S5_PAIR, P)
        wm, wm2, kker = wms[:, 0:S5_PAIR, :], wms[:, S5_PAIR:, :], wms
        s5_tmp = take(1152)
        s_ret = s5_tmp[:, 0:3 * DV].rearrange("p (a b) -> p a b", a=3)
        k_flat = wms.rearrange("p a b -> p (a b)")
        vin, xst = (k_flat[:, o:o + 2048].rearrange("p (c r q) -> p c r q", c=S5_C, r=2) for o in (0, 2048))
        xc = k_flat[:, 0:2048].rearrange("p (r a b) -> p r a b", r=2, a=S5_PAIR)
        yc = k_flat[:, 2048:4096].rearrange("p (g c) -> p g c", g=S5_G)
        y_ext = y_t[:, :, :].rearrange("p a b -> p (a b)")
        wt_r = y_ext[:, 0:S5_PAIR * P].rearrange("p (a b) -> p a b", a=S5_PAIR)
        wt_i = y_ext[:, 8 * T:8 * T + S5_PAIR * P].rearrange("p (a b) -> p a b", a=S5_PAIR)

        def K1(name, j=0, n=None):
            o, m = O_CON1[name]
            return con1[:, o + j:o + j + (m if n is None else n)]

        def K1d(name, j, n):
            return con1[:, bass.ds(O_CON1[name][0] + j, n)]

        def C1(name):
            o, n = O_COL1[name]
            return col1[:, o:o + n]

        x_in = h_t[:, :, :].rearrange("p a b -> p (a b)").rearrange("p (t d) -> p t d", t=TT)
        d_acc = nc.dram_tensor("d_acc", [64, P], F32, kind="Internal").ap()
        d_u = nc.dram_tensor("d_u", [512, 8, 64], F32, kind="Internal").ap()
        d_y = nc.dram_tensor("d_y", [512, 8, 64], F32, kind="Internal").ap()

        semaphores = {}

        def on(name):
            if name not in semaphores:
                semaphores[name] = ctx.enter_context(nc.semaphore(name))
            return semaphores[name]

        w_landed = [on("w_landed_0"), on("w_landed_1")]
        psum_free = [on("psum_free_0"), on("psum_free_1")]

        def bank(n, m=1):
            return ps[:, n, :] if m == 1 else ps[:, n:n + m, :]

        def split(v, n):
            return v.rearrange("p (a b) -> p a b", a=n)

        lora_banks = ((4, 5), (7, 1))

        row_banks = (4, 0, 2, 6)

        def over(v, n):
            return v.unsqueeze(2).broadcast_to([v.shape[0], v.shape[1], n])

        def each(v, n):
            return v.unsqueeze(1).broadcast_to([v.shape[0], n, v.shape[1]])

        block = ctx.enter_context(nc.Block())

        @block.sync
        def _(sp):
            sp.dma_start(con[:], a["con"]).then_inc(on("consts_in"), 16)
            for t in range(TT):
                sp.dma_start(x_in[:, t, :], a["x"].rearrange("b (t p) d -> (b t) p d", p=P)[t])\
                    .then_inc(on(f"x_loaded_{t}"), 16)
            sp.dma_start(col0[:], a["col0"]).then_inc(on("cols_in"), 16)

            def load(src, n, step, slot, first):
                if first in range(S0["out0"] + 2, S0["u"] + 2) or first >= S0["out1"] + 2:
                    sp.wait_ge(on("w_split"), step - first + pieces_before(first - 2) + 1)
                elif first >= 2:
                    sp.wait_ge(on("gemm_done"), step - 1)
                sp.dma_start(wslot[:, slot, 0:n], src).then_inc(w_landed[slot], 16)

            def stream(name, phase, n, skip=0):
                w, base, count = a[name], S0[phase], O_STEP[phase][1]
                u = 0
                while u < count and (u < 2 or (count - u) % 2):
                    load(w[skip + u], n, base + u, (base + u) % 2, base + u)
                    u += 1
                if count == u:
                    return
                with sp.Fori(0, (count - u) // 2) as i:
                    for v in (u, u + 1):
                        load(w[bass.ds(2 * i + v + skip, 1)].rearrange("a p n -> p (a n)"), n, base + v + 2 * i,
                             (base + v) % 2, base + v)

            def mlp(layer):
                for part, kh in enumerate(KH):
                    stream(f"w_up{layer}", f"up{layer}{'ab'[part]}", KD * P, 2 * KH[0] * part)
                    stream(f"w_down{layer}{'ab'[part]}", f"down{layer}{'ab'[part]}", kh * P)

            stream("w_lora", "lora", 2048)
            sp.dma_start(con0[:], a["con0"]).then_inc(on("consts0_in"), 16)
            for name, phase, n in (("w_rwkv", "rwkv", 2048), ("w_ssd", "ssd", 2048),
                                   ("w_out0", "out0", KO * P)):
                stream(name, phase, n)
            mlp(0)
            for name, phase, n in (("w_u", "u", 2048), ("w_ret", "ret", 2048), ("w_glu", "glu", 1024),
                                   ("w_out1", "out1", KO * P)):
                stream(name, phase, n)
            mlp(1)
            for t in range(TT):
                sp.wait_ge(on("rows_dve"), t + 1)
                sp.wait_ge(on("rows_act"), t + 1)
                sp.dma_start(a["out"].rearrange("b (t p) d -> (b t) p d", p=P)[t],
                             x_t[:, 2 * t:2 * t + 2, :].rearrange("p a b -> p (a b)")).then_inc(on("stored"), 16)
            sp.wait_ge(on("stored"), 16 * TT)

        @block.gpsimd
        def _(pool):
            own = Own(pool, on("pool_own"))
            pool.dma_start(at_[0:64, 0:4, :], a["w2"]).then_inc(on("lora_in"), 16)
            pool.dma_start(at_[64:128, 0:4, :], a["a2"]).then_inc(on("lora_in"), 16)
            pool.dma_start(bt_[:, 0:4, :], a["g2"]).then_inc(on("lora_in"), 16)
            pool.wait_ge(on("acc_turned"), 1)
            pool.dma_start(d_acc, acc_t[:, :]).then_inc(on("acc_stored"), 16)
            pool.wait_ge(on("acc_stored"), 16)
            for g in range(SSD_G):
                if g == 0:
                    pool.wait_ge(on("rwkv_head"), 4)
                else:
                    pool.wait_ge(on("ssd_y"), g)
                pool.dma_start(acb, d_acc[g * 32:(g + 1) * 32].unsqueeze(0).broadcast_to([P, 32, P]))\
                    .then_inc(on("acc_spread"), 16)
            pool.wait_ge(on("ssd_y"), SSD_G)
            pool.dma_start(col1, a["col1"]).then_inc(on("cols1_in"), 16)

            def split_weights(phase, kt):
                base, n = S0[phase], kt * P
                with own.loop(O_STEP[phase][1] // 2, 2) as i:
                    for u in (0, 1):
                        slot, _ = slot_of(base, u, i)
                        pool.wait_ge(on("w_high"), pieces_before(base) + u + 2 * i + 1)
                        own.do(pool.tensor_tensor(w_s[:, slot, 1, 0:n], wslot[:, slot, 0:n],
                                                  w_s[:, slot, 0, 0:n].bitcast(F32), ALU.subtract))
                        pool.sem_inc(on("w_split"), 1)

            def split_layer(layer):
                split_weights(f"out{layer}", KO)
                for part, kh in enumerate(KH):
                    split_weights(f"up{layer}{'ab'[part]}", KD)
                    split_weights(f"down{layer}{'ab'[part]}", kh)

            split_layer(0)
            TTo = pool.tensor_tensor
            pool.wait_ge(on("gemm_done"), S0["u"])
            pool.dma_start(con1, a["con1"]).then_inc(on("consts1_in"), 16)
            own.do(pool.memset(toep, 0.0))
            pool.wait_ge(on("u_ready"), 4)
            for i in range(4):
                pool.dma_start(d_u[i * P:(i + 1) * P].rearrange("p s c -> p (s c)"), u_p[:, i, :])\
                    .then_inc(on("u_stored"), 16)
            pool.wait_ge(on("u_stored"), 64)
            for s in range(S5_T):
                pool.dma_start(uc[s * 16:(s + 1) * 16, :, :],
                               d_u[:, s, :].rearrange("(g c) k -> c g k", c=16)).then_inc(on("u_spread"), 16)
            pool.wait_ge(on("kernels_out"), 2)
            for s in range(S5_T):
                pool.dma_start(toep[s * 16:(s + 1) * 16, :, s * 16:P], kker[0:16, :, 0:P - s * 16])\
                    .then_inc(on("kernels_spread"), 16)

            pool.wait_ge(on("vin_out"), 1)
            own.do(pool.memset(xst[:, 0, :, :], 0.0))
            own.do(pool.tensor_copy(xst[:, 1, :, :], vin[:, 0, :, :]))
            turn = lambda v, c: v[:, bass.ds(c, 1), :, :].rearrange("p a r q -> p (a r q)")
            keep_, cross = lam[:, 14:16, :].rearrange("p a b -> p (a b)"), lam[:, 18:20, :]
            with own.loop(S5_C - 2, 5) as c:
                x_c = xst[:, bass.ds(c + 1, 1), :, :].rearrange("p a r q -> p (a r) q")
                own.go(TTo(lam[:, 20:22, :].rearrange("p a b -> p (a b)"), turn(xst, c + 1), keep_, ALU.mult))
                own.go(TTo(cross[:, 0, :], x_c[:, 1, :], lam[:, 16, :], ALU.mult))
                own.go(TTo(cross[:, 1, :], x_c[:, 0, :], lam[:, 17, :], ALU.mult))
                own.wait()
                own.do(TTo(cross, cross, lam[:, 20:22, :], ALU.add))
                own.do(TTo(turn(xst, c + 2), cross.rearrange("p a b -> p (a b)"), turn(vin, c + 1), ALU.add))
            for ri in (0, 1):
                own.go(pool.tensor_copy(xc[:, ri, :, :], xst[:, :, ri, :].rearrange("p c q -> p q c")))
            own.wait()
            pool.sem_inc(on("s5_states"), 1)
            pool.wait_ge(on("s5_out"), 4)
            for t in range(S5_T):
                pool.dma_start(d_y[:, t, :].rearrange("(g c) k -> c g k", c=16), yc[t * 16:(t + 1) * 16, :, :])\
                    .then_inc(on("s5_stored"), 16)
            pool.wait_ge(on("s5_stored"), 16 * S5_T)
            for i in range(4):
                pool.dma_start(y_in[:, i, :], d_y[i * P:(i + 1) * P].rearrange("p s c -> p (s c)"))\
                    .then_inc(on("s5_back"), 16)
            pool.wait_ge(on("s5_back"), 64)
            pool.wait_ge(on("glu_out"), 4)
            split_layer(1)

        @block.scalar
        def _(act):
            own = Own(act, on("act_own"))

            def tables_of(function):
                own.do(act.activation(spare[:], K("eps"), function))

            def root(summed, n, src, scale, eps, read, done):
                tables_of(ACT.Ln)
                act.wait_ge(on(summed), n)
                own.do(act.activation(rn[:], src, ACT.Ln, scale=scale, bias=K(eps)))
                if read:
                    act.sem_inc(on(read), 1)
                own.do(act.activation(rn[:], rn[:], ACT.Exp, scale=-0.5))
                act.sem_inc(on(done), 1)

            def norm(n, between=None):
                for k in range(KD):
                    act.wait_ge(on("x_ready"), KD * n + k + 1)
                    own.go(act.activation(h_t[:, k, :], x_t[:, k, :], ACT.Square))
                    own.wait()
                    act.sem_inc(on("squares"), 1)
                if between:
                    between()
                root("norm_sum", n + 1, bank(7), 1.0 / D, "eps", "norm_read", "norm_root")

            def high(phase, u, i=0, stride=2):
                base, n = S0[phase], (KD if "up" in phase else KH["b" in phase]) * P
                slot, before = slot_of(base, u, i, stride)
                act.wait_ge(w_landed[slot], 16 * (before + 1))
                act.wait_ge(on("gemm_done"), base + u + stride * i - 1)
                own.do(act.activation(w_s[:, slot, 0, 0:n], wslot[:, slot, 0:n], ACT.Copy))
                act.sem_inc(on("w_high"), 1)

            def norm_split(n, phase):
                norm(n, lambda: [high(phase, u) for u in (0, 1)])
                for k in range(KD):
                    act.wait_ge(on("h_whole"), KD * (n // 2) + k + 1)
                    own.do(act.activation(h_s[:, 0, k, :], h_t[:, k, :], ACT.Copy))
                    act.sem_inc(on("h_high"), 1)

            def up(layer, part):
                phase, down = (f"{name}{layer}{'ab'[part]}" for name in ("up", "down"))
                base, first = S0[phase], KH[0] * part

                def turn(i, last):
                    for v in (0, 1):
                        pair = layer * KF + first + v + 2 * i
                        def ahead(u):
                            if last and v:
                                high(down, u)
                            else:
                                high(phase, 2 * v + 2 + u, i, 4)

                        end = last and v == 1
                        ahead(0)
                        if not end:
                            ahead(1)
                        act.wait_ge(on("gemm_done"), base + 2 * v + 4 * i + 2)
                        act.wait_ge(on("cg_read"), pair + 1)
                        for half in (0, 1):
                            j = first + v + 2 * i + KF * half
                            own.go(act.activation(cg[:, v, half, :], bank(mlp_bank(base, 2 * v + half)), ACT.Identity,
                                                  scale=Cd(f"fcw{layer}", j + 2 * 2 * KF), bias=Cd(f"fcb{layer}", j)))
                        own.wait()
                        act.sem_inc(on("mlp_affine"), 1)
                        if end:
                            ahead(1)
                        act.wait_ge(on("mlp_conv"), pair + 1)
                        own.do(act.activation(cg[:, v, 0, :], cg[:, v, 0, :], ACT.Silu))
                        act.sem_inc(on("mlp_gate"), 1)

                tables_of(ACT.Silu)
                with own.loop(KH[part] // 2 - 1, 10) as i:
                    turn(i, False)
                turn(KH[part] // 2 - 1, True)

            def highs(phase):
                with own.loop(KD // 2 - 1, 2) as i:
                    for u in (2, 3):
                        high(phase, u, i)

            def down(layer, part):
                highs(f"down{layer}{'ab'[part]}")
                if part == 0:
                    for u in (0, 1):
                        high(f"up{layer}b", u)

            def high_y(first, last):
                for k in range(first, last):
                    own.do(act.activation(hid_s[:, 0, k, :], y_t[:, k, :], ACT.Copy))
                    act.sem_inc(on("y_high"), 1)

            act.wait_ge(on("consts_in"), 16)
            norm(0)
            act.wait_ge(on("cols_in"), 16)

            for j in range(3):
                own.do(act.activation(pad[:, j, 0:1], col0[:, 0:1], ACT.Copy, scale=0.0))
            act.wait_ge(on("gemm_done"), 1)
            for j in (0, 1):
                own.do(act.activation(pad[:, j, 1:T + 1], bank(j), ACT.Copy))
            act.sem_inc(psum_free[0], 1)
            act.sem_inc(on("lora_pad"), 1)
            act.wait_ge(on("lora_mixed"), 1)
            own.do(act.activation(rr[0:64], kq[0:64], ACT.Tanh))
            own.do(act.activation(rr[64:128], kq[64:128], ACT.Copy))
            own.do(act.activation(vv[:], kk[:], ACT.Sigmoid))
            act.sem_inc(on("lora_acts"), 1)
            act.wait_ge(on("dt_abs"), 1)
            own.do(act.activation(dts[:, 1, :], dts[:, 1, :], ACT.Exp, scale=-1.0))
            own.do(act.activation(dts[:, 2, :], dts[:, 1, :], ACT.Ln, bias=1.0))
            own.do(act.activation(dts[:, 3, :], C("a_log", 0, 64), ACT.Exp))
            act.sem_inc(on("dt_exp"), 1)

            for j in range(4):
                act.wait_ge(on("lora_w"), j + 1)
                own.do(act.activation(sw[:, j, :], bank(lora_banks[j % 2][0]), ACT.Sigmoid, bias=C("w0", j)))
                own.do(act.activation(ai[:, j, :], bank(lora_banks[j % 2][1]), ACT.Sigmoid, bias=C("a0", j)))
                act.sem_inc(on("lora_w_out"), 1)

            base = S0["rwkv"]
            with own.loop(4, 32) as r:
                act.wait_ge(on("gemm_done"), base + 4 * r + 1)
                act.wait_ge(on("pads_read"), r + 1)
                for j in (0, 1):
                    own.do(act.activation(pad[:, j, 1:T + 1], bank(2 + j), ACT.Copy))
                act.sem_inc(psum_free[1], 1)
                act.sem_inc(on("rk_pad"), 1)
                act.wait_ge(on("gemm_done"), base + 4 * r + 2)
                own.do(act.activation(pad[:, 2, 1:T + 1], bank(0), ACT.Copy))
                act.sem_inc(psum_free[0], 1)
                act.sem_inc(on("v_pad"), 1)
                act.wait_ge(on("log_decay"), r + 1)
                own.do(act.activation(pp[:], zz[:], ACT.Exp, scale=-SOFT))
                own.do(act.activation(ip[:], zz[:], ACT.Exp, scale=SOFT))
                act.sem_inc(on("decays"), 1)
                tables_of(ACT.Ln)
                act.wait_ge(on("kk_var"), r + 1)
                own.do(act.activation(rn[:], rn[:], ACT.Ln))
                own.do(act.activation(rn[:], rn[:], ACT.Exp, scale=-0.5))
                act.sem_inc(on("kk_root"), 1)
                for v, par in ((0, 1), (1, 0)):
                    act.wait_ge(on("gemm_done"), base + 4 * r + 3 + v)
                    own.do(act.activation(y_t[:, bass.ds(4 + 2 * r + v, 1), :].rearrange("p a b -> p (a b)"),
                                          bank(2 * par), ACT.Silu))
                    act.sem_inc(psum_free[par], 1)
                    act.sem_inc(on("z_out"), 1)
                act.wait_ge(on("tok_turned"), r + 1)
                for hd in (0, 1):
                    own.do(act.activation(rh[:, 4 * hd:4 * hd + 4, 0:64],
                                          split(bank(0), 4)[:, :, 64 * hd:64 * hd + 64], ACT.Copy))
                own.do(act.activation(v_tok, split(bank(1), 4), ACT.Copy))
                own.do(act.activation(b_tok, split(bank(2), 4), ACT.Copy))
                own.do(act.activation(k_tok, split(bank(3), 4), ACT.Copy))
                act.sem_inc(on("toks"), 1)
                act.wait_ge(on("bv_done"), r + 1)
                own.do(act.activation(rh[:, :, 64:128], split(bank(0), 8), ACT.Copy))
                act.sem_inc(on("rhs_ready"), 1)
                for level in range(1, 6):
                    for hd in (0, 1):
                        act.wait_ge(on("x_done"), 12 * r + 2 * level + hd + 1)
                        own.do(act.activation(xx[:, 4 * hd:4 * hd + 4, :], split(bank(2 + hd), 4), ACT.Copy))
                        act.sem_inc(on("x_out"), 1)
                for half in (0, 1):
                    act.wait_ge(on("wu_done"), 2 * r + half + 1)
                    own.do(act.activation(wn[:, 4 * half:4 * half + 4, :], split(bank(6 + half), 4), ACT.Copy,
                                          scale=-1.0))
                act.sem_inc(on("wn_ready"), 1)
                act.wait_ge(on("gn_dev"), r + 1)
                own.do(act.activation(tmp[:], kk[:], ACT.Square))
                act.sem_inc(on("gn_sq"), 1)
                root("gn_sum", r + 1, bank(0), 1.0, "gn_eps", "gn_read", "gn_root")

            base = S0["ssd"]
            ssd_tiles = [[(bc_f[:, 0, :], 0)], [(bc_f[:, 1, :], 1)], [(xs[:, 0, :], 2), (xs[:, 1, :], 3)],
                         [(xs[:, 2, :], 4), (xs[:, 3, :], 5)]]

            def affine(n):
                act.wait_ge(on("gemm_done"), base + n + 1)
                slot, _ = slot_of(base, n)
                for m, (dst, j) in enumerate(ssd_tiles[n % 4]):
                    own.go(act.activation(dst, bank(2 * slot + m), ACT.Identity,
                                          scale=C("cw", 3 * 12 + 6 * (n // 4) + j), bias=C("cb", 6 * (n // 4) + j)))
                own.wait()
                act.sem_inc(on("ssd_affine"), 1)

            def silu(n):
                act.wait_ge(on("ssd_conv"), n + 1)
                for dst, _ in ssd_tiles[n % 4]:
                    own.go(act.activation(dst, dst, ACT.Silu))
                own.wait()
                act.sem_inc(on("xbc_ready"), 1)

            act.wait_ge(on("rwkv_head"), 4)
            affine(0)
            affine(1)
            silu(0)
            silu(1)
            for g in range(SSD_G):
                affine(4 * g + 2)
                silu(4 * g + 2)
                act.wait_ge(on("ssd_logs"), g + 1)
                own.do(act.activation(dte, dte, ACT.Exp))
                act.sem_inc(on("ssd_ends"), 1)
                affine(4 * g + 3)
                silu(4 * g + 3)
                own.do(act.activation(seg.rearrange("p a b -> p (a b)"), seg.rearrange("p a b -> p (a b)"), ACT.Exp))
                own.do(act.activation(acb.rearrange("p a b -> p (a b)"), acb.rearrange("p a b -> p (a b)"), ACT.Exp))
                act.sem_inc(on("ssd_exps"), 1)
                if g == 0:
                    for n in (4, 5):
                        affine(n)
                        silu(n)
                if g == SSD_G - 1:
                    act.wait_ge(on("ssd_new"), SSD_G)
                    act.wait_ge(on("ssd_masks"), SSD_G)
                    for u in (0, 1):
                        high("out0", u)
                for i in range(4):
                    act.wait_ge(on("yg_ready"), 4 * g + i + 1)
                    own.do(act.activation(xs[:, i, :], yg[:, i, :], ACT.Square))
                    act.sem_inc(on("yg_sq"), 1)
                root("ssd_sum", g + 1, bank(4), 1.0 / 512, "eps", None, "ssd_root")

            high_y(0, 8)
            act.wait_ge(on("ssd_group"), SSD_G)
            high_y(8, KO)
            highs("out0")
            norm_split(1, "up0a")
            up(0, 0)

            act.wait_ge(on("cols1_in"), 16)
            own.do(act.activation(lam[:, 0, :], C1("log_dt"), ACT.Exp))
            act.sem_inc(on("s5_dt"), 1)
            act.wait_ge(on("s5_angle"), 1)
            own.do(act.activation(lam[:, 1, :], lam[:, 1, :], ACT.Exp))
            own.do(act.activation(lam[:, 3, :], lam[:, 2, :], ACT.Sin))
            own.do(act.activation(lam[:, 4, :], lam[:, 2, :], ACT.Sin, scale=0.5))
            act.sem_inc(on("s5_trig"), 1)
            down(0, 0)
            up(0, 1)
            down(0, 1)
            norm(2)

            for half, dst in ((0, wt_r), (1, wt_i)):
                act.wait_ge(on("wm_turned"), half + 1)
                for b in range(4):
                    own.do(act.activation(dst[:, 4 * b:4 * b + 4, :], split(bank(4 + b), 4), ACT.Copy))
                act.sem_inc(on("wm_out"), 1)
            for half in (0, 1):
                act.wait_ge(on("kernels_done"), half + 1)
                for b in range(4):
                    eight = kker[0:16, 16 * half + 8 * (b % 2):16 * half + 8 * (b % 2) + 8, :]
                    own.do(act.activation(eight.rearrange("p (g o) c -> p g o c", o=2)[:, :, b // 2, :],
                                          split(bank(4 + b), 4)[0:16], ACT.Copy))
                act.sem_inc(on("kernels_out"), 1)

            base = S0["ret"]
            act.wait_ge(on("consts1_in"), 16)
            for h in range(RET_H):
                if h == 3:
                    act.wait_ge(on("s5_y"), 1)
                    for b in range(4):
                        every_other = yc[:, 16 * (b % 2):16 * (b % 2) + 16, :].rearrange("p (g o) c -> p g o c", o=2)
                        own.do(act.activation(every_other[:, :, b // 2, :], split(bank(4 + b), 8), ACT.Copy))
                        act.sem_inc(on("s5_out"), 1)
                act.wait_ge(on("ret_read"), h + 1)
                for v in (0, 1):
                    act.wait_ge(on("gemm_done"), base + 1 + v + 4 * h + 1)
                    slot, _ = slot_of(base, 1 + v)
                    own.do(act.activation(v_tk[:, :, v * P:(v + 1) * P], split(bank(2 * slot), 4), ACT.Copy))
                    act.sem_inc(psum_free[slot], 1)
                act.sem_inc(on("v_tok_ready"), 1)
                act.wait_ge(on("gemm_done"), base + 3 + 4 * h + 1)
                slot, _ = slot_of(base, 3)
                for m in (0, 1):
                    own.do(act.activation(gs[:, m, :], bank(2 * slot + m), ACT.Silu))
                act.sem_inc(psum_free[slot], 1)
                act.sem_inc(on("gs_ready"), 1)
                if h == 0:
                    act.wait_ge(on("kernels_spread"), 16 * S5_T)
                    act.wait_ge(on("vin_done"), 1)
                    for ri in (0, 1):
                        for b in (0, 1):
                            own.do(act.activation(vin[:, :, ri, 8 * b:8 * b + 8],
                                                  split(bank(4 + 2 * ri + b), 8).rearrange("p q c -> p c q"), ACT.Copy))
                    act.sem_inc(on("vin_out"), 1)
                if h == 3:
                    for i in range(4):
                        act.wait_ge(on("s5_skip"), i + 1)
                        own.do(act.activation(y_gl[:, i, :].rearrange("p (c s) -> p s c", s=S5_T), split(y_in[:, i, :], S5_T),
                                              ACT.Gelu_apprx_tanh))
                        act.sem_inc(on("gelu_ready"), 1)
                    for u in (0, 1):
                        slot, _ = slot_of(S0["glu"], u)
                        act.wait_ge(on("gemm_done"), S0["glu"] + u + 1)
                        for m in (0, 1):
                            own.do(act.activation(y_gate[:, 2 * u + m, :], bank(2 * slot + m), ACT.Sigmoid,
                                                  bias=C("b_glu", 2 * u + m)))
                        act.sem_inc(psum_free[slot], 1)
                        act.sem_inc(on("glu_gate"), 1)
                act.wait_ge(on("scores_done"), h + 1)
                own.do(act.activation(k_tk, split(bank(5), 4), ACT.Copy, scale=K1("kdec", h, 1)))
                act.sem_inc(on("k_tok_ready"), 1)
                if h == 3:
                    act.wait_ge(on("glu_out"), 4)
                    for u in (0, 1):
                        high("out1", u)
                act.wait_ge(on("ret_y"), h + 1)
                for m in (0, 1):
                    own.do(act.activation(sq2[:, m, :], bank(4 + m), ACT.Square))
                act.sem_inc(on("ret_sq"), 1)
                root("ret_sum", h + 1, bank(6), 1.0 / DV, "eps", None, "ret_root")

            high_y(0, N_CON1 // T)
            act.wait_ge(on("ret_head"), RET_H)
            high_y(N_CON1 // T, KO)
            highs("out1")
            norm_split(3, "up1a")
            for part in (0, 1):
                up(1, part)
                down(1, part)
            norm(4)
            for t in range(TT):
                act.wait_ge(on("rows_turned"), t + 1)
                act.wait_ge(on("factors_ready"), 1)
                own.do(act.activation(x_t[:, 2 * t + 1, :], bank(row_banks[t] + 1), ACT.Copy, scale=factors[:, t:t + 1]))
                act.sem_inc(on("rows_act"), 1)

        @block.tensor
        def _(pe):
            ones, ident, bones = K("ones"), K("ident"), K("bones")

            def begin(base, u, i=0, stride=2):
                slot, before = slot_of(base, u, i, stride)
                pe.wait_ge(w_landed[slot], 16 * (before + 1))
                if base + u >= 2:
                    pe.wait_ge(psum_free[slot], before)
                return slot

            def h_tile(n):
                return lambda k: pe.wait_ge(on("h_ready"), KD * n + k + 1)

            def product(base, u, i, stride, kt_, rhs, tiles=2, before_k=None):
                slot = begin(base, u, i, stride)
                w = wslot[:, slot, 0:tiles * kt_ * P].rearrange("p (m k c) -> p m k c", m=tiles, k=kt_)
                for m in range(tiles):
                    for k in range(kt_):
                        if before_k and m == 0:
                            before_k(k)
                        mm = pe.matmul(bank(2 * slot + m), w[:, m, k, :], rhs(k), start=k == 0, stop=k == kt_ - 1)
                mm.then_inc(on("gemm_done"), 1)

            h_of = lambda k: h_t[:, k, :]

            def product_split(base, u, i, stride, kt_, operand, before_k=None):
                slot, before = slot_of(base, u, i, stride)
                pe.wait_ge(on("w_split"), pieces_before(base) + u + stride * i + 1)
                pe.wait_ge(psum_free[slot], before - 1)
                out = bank(mlp_bank(base, u))
                for k in range(kt_):
                    if before_k:
                        before_k(k)
                    high, low = (w_s[:, slot, part, k * P:(k + 1) * P] for part in (0, 1))
                    pe.matmul(out, high, operand[:, 0, k, :], start=k == 0, stop=False)
                    pe.matmul(out, high, operand[:, 1, k, :], start=False, stop=False)
                    mm = pe.matmul(out, low, operand[:, 0, k, :], start=False, stop=k == kt_ - 1)
                mm.then_inc(on("gemm_done"), 1)

            def norm(n):
                for k in range(KD):
                    pe.wait_ge(on("squares"), KD * n + k + 1)
                    mm = pe.matmul(bank(7), ones, h_t[:, k, :], start=k == 0, stop=k == KD - 1)
                mm.then_inc(on("norm_sum"), 1)

            def mlp(layer):
                for part, kh in enumerate(KH):
                    up, down = (S0[f"{name}{layer}{'ab'[part]}"] for name in ("up", "down"))
                    with pe.Fori(0, kh // 2) as i:
                        for u in range(4):
                            product_split(up, u, i, 4, KD, h_s, h_tile(1 + 2 * layer))

                    def hidden(k):
                        if k in (0, kh - 1):
                            pe.wait_ge(on("hid_ready"), KF * layer + KH[0] * part + kh - (k == 0))

                    with pe.Fori(0, KD // 4) as i:
                        for u in range(4):
                            product_split(down, u, i, 4, kh, hid_s, hidden)

            def project_out(layer):
                with pe.Fori(0, KD // 4) as i:
                    for u in range(4):
                        product_split(S0[f"out{layer}"], u, i, 4, KO, hid_s,
                                      lambda k: pe.wait_ge(on("y_split"), KO * layer + k + 1))

            pe.wait_ge(on("consts_in"), 16)
            for t in range(TT):
                pe.wait_ge(on(f"x_loaded_{t}"), 16)
                for k in range(KD):
                    pe.transpose(ps[:, k, t * P:(t + 1) * P], x_in[:, t, k * P:(k + 1) * P], ident)\
                        .then_inc(on("x_turned"), 1)
            pe.wait_ge(on("x_ready"), KD)
            norm(0)

            product(S0["lora"], 0, 0, 2, KD, h_of, 2, h_tile(0))
            pe.wait_ge(on("cols_in"), 16)
            wdt = C("w_dt", 0, 128).rearrange("p (k h) -> p k h", k=KD)
            for t in range(TT):
                for k in range(KD):
                    mm = pe.matmul(ps[:, 6, t * 16:(t + 1) * 16], h_t[:, k, t * P:(t + 1) * P], wdt[:, k, :],
                                   start=k == 0, stop=k == KD - 1)
            mm.then_inc(on("dt_sum"), 1)
            pe.wait_ge(on("lora_acts"), 1)
            pe.wait_ge(on("lora_in"), 48)
            for j in range(4):
                if j >= 2:
                    pe.wait_ge(on("lora_w_out"), j - 1)
                b, c = lora_banks[j % 2]
                pe.matmul(bank(b), at_[0:64, j, :], rr[0:64], start=True, stop=True)
                pe.matmul(bank(c), at_[64:128, j, :], rr[64:128], start=True, stop=True)\
                    .then_inc(on("lora_w"), 1)
            for j in range(4):
                if j >= 2:
                    pe.wait_ge(on("lora_g_out"), j - 1)
                pe.matmul(bank(2 + j % 2), bt_[:, j, :], vv[:], start=True, stop=True).then_inc(on("lora_g"), 1)
            pe.wait_ge(on("lora_g_out"), 4)
            pe.wait_ge(on("dt_rates"), 1)
            pe.wait_ge(on("consts0_in"), 16)
            pe.matmul(ps[:, 6, 0:64], K("triu"), dts[:, 5, :], start=True, stop=True).then_inc(on("acc_sum"), 1)
            pe.wait_ge(on("acc_ready"), 1)
            pe.transpose(ps[0:64, 6, 0:P], dts[:, 6, :], ident).then_inc(on("acc_turn"), 1)
            pe.wait_ge(on("acc_turned"), 1)

            base = S0["rwkv"]
            pairs = [(hd, t) for hd in (0, 1) for t in range(TT)]

            def mat(b0, m):
                return ps[:, b0 + m // 4, (m % 4) * P:(m % 4 + 1) * P]

            with pe.Fori(0, 4) as r:
                product(base, 0, r, 4, KD, h_of)
                pe.wait_ge(on("gn_read"), r + 1)
                product(base, 1, r, 4, KD, h_of, 1)
                pe.wait_ge(on("kk_sq"), r + 1)
                pe.matmul(bank(4), bones, tmp[:], start=True, stop=True).then_inc(on("kk_sum"), 1)
                product(base, 2, r, 4, KD, h_of, 1)
                product(base, 3, r, 4, KD, h_of, 1)
                pe.wait_ge(on("z_out"), 2 * r + 2)
                pe.wait_ge(on("keys"), r + 1)
                for hd in (0, 1):
                    lo, hi = 64 * hd, 64 * hd + 64
                    for b, (lh, rhs_) in enumerate(((bh, zz), (kh, zz), (bh, rd), (kh, rd))):
                        for t in range(TT):
                            mm = pe.matmul(ps[:, 4 * hd + b, t * P:(t + 1) * P], lh[lo:hi, t * P:(t + 1) * P],
                                           rhs_[lo:hi, t * P:(t + 1) * P], start=True, stop=True)
                    mm.then_inc(on("grams"), 1)
                pe.wait_ge(on("tails"), r + 1)
                pe.wait_ge(on("grams_out"), 2 * r + 1)
                for b, src in enumerate((zz, vv, bt, kt)):
                    for t in range(TT):
                        mm = pe.transpose(ps[:, b, t * P:(t + 1) * P], src[:, t * P:(t + 1) * P], ident)
                mm.then_inc(on("tok_turned"), 1)
                for hd in (0, 1):
                    pe.wait_ge(on("al_ready"), 12 * r + hd + 1)
                    for m in range(4 * hd, 4 * hd + 4):
                        mm = pe.matmul(mat(4, m), al_[:, m, :], ident, start=True, stop=True)
                    mm.then_inc(on("x_done"), 1)
                pe.wait_ge(on("toks"), r + 1)
                for m, (hd, t) in enumerate(pairs):
                    mm = pe.matmul(ps[:, 0, m * 64:(m + 1) * 64], bt_[:, m, :], v_tok[:, t, 64 * hd:64 * hd + 64],
                                   start=True, stop=True)
                mm.then_inc(on("bv_done"), 1)
                for level in range(1, 6):
                    for hd in (0, 1):
                        pe.wait_ge(on("al_ready"), 12 * r + 2 * level + hd + 1)
                        for m in range(4 * hd, 4 * hd + 4):
                            mm = pe.matmul(mat(2, m), al_[:, m, :], tl[:, m, :], start=True, stop=True)
                        mm.then_inc(on("x_done"), 1)
                    for hd in (0, 1):
                        if level > 1:
                            pe.wait_ge(on("t_ready"), 8 * r + 2 * (level - 2) + hd + 1)
                        pe.wait_ge(on("x_out"), 10 * r + 2 * (level - 1) + hd + 1)
                        if level < 5:
                            for m in range(4 * hd, 4 * hd + 4):
                                pe.matmul(mat(6, m), tu[:, m, :], xx[:, m, :], start=True, stop=True)
                        for m in range(4 * hd, 4 * hd + 4):
                            mm = pe.matmul(mat(4, m), xx[:, m, :], tu[:, m, :], start=True, stop=True)
                        mm.then_inc(on("tx_done"), 1)
                pe.wait_ge(on("rhs_ready"), r + 1)
                for hd in (0, 1):
                    pe.wait_ge(on("tu_ready"), 2 * r + hd + 1)
                    for m in range(4 * hd, 4 * hd + 4):
                        mm = pe.matmul(mat(6, m), tu[:, m, :], rh[:, m, :], start=True, stop=True)
                    mm.then_inc(on("wu_done"), 1)
                pe.wait_ge(on("wn_ready"), r + 1)
                for m, (hd, t) in enumerate(pairs):
                    lo, hi = 64 * hd, 64 * hd + 64
                    pe.matmul(ps[lo:hi, 4, t * P:(t + 1) * P], wn[:, m, 0:64], qb_[:, m, :], start=True, stop=True)
                    for q in (0, 1):
                        c, ql, qh = 2 * t + q, 64 * q, 64 * q + 64
                        pe.matmul(ps[lo:hi, 5 + q, c * 64:(c + 1) * 64], wn[ql:qh, m, 0:64], b_tok[ql:qh, t, lo:hi],
                                  start=True, stop=True)
                        pe.matmul(ps[lo:hi, 7 * q, c * 64:(c + 1) * 64], b_tok[ql:qh, t, lo:hi], wn[ql:qh, m, 64:128],
                                  start=True, stop=False)
                        mm = pe.matmul(ps[lo:hi, 7 * q, c * 64:(c + 1) * 64], k_tok[ql:qh, t, lo:hi],
                                       v_tok[ql:qh, t, lo:hi], start=False, stop=True)
                mm.then_inc(on("chunk_maps"), 1)
                pe.matmul(bank(3), bones, bonus[:], start=True, stop=True).then_inc(on("bonus_sum"), 1)
                for c in range(1, NC - 1):
                    pe.wait_ge(on("state_ready"), (NC - 1) * r + c)
                    pe.sem_inc(on("state_seen"), 1)
                    for lo in (0, 64):
                        mm = pe.matmul(ps[lo:lo + 64, 1, c * 64:(c + 1) * 64], gt[lo:lo + 64, c, :],
                                       st[lo:lo + 64, c, :], start=True, stop=True)
                    mm.then_inc(on("state_moved"), 1)
                pe.wait_ge(on("state_ready"), (NC - 1) * (r + 1))
                for m, (hd, t) in enumerate(pairs):
                    lo, hi = 64 * hd, 64 * hd + 64
                    out = ps[lo:hi, 2, t * P:(t + 1) * P]
                    pe.matmul(out, v_tok[:, t, lo:hi], qk_[:, m, :], start=True, stop=False)
                    mm = pe.matmul(out, wn[:, m, 64:128], qb_[:, m, :], start=False, stop=True)
                    for q in (0, 1):
                        c = 2 * t + q
                        if c:
                            mm = pe.matmul(ps[lo:hi, 2, c * 64:(c + 1) * 64], st[lo:hi, c, :],
                                           rd[lo:hi, c * 64:(c + 1) * 64], start=False, stop=True,
                                           skip_group_check=True)
                mm.then_inc(on("rwkv_y"), 1)
                pe.wait_ge(on("gn_in"), r + 1)
                pe.matmul(bank(6), bones, kk[:], start=True, stop=True).then_inc(on("gn_mean"), 1)
                pe.wait_ge(on("gn_sq"), r + 1)
                pe.matmul(bank(0), bones, tmp[:], start=True, stop=True).then_inc(on("gn_sum"), 1)
            base = S0["ssd"]

            def ssd_step(n):
                product(base, n, 0, 2, KD, h_of, (1, 1, 2, 2)[n % 4])

            ssd_step(0)
            pe.wait_ge(on("gn_read"), 5)
            ssd_step(1)
            ssd_step(2)
            for g in range(SSD_G):
                pe.wait_ge(on("xbc_ready"), 4 * g + 2)
                if g:
                    pe.wait_ge(on("ssd_root"), g)
                for t in range(TT):
                    tok = slice(t * P, (t + 1) * P)
                    pe.matmul(ps[:, 4, tok], bc_f[:, 0, tok], bc_f[:, 1, tok], start=True, stop=True)
                    mm = pe.transpose(ps[:, 5, tok], bc_f[:, 0, tok], ident)
                mm.then_inc(on("cb_done"), 1)
                ssd_step(4 * g + 3)
                pe.wait_ge(on("cb_out"), g + 1)
                pe.wait_ge(on("xbc_ready"), 4 * g + 4)
                for t in range(TT):
                    for i in range(4):
                        mm = pe.transpose(ps[:, 4 + t, i * P:(i + 1) * P], xs[:, i, t * P:(t + 1) * P], ident)
                mm.then_inc(on("xs_turned"), 1)
                if g == 0:
                    ssd_step(4)
                pe.wait_ge(on("xd_ready"), g + 1)
                for t in range(TT - 1):
                    mm = pe.matmul(bank(4 + t), b_tk[:, t, :], xdd[:, t, :], start=True, stop=True)
                mm.then_inc(on("ssd_new"), 1)
                if g == 0:
                    ssd_step(5)
                pe.wait_ge(on("ssd_state"), g + 1)
                pe.wait_ge(on("ssd_masks"), g + 1)
                for i in range(4):
                    for t in range(TT):
                        for hd in (0, 1):
                            j = 2 * i + hd
                            out = ps[64 * hd:64 * hd + 64, 4 + i, t * P:(t + 1) * P]
                            mm = pe.matmul(out, xdt[:, t, j * 64:(j + 1) * 64], seg[:, t * 8 + j, :],
                                           start=True, stop=t == 0)
                            if t:
                                mm = pe.matmul(out, s_ssd[:, t - 1, j * 64:(j + 1) * 64], acb[:, t * 8 + j, :],
                                               start=False, stop=True)
                mm.then_inc(on("ssd_y"), 1)
                if g == 0:
                    ssd_step(6)
                for i in range(4):
                    pe.wait_ge(on("yg_sq"), 4 * g + i + 1)
                    if i == 0:
                        pe.wait_ge(on("yg_ready"), 4 * g + 4)
                    mm = pe.matmul(bank(4), ones, xs[:, i, :], start=i == 0, stop=i == 3)
                mm.then_inc(on("ssd_sum"), 1)

            project_out(0)
            norm(1)
            mlp(0)
            norm(2)

            def turn_wm(half):
                pe.wait_ge(on("wm_ready"), 1)
                pe.wait_ge(on("norm_read"), 3)
                if half:
                    pe.wait_ge(on("wm_out"), 1)
                for q in range(S5_PAIR):
                    mm = pe.transpose(mat(4, q), (wm, wm2)[half][:, q, :], ident)
                mm.then_inc(on("wm_turned"), 1)

            def kernels(half):
                pe.wait_ge(on("wm_out"), 2)
                pe.wait_ge(on("ck_ready"), 1)
                if half:
                    pe.wait_ge(on("kernels_out"), 1)
                for n in range(16):
                    g = 16 * half + n
                    q, lo = g // 2, 64 * (g % 2)
                    out = ps[0:16, 4 + 2 * (n % 2) + n // 8, (n // 2 % 4) * P:(n // 2 % 4 + 1) * P]
                    pe.matmul(out, bb[lo:lo + 64, 0, q, :], ck[lo:lo + 64, 0, q, 0:P], start=True, stop=False)
                    mm = pe.matmul(out, bb[lo:lo + 64, 1, q, :], ck[lo:lo + 64, 1, q, 0:P], start=False, stop=True)
                mm.then_inc(on("kernels_done"), 1)

            turn_wm(0)
            product(S0["u"], 0, 0, 2, KD, h_of, 2, h_tile(2))
            turn_wm(1)
            product(S0["u"], 1, 0, 2, KD, h_of)
            kernels(0)

            def s5_inputs():
                pe.wait_ge(on("u_spread"), 16 * S5_T)
                for ri, src in ((0, wt_r), (1, wt_i)):
                    for g in range(S5_G):
                        q, lo = g // 2, 64 * (g % 2)
                        mm = pe.matmul(ps[lo:lo + 64, 4 + 2 * ri + q // 8, (q % 8) * 64:(q % 8 + 1) * 64],
                                       src[:, q, lo:lo + 64], uc[:, g, :], start=True, stop=True)
                mm.then_inc(on("vin_done"), 1)
                pe.wait_ge(on("vin_out"), 1)

            def s5_outputs():
                pe.wait_ge(on("kernels_spread"), 16 * S5_T)
                pe.wait_ge(on("s5_states"), 1)
                for g in range(S5_G):
                    q, lo = g // 2, 64 * (g % 2)
                    out = ps[:, 4 + 2 * (g % 2) + q // 8, (q % 8) * 64:(q % 8 + 1) * 64]
                    pe.matmul(out, toep[:, g, :], uc[:, g, :], start=True, stop=False)
                    pe.matmul(out, ck[lo:lo + 64, 0, q, 16:144], xc[lo:lo + 64, 0, q, :], start=False, stop=False)
                    mm = pe.matmul(out, ck[lo:lo + 64, 1, q, 16:144], xc[lo:lo + 64, 1, q, :], start=False, stop=True)
                mm.then_inc(on("s5_y"), 1)
                pe.wait_ge(on("s5_out"), 4)

            base = S0["ret"]
            for h in range(RET_H):
                product(base, 0, h, 4, KD, h_of)
                if h == 0:
                    kernels(1)
                if h == 3:
                    pe.wait_ge(on("ret_read"), h + 1)
                    s5_outputs()
                for v in (0, 1):
                    slot = begin(base, 1 + v, h, 4)
                    w = wslot[:, slot, 0:KD * P].rearrange("p (k c) -> p k c", k=KD)
                    for t in range(TT):
                        for k in range(KD):
                            mm = pe.matmul(ps[:, 2 * slot, t * P:(t + 1) * P], h_t[:, k, t * P:(t + 1) * P],
                                           w[:, k, :], start=k == 0, stop=k == KD - 1)
                    mm.then_inc(on("gemm_done"), 1)
                product(base, 3, h, 4, KD, h_of)
                if h == 3:
                    pe.wait_ge(on("gelu_ready"), 4)
                    for u in (0, 1):
                        product(S0["glu"], u, 0, 2, 4, lambda k: y_gl[:, k, :])
                pe.wait_ge(on("ret_read"), h + 1)
                pe.wait_ge(on("kernels_out"), 2)
                if h == 0:
                    s5_inputs()
                pe.wait_ge(on("qk_ready"), h + 1)
                for t in range(TT):
                    tok = slice(t * P, (t + 1) * P)
                    pe.matmul(ps[:, 4, tok], kr[:, tok], qr[:, tok], start=True, stop=True)
                    mm = pe.transpose(ps[:, 5, tok], kr[:, tok], ident)
                mm.then_inc(on("scores_done"), 1)
                pe.wait_ge(on("k_tok_ready"), h + 1)
                pe.wait_ge(on("v_tok_ready"), h + 1)
                for t in range(TT - 1):
                    mm = pe.matmul(ps[:, 6 + t // 2, (t % 2) * DV:(t % 2 + 1) * DV], k_tk[:, t, :], v_tk[:, t, :],
                                   start=True, stop=True)
                mm.then_inc(on("ret_new"), 1)
                pe.wait_ge(on("scores_ready"), h + 1)
                pe.wait_ge(on("ret_state"), h + 1)
                for m in (0, 1):
                    for t in range(TT):
                        out = ps[:, 4 + m, t * P:(t + 1) * P]
                        mm = pe.matmul(out, v_tk[:, t, m * P:(m + 1) * P], sm[:, t, :], start=True, stop=t == 0)
                        if t:
                            mm = pe.matmul(out, s_ret[:, t - 1, m * P:(m + 1) * P], qd[:, t * P:(t + 1) * P],
                                           start=False, stop=True)
                mm.then_inc(on("ret_y"), 1)
                pe.wait_ge(on("ret_sq"), h + 1)
                for m in (0, 1):
                    mm = pe.matmul(bank(6), ones, sq2[:, m, :], start=m == 0, stop=m == 1)
                mm.then_inc(on("ret_sum"), 1)
            project_out(1)
            norm(3)
            mlp(1)
            norm(4)
            for t in range(TT):
                if t == 2:
                    pe.wait_ge(on("norm_root"), 5)
                    for u in range(TT):
                        mm = pe.matmul(ps[:, 6, u:u + 1], rn[0:1, u * P:(u + 1) * P], K("ones")[0:1, 0:1],
                                       start=True, stop=True)
                    mm.then_inc(on("factors_made"), 1)
                if t == 3:
                    pe.wait_ge(on("factors_ready"), 1)
                for k in range(KD):
                    pe.wait_ge(on("gained"), k + 1)
                    mm = pe.transpose(ps[:, row_banks[t] + k // 4, (k % 4) * P:(k % 4 + 1) * P],
                                      y_t[:, k, t * P:(t + 1) * P], ident)
                mm.then_inc(on("rows_turned"), 1)

        @block.vector
        def _(dve):
            own = Own(dve, on("dve_own"))
            do, go = own.do, own.go
            TTo, TS, STT = dve.tensor_tensor, dve.tensor_scalar, dve.scalar_tensor_tensor

            def norm(n, gain):
                dve.wait_ge(on("norm_root"), n + 1)
                for k in range(KD):
                    do(STT(h_t[:, k, :], x_t[:, k, :], C(gain, k), rn[:], ALU.mult, ALU.mult))
                    dve.sem_inc(on("h_ready"), 1)

            def norm_split(n, gain):
                dve.wait_ge(on("norm_root"), n + 1)
                for k in range(KD + 1):
                    if k < KD:
                        do(STT(h_t[:, k, :], x_t[:, k, :], C(gain, k), rn[:], ALU.mult, ALU.mult))
                        dve.sem_inc(on("h_whole"), 1)
                    if k:
                        dve.wait_ge(on("h_high"), KD * (n // 2) + k)
                        do(TTo(h_s[:, 1, k - 1, :], h_t[:, k - 1, :], h_s[:, 0, k - 1, :].bitcast(F32), ALU.subtract))
                        dve.sem_inc(on("h_ready"), 1)

            def add_part(base, u, i=0):
                dve.wait_ge(on("gemm_done"), base + u + 4 * i + 1)
                xj = x_t[:, bass.ds(4 * i + u, 1), :].rearrange("p a b -> p (a b)")
                do(TTo(xj, xj, bank(mlp_bank(base, u)), ALU.add))
                dve.sem_inc(psum_free[(base + u) % 2], 1)

            def add_parts(phase, last):
                with own.loop(KD // 4, 4) as i:
                    for u in range(4):
                        add_part(S0[phase], u, i)
                        if last:
                            dve.sem_inc(on("x_ready"), 1)

            def project_out(layer):
                for k in range(KO):
                    dve.wait_ge(on("y_high"), KO * layer + k + 1)
                    do(TTo(hid_s[:, 1, k, :], y_t[:, k, :], hid_s[:, 0, k, :].bitcast(F32), ALU.subtract))
                    dve.sem_inc(on("y_split"), 1)
                add_parts(f"out{layer}", True)

            def up(layer, part):
                base, first = S0[f"up{layer}{'ab'[part]}"], KH[0] * part
                with own.loop(KH[part] // 2, 14) as i:
                    for v in (0, 1):
                        pair = layer * KF + first + v + 2 * i
                        dve.wait_ge(on("mlp_affine"), pair + 1)
                        for tap in (1, 0):
                            sh = 2 - tap
                            for half in (0, 1):
                                dst = cg[:, v, half, sh:T]
                                j = first + v + 2 * i + KF * half + tap * 2 * KF
                                go(STT(dst, bank(mlp_bank(base, 2 * v + half))[:, 0:T - sh], Cd(f"fcw{layer}", j), dst,
                                       ALU.mult, ALU.add))
                            own.wait()
                        dve.sem_inc(psum_free[0], 1)
                        dve.sem_inc(psum_free[1], 1)
                        dve.sem_inc(on("mlp_conv"), 1)
                        dve.wait_ge(on("mlp_gate"), pair + 1)
                        if part:
                            dve.wait_ge(on("gemm_done"), S0[f"up{layer}b"])
                        tile = lambda n: hid_s[:, n, bass.ds(v + 2 * i, 1), :].rearrange("p a b -> p (a b)")
                        go(TTo(tile(0), cg[:, v, 0, :], cg[:, v, 1, :], ALU.mult))
                        own.wait()
                        do(TTo(cg[:, v, 0, :], cg[:, v, 0, :], cg[:, v, 1, :], ALU.mult))
                        do(TTo(tile(1), cg[:, v, 0, :], tile(0).bitcast(F32), ALU.subtract))
                        dve.sem_inc(on("cg_read"), 1)
                        dve.sem_inc(on("hid_ready"), 1)

            for name, free in (("pads_read", 1), ("gn_read", 1), ("cg_read", 2), ("ret_read", 1)):
                dve.sem_inc(on(name), free)
            for k in range(KD):
                dve.wait_ge(on("x_turned"), KD * (TT - 1) + k + 1)
                do(dve.tensor_copy(x_t[:, k, :], bank(k)))
                dve.sem_inc(on("x_ready"), 1)
            dve.wait_ge(on("cols_in"), 16)
            norm(0, "mix_g0")

            def mix(dst, j, mu):
                do(TTo(dst, pad[:, j, 0:T], pad[:, j, 1:T + 1], ALU.subtract))
                do(STT(dst, dst, mu, pad[:, j, 1:T + 1], ALU.mult, ALU.add))

            dve.wait_ge(on("lora_pad"), 1)
            mix(kq, 0, C("mu", 12))
            mix(kk, 1, C("mu", 13))
            dve.sem_inc(on("lora_mixed"), 1)
            grp = lambda n, g: split(dts[:, n, g * 32:(g + 1) * 32], TT)
            dve.wait_ge(on("dt_sum"), 1)
            for g in range(SSD_G):
                do(TTo(grp(0, g), split(ps[:, 6, 0:64], TT)[:, :, 8 * g:8 * g + 8],
                       split(C("dt_bias", g * 32, 32), TT), ALU.add))
            do(STT(dts[:, 1, :], dts[:, 0, :], -1.0, dts[:, 0, :], ALU.mult, ALU.max))
            dve.sem_inc(on("dt_abs"), 1)
            dve.wait_ge(on("dt_exp"), 1)
            do(TS(dts[:, 4, :], dts[:, 1, :], 1.0, None, ALU.add))
            do(STT(dts[:, 1, :], dts[:, 4, :], -1.0, dts[:, 1, :], ALU.add, ALU.subtract))
            do(dve.reciprocal(dts[:, 4, :], dts[:, 4, :]))
            do(TTo(dts[:, 1, :], dts[:, 1, :], dts[:, 4, :], ALU.mult))
            do(TTo(dts[:, 2, :], dts[:, 2, :], dts[:, 1, :], ALU.subtract))
            do(STT(dts[:, 0, :], dts[:, 0, :], 0.0, dts[:, 2, :], ALU.max, ALU.add))
            do(STT(dts[:, 5, :], dts[:, 0, :], -1.0, dts[:, 3, :], ALU.mult, ALU.mult))
            dve.sem_inc(on("dt_rates"), 1)
            for j in range(4):
                dve.wait_ge(on("lora_g"), j + 1)
                do(dve.tensor_copy(gate[:, j, :], bank(2 + j % 2)))
                dve.sem_inc(on("lora_g_out"), 1)
            dve.wait_ge(on("acc_sum"), 1)
            do(dve.tensor_copy(dts[:, 6, :], ps[:, 6, 0:64]))
            dve.sem_inc(on("acc_ready"), 1)
            dve.wait_ge(on("acc_turn"), 1)
            do(dve.tensor_copy(acc_t[:, :], ps[0:64, 6, 0:P]))
            dve.sem_inc(on("acc_turned"), 1)
            dve.wait_ge(on("lora_w_out"), 4)
            dve.wait_ge(on("consts0_in"), 16)

            def row(v, r):
                return v[:, bass.ds(r, 1), :].rearrange("p a b -> p (a b)")

            chunks = lambda v: split(v, NC)
            with own.loop(4, 84) as r:
                dve.wait_ge(on("rk_pad"), r + 1)
                mix(kq, 1, Cd("mu", r + 4))
                do(TS(kk, kq, Cd("k_k", r), None, ALU.mult))
                do(TTo(tmp, kk, kk, ALU.mult))
                dve.sem_inc(on("kk_sq"), 1)
                mix(rr, 0, Cd("mu", r))
                do(dve.tensor_tensor_scan(zz, K("reset"), row(sw, r), 0.0, ALU.mult, ALU.add))
                dve.sem_inc(on("log_decay"), 1)
                do(TS(bh, row(ai, r), -1.0, Cd("k_a", r), ALU.add, ALU.mult))
                do(STT(kh, bh, 1.0, kq, ALU.add, ALU.mult))
                dve.wait_ge(on("kk_sum"), r + 1)
                do(TS(rn[:], bank(4), float(N_RWKV), 1e-24, ALU.mult, ALU.max))
                dve.sem_inc(on("kk_var"), 1)
                do(STT(bonus, rr, Cd("r_k", r), kh, ALU.mult, ALU.mult))
                dve.wait_ge(on("decays"), r + 1)
                do(TTo(rd, rr, pp, ALU.mult))
                do(TTo(kh, kh, ip, ALU.mult))
                dve.wait_ge(on("kk_root"), r + 1)
                do(TTo(kk, kk, rn[:], ALU.mult))
                do(TTo(bh, kk, row(ai, r), ALU.mult))
                do(TTo(bh, bh, ip, ALU.mult))
                go(TTo(chunks(zz)[:, :, 1:CH], chunks(kk)[:, :, 1:CH], chunks(pp)[:, :, 0:CH - 1], ALU.mult))
                go(dve.tensor_copy(chunks(zz)[:, :, 0:1], chunks(kk)[:, :, 0:1]))
                own.wait()
                dve.sem_inc(on("keys"), 1)
                dve.wait_ge(on("v_pad"), r + 1)
                mix(vv, 2, Cd("mu", r + 8))
                dve.sem_inc(on("pads_read"), 1)
                end = chunks(pp)[:, :, CH - 1:CH].broadcast_to([P, NC, CH])
                go(TTo(chunks(bt), chunks(bh), end, ALU.mult))
                go(TTo(chunks(kt), chunks(kh), end, ALU.mult))
                go(TTo(gt, each(K("ident2"), NC), end, ALU.mult))
                own.wait()
                dve.sem_inc(on("tails"), 1)
                for hd in (0, 1):
                    dve.wait_ge(on("grams"), 2 * r + hd + 1)
                    for b, (dst, mask) in enumerate(((at_, "strict"), (bt_, "strict"), (qb_, "incl"), (qk_, "incl"))):
                        go(TTo(dst[:, 4 * hd:4 * hd + 4, :], split(bank(4 * hd + b), 4), each(K(mask), 4), ALU.mult))
                    own.wait()
                    dve.sem_inc(on("grams_out"), 1)

                def level_part(level, hd):
                    mask, m = K("level")[:, level * P:(level + 1) * P], slice(4 * hd, 4 * hd + 4)
                    go(TTo(al_[:, m, :], at_[:, m, :], each(mask, 4), ALU.mult))

                for hd in (0, 1):
                    m = slice(4 * hd, 4 * hd + 4)
                    level_part(0, hd)
                    own.wait()
                    do(TTo(tu[:, m, :], each(K("ident"), 4), al_[:, m, :], ALU.subtract))
                    dve.sem_inc(on("al_ready"), 1)
                for hd in (0, 1):
                    dve.wait_ge(on("x_done"), 12 * r + hd + 1)
                    go(TTo(tl[:, 4 * hd:4 * hd + 4, :], each(K("ident"), 4), split(bank(4 + hd), 4), ALU.subtract))
                    level_part(1, hd)
                    own.wait()
                    dve.sem_inc(on("al_ready"), 1)
                for level in range(1, 6):
                    if level < 5:
                        for hd in (0, 1):
                            dve.wait_ge(on("x_done"), 12 * r + 2 * level + hd + 1)
                            level_part(level + 1, hd)
                    for hd in (0, 1):
                        m = slice(4 * hd, 4 * hd + 4)
                        dve.wait_ge(on("tx_done"), 10 * r + 2 * (level - 1) + hd + 1)
                        if level < 5:
                            do(TTo(tl[:, m, :], tl[:, m, :], split(bank(6 + hd), 4), ALU.subtract))
                            dve.sem_inc(on("al_ready"), 1)
                        do(TTo(tu[:, m, :], tu[:, m, :], split(bank(4 + hd), 4), ALU.subtract))
                        dve.sem_inc(on("t_ready" if level < 5 else "tu_ready"), 1)
                dve.wait_ge(on("chunk_maps"), r + 1)
                go(TTo(rd, rd, bank(4), ALU.add))
                half = lambda v, q: v.rearrange("p (t q) c -> p t q c", q=2)[:, :, q, :]
                for q in (0, 1):
                    go(TTo(half(gt, q), half(gt, q), half(chunks(bank(5 + q)), q), ALU.add))
                    go(dve.tensor_copy(half(hh_, q), half(chunks(bank(7 * q)), q)))
                own.wait()
                do(dve.tensor_copy(st[:, 1, :], hh_[:, 0, :]))
                dve.sem_inc(on("state_ready"), 1)
                for c in range(1, NC - 1):
                    dve.wait_ge(on("state_moved"), (NC - 2) * r + c)
                    do(TTo(st[:, c + 1, :], hh_[:, c, :], ps[:, 1, c * 64:(c + 1) * 64], ALU.add))
                    dve.sem_inc(on("state_ready"), 1)
                dve.wait_ge(on("bonus_sum"), r + 1)
                do(STT(bonus, bank(3), float(N_RWKV), vv, ALU.mult, ALU.mult))
                dve.wait_ge(on("rwkv_y"), r + 1)
                do(dve.tensor_copy(kk, bank(2)))
                dve.sem_inc(on("gn_in"), 1)
                dve.wait_ge(on("gn_mean"), r + 1)
                do(TTo(kk, kk, bank(6), ALU.subtract))
                dve.sem_inc(on("gn_dev"), 1)
                dve.wait_ge(on("gn_root"), r + 1)
                do(TTo(kk, kk, rn[:], ALU.mult))
                do(TS(kk, kk, Cd("ln_g", r), Cd("ln_b", r), ALU.mult, ALU.add))
                do(TTo(kk, kk, bonus, ALU.add))
                do(TTo(row(y_t, r), kk, row(gate, r), ALU.mult))
                dve.sem_inc(on("rwkv_head"), 1)

            base = S0["ssd"]

            def dt_of(n, g, t=None):
                o = 32 * g + (0 if t is None else 8 * t)
                return dts[:, n, o:o + (32 if t is None else 8)]

            ssd_tiles = [[(bc_f[:, 0, :], 0)], [(bc_f[:, 1, :], 1)], [(xs[:, 0, :], 2), (xs[:, 1, :], 3)],
                         [(xs[:, 2, :], 4), (xs[:, 3, :], 5)]]

            def conv(n):
                dve.wait_ge(on("ssd_affine"), n + 1)
                slot, _ = slot_of(base, n)
                for tap in (2, 1, 0):
                    sh = 3 - tap
                    for m, (dst, j) in enumerate(ssd_tiles[n % 4]):
                        go(STT(dst[:, sh:T], bank(2 * slot + m)[:, 0:T - sh], C("cw", 12 * tap + 6 * (n // 4) + j),
                               dst[:, sh:T], ALU.mult, ALU.add))
                    own.wait()
                dve.sem_inc(psum_free[slot], 1)
                dve.sem_inc(on("ssd_conv"), 1)

            heads = lambda v: split(v, SSD_J)
            conv(0)
            conv(1)
            for g in range(SSD_G):
                conv(4 * g + 2)
                dve.wait_ge(on("acc_spread"), 16 * (g + 1))
                go(TTo(dte, acb[:, :, P - 1:P].rearrange("p a b -> p (a b)"), dt_of(6, g), ALU.subtract))
                go(TTo(seg, acb, over(dt_of(6, g), P), ALU.subtract))
                own.wait()
                do(TS(seg, seg, 0.0, None, ALU.min))
                dve.sem_inc(on("ssd_logs"), 1)
                dve.wait_ge(on("cb_done"), g + 1)
                go(TTo(cbm, split(bank(4), TT), each(K("triu"), TT), ALU.mult))
                go(dve.tensor_copy(b_tk, split(bank(5), TT)))
                own.wait()
                dve.sem_inc(on("cb_out"), 1)
                conv(4 * g + 3)
                dve.wait_ge(on("ssd_ends"), g + 1)
                dve.wait_ge(on("xs_turned"), g + 1)
                for t in range(TT):
                    go(TTo(heads(xdt[:, t, :]), heads(bank(4 + t)), over(dt_of(0, g, t), 64), ALU.mult))
                own.wait()
                for t in range(TT - 1):
                    go(TTo(heads(xdd[:, t, :]), heads(xdt[:, t, :]), over(dte[:, 8 * t:8 * t + 8], 64), ALU.mult))
                own.wait()
                dve.sem_inc(on("xd_ready"), 1)
                dve.wait_ge(on("ssd_exps"), g + 1)
                do(dve.tensor_copy(cdk, acb[:, :, P - 1:P].rearrange("p a b -> p (a b)")))
                for t in range(TT):
                    go(TTo(seg[:, 8 * t:8 * t + 8, :], seg[:, 8 * t:8 * t + 8, :], each(cbm[:, t, :], 8), ALU.mult))
                    go(TTo(acb[:, 8 * t:8 * t + 8, :], acb[:, 8 * t:8 * t + 8, :],
                           each(bc_f[:, 1, t * P:(t + 1) * P], 8), ALU.mult))
                own.wait()
                dve.sem_inc(on("ssd_masks"), 1)
                if g == 0:
                    conv(4)
                dve.wait_ge(on("ssd_new"), g + 1)
                do(dve.tensor_copy(s_ssd[:, 0, :], bank(4)))
                for t in (1, 2):
                    do(TTo(heads(s_ssd[:, t, :]), heads(s_ssd[:, t - 1, :]), over(cdk[:, 8 * t:8 * t + 8], 64),
                           ALU.mult))
                    do(TTo(s_ssd[:, t, :], s_ssd[:, t, :], bank(4 + t), ALU.add))
                dve.sem_inc(on("ssd_state"), 1)
                if g == 0:
                    conv(5)
                dve.wait_ge(on("ssd_y"), g + 1)
                y_tile = lambda i: y_t[:, 4 + 4 * g + i, :]
                for i in range(4):
                    do(STT(yg[:, i, :], xs[:, i, :], C("ssd_d", 4 * g + i), bank(4 + i), ALU.mult, ALU.add))
                    do(TTo(yg[:, i, :], yg[:, i, :], y_tile(i), ALU.mult))
                    dve.sem_inc(on("yg_ready"), 1)
                dve.wait_ge(on("ssd_root"), g + 1)
                for i in range(4):
                    go(STT(y_tile(i), yg[:, i, :], C("ssd_g", 4 * g + i), rn[:], ALU.mult, ALU.mult))
                own.wait()
                dve.sem_inc(on("ssd_group"), 1)

            project_out(0)
            norm_split(1, "ffn_g0")
            up(0, 0)
            dve.wait_ge(on("s5_dt"), 1)
            L = lambda n: lam[:, n, :]
            mul = lambda o, p, q: do(TTo(o, p, q, ALU.mult))
            mul(L(1), C1("lam_re"), L(0))
            mul(L(2), C1("lam_im"), L(0))
            do(TS(L(5), L(2), INV_2PI, MAGIC, ALU.mult, ALU.add))
            do(TS(L(5), L(5), -MAGIC, None, ALU.add))
            for part in (PI_A, PI_B, PI_C):
                do(STT(L(2), L(5), -part, L(2), ALU.mult, ALU.add))
            do(TS(L(2), L(2), PI_MAX, -PI_MAX, ALU.min, ALU.max))
            dve.sem_inc(on("s5_angle"), 1)
            dve.wait_ge(on("s5_trig"), 1)
            mul(L(4), L(4), L(4))
            do(TS(L(4), L(4), -2.0, 1.0, ALU.mult, ALU.add))
            mul(L(6), L(1), L(4))
            mul(L(7), L(1), L(3))
            do(TS(L(8), L(6), -1.0, None, ALU.add))
            mul(L(9), C1("lam_re"), C1("lam_re"))
            mul(L(10), C1("lam_im"), C1("lam_im"))
            do(TTo(L(9), L(9), L(10), ALU.add))
            do(dve.reciprocal(L(9), L(9)))
            mul(L(10), L(8), C1("lam_re"))
            mul(L(11), L(7), C1("lam_im"))
            do(TTo(L(10), L(10), L(11), ALU.add))
            mul(L(10), L(10), L(9))
            mul(L(11), L(7), C1("lam_re"))
            mul(L(12), L(8), C1("lam_im"))
            do(TTo(L(11), L(11), L(12), ALU.subtract))
            mul(L(11), L(11), L(9))

            t_a = s5_tmp

            def cmul(o_re, o_im, p_re, p_im, q_re, q_im, t):
                mul(o_re, p_re, q_re)
                mul(t, p_im, q_im)
                do(TTo(o_re, o_re, t, ALU.subtract))
                mul(o_im, p_re, q_im)
                mul(t, p_im, q_re)
                do(TTo(o_im, o_im, t, ALU.add))

            ch16 = lambda v: split(v, S5_PAIR)
            cmul(bb[:, 0], bb[:, 1], over(L(10), 16), over(L(11), 16), ch16(C1("b_re")), ch16(C1("b_im")),
                 ch16(t_a[:, 0:256]))
            do(dve.memset(pw[:, 0, :, 0:1], 1.0))
            do(dve.memset(pw[:, 1, :, 0:1], 0.0))
            col = lambda ri, n: pw[:, ri, :, n:n + 1].rearrange("p a b -> p (a b)")
            for n in range(1, 9):
                cmul(col(0, n), col(1, n), col(0, n - 1), col(1, n - 1), L(6), L(7), L(13))
            for s in range(S5_T):
                go(dve.tensor_copy(pwr[:, :, :, s:s + 1], pw[:, :, :, 7 - s:8 - s]))
            own.wait()
            for ri in (0, 1):
                do(dve.tensor_copy(lam[:, 14 + ri, :], col(0, 8)))
            do(TS(L(16), col(1, 8), -1.0, None, ALU.mult))
            do(dve.tensor_copy(L(17), col(1, 8)))
            do(TS(C1("c_im"), C1("c_im"), -1.0, None, ALU.mult))

            def by(v, n):
                return v.unsqueeze(3).broadcast_to([P, v.shape[1], v.shape[2], n])

            def times(v, n):
                return v.unsqueeze(2).broadcast_to([P, v.shape[1], n, v.shape[2]])

            def matrices(u):
                q, n = slice(4 * (u % 4), 4 * (u % 4) + 4), 8 if u < 4 else 9
                part = lambda v: v[:, q, :].rearrange("p q (a b) -> p q a b", a=n)
                t = s5_tmp[:, 0:4 * n * 16].rearrange("p (q a b) -> p q a b", q=4, a=n)
                if u < 4:
                    o_re, o_im, last = part(wm), part(wm2), ALU.add
                    p_re, p_im = by(pwr[:, 0, q, :], 16), by(pwr[:, 1, q, :], 16)
                    q_re, q_im = times(bb[:, 0, q, :], n), times(bb[:, 1, q, :], n)
                else:
                    o_re, o_im, last = part(ck[:, 0]), part(ck[:, 1]), ALU.subtract
                    p_re, p_im = by(pw[:, 0, q, :], 16), by(pw[:, 1, q, :], 16)
                    q_re, q_im = times(ch16(C1("c_re"))[:, q, :], n), times(ch16(C1("c_im"))[:, q, :], n)
                go(TTo(o_re, p_re, q_re, ALU.mult))
                go(TTo(t, p_im, q_im, ALU.mult))
                own.wait()
                go(TTo(o_re, o_re, t, ALU.subtract if u < 4 else ALU.add))
                go(TTo(o_im, p_re, q_im, ALU.mult))
                own.wait()
                do(TTo(t, p_im, q_re, ALU.mult))
                do(TTo(o_im, o_im, t, last))

            for u in range(KD):
                add_part(S0["down0a"], u)
                matrices(u)
                if u % 4 == 3:
                    dve.sem_inc(on("wm_ready" if u == 3 else "ck_ready"), 1)
            up(0, 1)
            add_parts("down0b", True)
            norm(2, "mix_g1")

            base = S0["u"]
            for u in (0, 1):
                slot, _ = slot_of(base, u)
                dve.wait_ge(on("gemm_done"), base + u + 1)
                for m in (0, 1):
                    do(dve.tensor_copy(split(u_p[:, 2 * u + m, :], S5_T),
                                       bank(2 * slot + m).rearrange("p (c s) -> p s c", s=S5_T)))
                    dve.sem_inc(on("u_ready"), 1)
                dve.sem_inc(psum_free[slot], 1)

            dve.wait_ge(on("consts1_in"), 16)
            base = S0["ret"]
            def s5_finish():
                dve.wait_ge(on("s5_back"), 64)
                for i in range(4):
                    do(STT(y_in[:, i, :], u_p[:, i, :], C("s5_d", i), y_in[:, i, :], ALU.mult, ALU.add))
                    dve.sem_inc(on("s5_skip"), 1)
                for u in (0, 1):
                    dve.wait_ge(on("glu_gate"), u + 1)
                    for m in (0, 1):
                        do(TTo(y_t[:, 2 * u + m, :], y_gl[:, 2 * u + m, :], y_gate[:, 2 * u + m, :], ALU.mult))
                        dve.sem_inc(on("glu_out"), 1)

            def head(h, last):
                dve.wait_ge(on("gemm_done"), base + 4 * h + 1)
                slot, _ = slot_of(base, 0)
                for m, (dst, cos, sin) in enumerate(((qr, "cosq", "sinq"), (kr, "cosk", "sink"))):
                    src = bank(2 * slot + m)
                    go(TTo(rm[0:64], src[64:128], K1(sin)[0:64], ALU.mult))
                    go(TTo(rm[64:128], src[0:64], K1(sin)[64:128], ALU.mult))
                    go(TTo(dst, src, K1(cos), ALU.mult))
                    own.wait()
                    do(TTo(dst, dst, rm, ALU.add))
                dve.sem_inc(psum_free[slot], 1)
                dve.sem_inc(on("qk_ready"), 1)
                do(TTo(split(qd, TT), split(qr, TT), each(K1d("qdec", P * h, P), TT), ALU.mult))
                if last:
                    s5_finish()
                dve.wait_ge(on("scores_done"), h + 1)
                do(TTo(sm, split(bank(4), TT), each(K1d("decay", P * h, P), TT), ALU.mult))
                dve.sem_inc(on("scores_ready"), 1)
                dve.wait_ge(on("ret_new"), h + 1)
                do(dve.tensor_copy(s_ret[:, 0:2, :], split(bank(6), 2)))
                do(STT(s_ret[:, 1, :], s_ret[:, 0, :], K1d("gchunk", h, 1), s_ret[:, 1, :], ALU.mult, ALU.add))
                do(STT(s_ret[:, 2, :], s_ret[:, 1, :], K1d("gchunk", h, 1), ps[:, 7, 0:DV], ALU.mult, ALU.add))
                dve.sem_inc(on("ret_state"), 1)
                dve.wait_ge(on("ret_root"), h + 1)
                dve.wait_ge(on("gs_ready"), h + 1)
                for m in (0, 1):
                    do(TTo(gs[:, m, :], gs[:, m, :], rn[:], ALU.mult))
                    do(TTo(y_t[:, bass.ds(4 + 2 * h + m, 1), :].rearrange("p a b -> p (a b)"), gs[:, m, :],
                           bank(4 + m), ALU.mult))
                dve.sem_inc(on("ret_read"), 1)
                dve.sem_inc(on("ret_head"), 1)

            with own.loop(RET_H - 1, 17) as h:
                head(h, False)
            head(RET_H - 1, True)

            project_out(1)
            norm_split(3, "ffn_g1")
            up(1, 0)
            add_parts("down1a", False)
            up(1, 1)
            add_parts("down1b", True)
            for k in range(KD):
                do(TS(y_t[:, k, :], x_t[:, k, :], C("final_g", k), None, ALU.mult))
                dve.sem_inc(on("gained"), 1)
            dve.wait_ge(on("factors_made"), 1)
            do(dve.tensor_copy(factors[:], ps[:, 6, 0:TT]))
            dve.sem_inc(on("factors_ready"), 1)
            for t in range(TT):
                dve.wait_ge(on("rows_turned"), t + 1)
                do(TS(x_t[:, 2 * t, :], bank(row_banks[t]), factors[:, t:t + 1], None, ALU.mult))
                dve.sem_inc(on("rows_dve"), 1)


def tiles_of(w, order):
    k, n = w.shape
    t = w.reshape(k // P, P, n // P, P).transpose(2, 1, 0, 3)
    width = max(len(o) for o in order) * (k // P) * P
    out = np.zeros((len(order), P, width), w.dtype)
    for s, o in enumerate(order):
        part = t[list(o)].transpose(1, 0, 2, 3).reshape(P, -1)
        out[s, :, :part.shape[1]] = part
    return out


def feature_cols(v):
    return v.reshape(-1, P).T


def per_pair(v):
    v = v.reshape(S5_PAIR, 2, S5_N, -1).transpose(1, 2, 0, 3)
    return v.reshape(P, -1)


def kernel(**inputs):
    import concourse.bacc as bacc
    from concourse.bass_utils import run_bass_kernel_spmd

    v = {k: np.asarray(x) for k, x in inputs.items()}
    w_in = v["l0_w_in"]
    con_, con0, con1_ = constants()
    order12 = [8, 10, 0, 1, 2, 3, 9, 11, 4, 5, 6, 7]
    per_head = lambda x: np.tile(x.reshape(SSD_G, 1, SSD_J), (P, 1, TT, 1)).reshape(P, 64)
    c0 = {
        "mix_g0": feature_cols(v["l0_norm_mix"]), "mu": feature_cols(v["l0_rwkv_mu"]),
        "w0": feature_cols(v["l0_rwkv_w0"]), "a0": feature_cols(v["l0_rwkv_a0"]),
        "k_k": feature_cols(v["l0_rwkv_k_k"]), "k_a": feature_cols(v["l0_rwkv_k_a"]),
        "r_k": feature_cols(v["l0_rwkv_r_k"].reshape(-1)), "ln_g": feature_cols(v["l0_rwkv_ln_g"]),
        "ln_b": feature_cols(v["l0_rwkv_ln_b"]),
        "cw": np.concatenate([feature_cols(w)[:, order12] for w in v["l0_ssd_conv_w"]], axis=1),
        "cb": feature_cols(v["l0_ssd_conv_b"])[:, order12],
        "dt_bias": per_head(v["l0_ssd_dt_bias"]), "a_log": per_head(v["l0_ssd_a_log"]),
        "w_dt": w_in[:, 4352:4368].reshape(KD, P, 16).transpose(1, 0, 2).reshape(P, -1),
        "ssd_d": feature_cols(np.repeat(v["l0_ssd_d"], SSD_P)), "ssd_g": feature_cols(v["l0_ssd_norm_g"]),
        "ffn_g0": feature_cols(v["l0_norm_ffn"]),
        "fcw0": np.concatenate([feature_cols(w) for w in v["l0_ffn_conv_w"]], axis=1),
        "fcb0": feature_cols(v["l0_ffn_conv_b"]), "mix_g1": feature_cols(v["l1_norm_mix"]),
        "s5_d": feature_cols(v["l1_s5_d"]), "b_glu": feature_cols(v["l1_s5_b_glu"]),
        "ffn_g1": feature_cols(v["l1_norm_ffn"]),
        "fcw1": np.concatenate([feature_cols(w) for w in v["l1_ffn_conv_w"]], axis=1),
        "fcb1": feature_cols(v["l1_ffn_conv_b"]), "final_g": feature_cols(v["final_norm"]),
    }
    c1 = {
        "lam_re": per_pair(v["l1_s5_lam_re"]), "lam_im": per_pair(v["l1_s5_lam_im"]),
        "log_dt": per_pair(np.repeat(v["l1_s5_log_dt"][:, None], S5_N, axis=1)),
        "b_re": per_pair(v["l1_s5_b_re"]), "b_im": per_pair(v["l1_s5_b_im"]),
        "c_re": per_pair(v["l1_s5_c_re"].transpose(0, 2, 1)), "c_im": per_pair(v["l1_s5_c_im"].transpose(0, 2, 1)),
    }
    ssd = []
    for g in range(SSD_G):
        o = order12[6 * g:6 * g + 6]
        ssd += [[22 + o[0]], [22 + o[1]], [22 + o[2], 22 + o[3]], [22 + o[4], 22 + o[5]]]
    ret = []
    for h in range(RET_H):
        ret += [[4 + h, 8 + h], [12 + 2 * h], [13 + 2 * h], [20 + 2 * h, 21 + 2 * h]]
    main = w_in[:, :4352]
    alone = [[j] for j in range(KD)]
    gates = [[j + KF * half] for j in range(KF) for half in (0, 1)]
    at = KH[0] * P
    arrays = {
        "x": v["x"], "con": con_, "con0": con0, "con1": con1_,
        "col0": np.concatenate([c0[n] for n, _ in COLS0], axis=1),
        "col1": np.concatenate([c1[n] for n, _ in COLS1], axis=1),
        "w2": v["l0_rwkv_w2"].reshape(64, 4, P), "a2": v["l0_rwkv_a2"].reshape(64, 4, P),
        "g2": v["l0_rwkv_g2"].reshape(P, 4, P),
        "w_lora": tiles_of(main, [[12, 13]]),
        "w_rwkv": tiles_of(main, [o for r in range(4) for o in ([r, 4 + r], [8 + r], [14 + 2 * r], [15 + 2 * r])]),
        "w_ssd": tiles_of(main, ssd),
        "w_out0": tiles_of(v["l0_w_out"], alone), "w_up0": tiles_of(v["l0_ffn_up"], gates),
        "w_down0a": tiles_of(v["l0_ffn_down"][:at], alone), "w_down0b": tiles_of(v["l0_ffn_down"][at:], alone),
        "w_u": tiles_of(v["l1_w_in"], [[0, 1], [2, 3]]), "w_ret": tiles_of(v["l1_w_in"], ret),
        "w_glu": tiles_of(v["l1_s5_w_glu"], [[0, 1], [2, 3]]),
        "w_out1": tiles_of(v["l1_w_out"], alone), "w_up1": tiles_of(v["l1_ffn_up"], gates),
        "w_down1a": tiles_of(v["l1_ffn_down"][:at], alone), "w_down1b": tiles_of(v["l1_ffn_down"][at:], alone),
    }
    arrays = {f"in_{k}": np.ascontiguousarray(x) for k, x in arrays.items()}
    nc = bacc.Bacc("TRN2", target_bir_lowering=False, num_devices=1)
    a = {k[3:]: nc.dram_tensor(k, x.shape, F32, kind="ExternalInput").ap() for k, x in arrays.items()}
    a["out"] = nc.dram_tensor("out_0", (1, T, D), F32, kind="ExternalOutput").ap()
    trunk(nc, a)
    r = run_bass_kernel_spmd(nc, [arrays], core_ids=[0])
    return r.results[0]["out_0"]
```
